# Optimizing a Trainium2 kernel written in Bass

```python
import jax, jax.numpy as jnp
from jax import lax
import numpy as np
import math

D_MODEL = 1024
BATCH = 1
SEQ = 512
DEPTH = 1

CHUNK = 64
CONV_CH = D_MODEL
CONV_WIDTH = 31
SG_WIDTH = D_MODEL
SG_HEADS = 8
SG_HEAD_DIM = SG_WIDTH // SG_HEADS
SG_BLOCK = 128
N_GROUPS = 4
EXPERTS_PER_GROUP = 8
N_EXPERTS = N_GROUPS * EXPERTS_PER_GROUP
TOP_K = 2
D_EXPERT = D_MODEL // 2
EXPERT_BLOCK = 256
IN_COLS = 2 * CONV_CH + 2 * SG_WIDTH + 2 * D_MODEL
EPS = 1e-6


def rms_norm(x, g):
    xf = x.astype(jnp.float32)
    y = xf * lax.rsqrt(jnp.mean(xf * xf, axis=-1, keepdims=True) + EPS)
    return (y * g.astype(jnp.float32)).astype(x.dtype)

def layer_norm(x, g, b):
    xf = x.astype(jnp.float32)
    mu = jnp.mean(xf, axis=-1, keepdims=True)
    var = jnp.mean(jnp.square(xf - mu), axis=-1, keepdims=True)
    y = (xf - mu) * lax.rsqrt(var + EPS)
    return (y * g.astype(jnp.float32) + b.astype(jnp.float32)).astype(x.dtype)

def conformer_conv_branch(a, conv_w, conv_b, ln_g, ln_b, w_o, b_o):
    a1, a2 = jnp.split(a, 2, axis=-1)
    a = a1 * jax.nn.sigmoid(a2)
    kern = conv_w[:, None, :]
    y = lax.conv_general_dilated(
        a, kern, window_strides=(1,), padding=[(CONV_WIDTH - 1, 0)],
        dimension_numbers=("NWC", "WIO", "NWC"), feature_group_count=CONV_CH) + conv_b
    y = jax.nn.silu(layer_norm(y, ln_g, ln_b))
    return y @ w_o + b_o

def spatial_gating_branch(z, ln_g, ln_b, w_s, b_s, w_o, b_o):
    z = jax.nn.gelu(z, approximate=False)
    u, v = jnp.split(z, 2, axis=-1)
    v = layer_norm(v, ln_g, ln_b)
    bsz, seq, _ = v.shape
    n_blk = seq // SG_BLOCK
    v = v.reshape(bsz, n_blk, SG_BLOCK, SG_HEADS, SG_HEAD_DIM)
    blk = np.arange(SG_BLOCK) // CHUNK
    mask = jnp.asarray(blk[:, None] >= blk[None, :])
    w = w_s * mask[None].astype(w_s.dtype)
    sv = jnp.einsum("hqk,bnkhc->bnqhc", w, v) + b_s.T[:, :, None]
    s = u * sv.reshape(bsz, seq, SG_WIDTH)
    return s @ w_o + b_o

def hierarchical_moe(h, w_rg, b_rg, w_re, b_re, w_gate, w_up, w_down):
    bsz, seq, d = h.shape
    n_tok = bsz * seq
    xt = h.reshape(n_tok, d)
    g_logits = (xt @ w_rg + b_rg).astype(jnp.float32)
    g_prob = jax.nn.softmax(g_logits, axis=-1)
    g_sel = jnp.argmax(g_logits, axis=-1)
    g_w = jnp.take_along_axis(g_prob, g_sel[:, None], axis=-1)
    e_logits = (xt @ w_re + b_re).astype(jnp.float32).reshape(n_tok, N_GROUPS, EXPERTS_PER_GROUP)
    e_logits = jnp.take_along_axis(e_logits, g_sel[:, None, None], axis=1)[:, 0]
    top_v, top_i = lax.top_k(e_logits, TOP_K)
    e_w = jax.nn.softmax(top_v, axis=-1) * g_w
    expert_id = g_sel[:, None] * EXPERTS_PER_GROUP + top_i
    n_assign = n_tok * TOP_K
    flat_e = expert_id.reshape(-1)
    order = jnp.argsort(flat_e)
    sorted_e = flat_e[order]
    sorted_tok = order // TOP_K
    sorted_w = e_w.reshape(-1)[order]
    counts = jnp.bincount(flat_e, length=N_EXPERTS)
    starts = jnp.cumsum(counts) - counts
    padded = ((counts + EXPERT_BLOCK - 1) // EXPERT_BLOCK) * EXPERT_BLOCK
    pad_ends = jnp.cumsum(padded)
    pad_starts = pad_ends - padded
    dest = pad_starts[sorted_e] + jnp.arange(n_assign) - starts[sorted_e]
    n_blocks = -(-n_assign // EXPERT_BLOCK) + N_EXPERTS
    cap = n_blocks * EXPERT_BLOCK
    x_pad = jnp.zeros((cap, d), h.dtype).at[dest].set(xt[sorted_tok])
    block_e = jnp.minimum(
        jnp.searchsorted(pad_ends, jnp.arange(n_blocks) * EXPERT_BLOCK, side="right"), N_EXPERTS - 1)

    def run_block(args):
        xb, e = args
        return (jax.nn.silu(xb @ w_gate[e]) * (xb @ w_up[e])) @ w_down[e]

    y_pad = lax.map(run_block, (x_pad.reshape(n_blocks, EXPERT_BLOCK, d), block_e)).reshape(cap, d)
    y = y_pad[dest] * sorted_w[:, None].astype(h.dtype)
    out = jnp.zeros((n_tok, d), h.dtype).at[sorted_tok].add(y)
    return out.reshape(bsz, seq, d)

def first_inputs(seed: int = 0) -> dict:
    key = jax.random.key(seed)
    ks = jax.random.split(key, 28)
    L, D = DEPTH, D_MODEL
    nrm = lambda k, shape, s: jax.random.normal(k, shape, jnp.float32) * s
    return {
        "x": nrm(ks[0], (BATCH, SEQ, D), 1.0),
        "norm_mix_g": 1.0 + nrm(ks[1], (L, D), 0.02),
        "w_in": nrm(ks[2], (L, D, IN_COLS), D ** -0.5),
        "b_in": nrm(ks[3], (L, IN_COLS), 0.02),
        "conv_w": nrm(ks[4], (L, CONV_WIDTH, CONV_CH), CONV_WIDTH ** -0.5),
        "conv_b": nrm(ks[5], (L, CONV_CH), 0.02),
        "conv_ln_g": 1.0 + nrm(ks[6], (L, CONV_CH), 0.02),
        "conv_ln_b": nrm(ks[7], (L, CONV_CH), 0.02),
        "w_conv_out": nrm(ks[8], (L, CONV_CH, D), CONV_CH ** -0.5),
        "b_conv_out": nrm(ks[9], (L, D), 0.02),
        "sg_ln_g": 1.0 + nrm(ks[10], (L, SG_WIDTH), 0.02),
        "sg_ln_b": nrm(ks[11], (L, SG_WIDTH), 0.02),
        "w_sg": nrm(ks[12], (L, SG_HEADS, SG_BLOCK, SG_BLOCK), SG_BLOCK ** -0.5),
        "b_sg": 1.0 + nrm(ks[13], (L, SG_HEADS, SG_BLOCK), 0.02),
        "w_sg_out": nrm(ks[14], (L, SG_WIDTH, D), SG_WIDTH ** -0.5),
        "b_sg_out": nrm(ks[15], (L, D), 0.02),
        "w_out": nrm(ks[16], (L, D, D), D ** -0.5),
        "b_out": nrm(ks[17], (L, D), 0.02),
        "norm_ffn_g": 1.0 + nrm(ks[18], (L, D), 0.02),
        "w_router_group": nrm(ks[19], (L, D, N_GROUPS), D ** -0.5),
        "b_router_group": nrm(ks[20], (L, N_GROUPS), 0.01),
        "w_router_expert": nrm(ks[21], (L, D, N_EXPERTS), D ** -0.5),
        "b_router_expert": nrm(ks[22], (L, N_EXPERTS), 0.01),
        "w_expert_gate": nrm(ks[23], (L, N_EXPERTS, D, D_EXPERT), D ** -0.5),
        "w_expert_up": nrm(ks[24], (L, N_EXPERTS, D, D_EXPERT), D ** -0.5),
        "w_expert_down": nrm(ks[25], (L, N_EXPERTS, D_EXPERT, D), D_EXPERT ** -0.5),
        "norm_final_g": 1.0 + nrm(ks[26], (D,), 0.02),
    }

def first_block(x, norm_mix_g, w_in, b_in, conv_w, conv_b, conv_ln_g, conv_ln_b, w_conv_out, b_conv_out,
              sg_ln_g, sg_ln_b, w_sg, b_sg, w_sg_out, b_sg_out, w_out, b_out, norm_ffn_g,
              w_router_group, b_router_group, w_router_expert, b_router_expert,
              w_expert_gate, w_expert_up, w_expert_down, norm_final_g):
    for l in range(DEPTH):
        h = rms_norm(x, norm_mix_g[l])
        proj = h @ w_in[l] + b_in[l]
        a, z, gate_logits = jnp.split(proj, [2 * CONV_CH, 2 * CONV_CH + 2 * SG_WIDTH], axis=-1)
        y_a = conformer_conv_branch(a, conv_w[l], conv_b[l], conv_ln_g[l], conv_ln_b[l],
                                    w_conv_out[l], b_conv_out[l])
        y_b = spatial_gating_branch(z, sg_ln_g[l], sg_ln_b[l], w_sg[l], b_sg[l],
                                    w_sg_out[l], b_sg_out[l])
        g_a, g_b = jnp.split(jax.nn.sigmoid(gate_logits), 2, axis=-1)
        x = x + (g_a * y_a + g_b * y_b) @ w_out[l] + b_out[l]
        h = rms_norm(x, norm_ffn_g[l])
        x = x + hierarchical_moe(h, w_router_group[l], b_router_group[l], w_router_expert[l],
                                 b_router_expert[l], w_expert_gate[l], w_expert_up[l], w_expert_down[l])
    return rms_norm(x, norm_final_g)


N_HEADS_A = 8
HEAD_DIM_A = 64
N_IDX_HEADS = 16
IDX_DIM = 64
TOPK_MAX = 256
N_HEADS_B = 8
QK_NOPE_DIM = 64
QK_ROPE_DIM = 32
V_DIM_B = 64
Q_LORA = 384
KV_LORA = 256
D_MIX = N_HEADS_A * HEAD_DIM_A + N_HEADS_B * V_DIM_B
D_FF = 2816
ROPE_THETA = 10000.0
Q_BLOCK = 128

PROJ_SIZES = (
    N_HEADS_A * HEAD_DIM_A,
    HEAD_DIM_A,
    HEAD_DIM_A,
    N_IDX_HEADS * IDX_DIM,
    IDX_DIM,
    N_IDX_HEADS,
    Q_LORA,
    KV_LORA,
    QK_ROPE_DIM,
)
D_PROJ = sum(PROJ_SIZES)


def rmsnorm(x, g):
    xf = x.astype(jnp.float32)
    y = xf * lax.rsqrt(jnp.mean(xf * xf, axis=-1, keepdims=True) + EPS)
    return (y * g.astype(jnp.float32)).astype(x.dtype)

def swiglu(x, w_gate, w_up, w_down):
    return (jax.nn.silu(x @ w_gate) * (x @ w_up)) @ w_down

def rope_tables(seq_len, dim):
    pos = jnp.arange(seq_len, dtype=jnp.float32)
    inv_freq = ROPE_THETA ** (-jnp.arange(0, dim, 2, dtype=jnp.float32) / dim)
    ang = pos[:, None] * inv_freq[None, :]
    return jnp.cos(ang), jnp.sin(ang)

def apply_rope(x, cos, sin):
    shape = (cos.shape[0],) + (1,) * (x.ndim - 3) + (cos.shape[1],)
    c = cos.reshape(shape)
    s = sin.reshape(shape)
    xf = x.astype(jnp.float32)
    x1, x2 = jnp.split(xf, 2, axis=-1)
    return jnp.concatenate([x1 * c - x2 * s, x1 * s + x2 * c], axis=-1).astype(x.dtype)

def block_slice(a, start):
    return lax.dynamic_slice_in_dim(a, start, Q_BLOCK, axis=1)

def dsa_sparse_attention(q, k, v, q_idx, k_idx, w_idx):
    B, T = q.shape[0], q.shape[1]
    top_k = min(TOPK_MAX, T // 4)
    n_blocks = T // Q_BLOCK
    key_pos = jnp.arange(T)
    scale = HEAD_DIM_A ** -0.5
    idx_scale = (N_IDX_HEADS * IDX_DIM) ** -0.5

    def one_block(i):
        s0 = i * Q_BLOCK
        qb = block_slice(q, s0)
        qib = block_slice(q_idx, s0)
        wb = block_slice(w_idx, s0).astype(jnp.float32) * idx_scale
        qpos = s0 + jnp.arange(Q_BLOCK)
        causal = key_pos[None, :] <= qpos[:, None]
        idx_logits = jnp.einsum('bqhd,bsd->bqhs', qib, k_idx).astype(jnp.float32)
        score = jnp.einsum('bqh,bqhs->bqs', wb, jax.nn.relu(idx_logits))
        score = jnp.where(causal[None], score, -jnp.inf)
        _, sel = lax.top_k(score, top_k)
        valid = sel <= qpos[None, :, None]
        kg = jax.vmap(lambda kb, ib: kb[ib])(k, sel)
        vg = jax.vmap(lambda vb, ib: vb[ib])(v, sel)
        att = jnp.einsum('bqhd,bqkd->bqhk', qb, kg).astype(jnp.float32) * scale
        att = jnp.where(valid[:, :, None, :], att, -jnp.inf)
        p = jax.nn.softmax(att, axis=-1)
        return jnp.einsum('bqhk,bqkd->bqhd', p.astype(vg.dtype), vg)

    out = lax.map(one_block, jnp.arange(n_blocks))
    return jnp.moveaxis(out, 0, 1).reshape(B, T, N_HEADS_A * HEAD_DIM_A)

def mla_attention(c_q, c_kv, k_rope, g_q_lat, g_kv_lat, w_uq, w_ukv, cos_b, sin_b):
    B, T = c_q.shape[0], c_q.shape[1]
    n_blocks = T // Q_BLOCK
    key_pos = jnp.arange(T)
    scale = (QK_NOPE_DIM + QK_ROPE_DIM) ** -0.5
    q = (rmsnorm(c_q, g_q_lat) @ w_uq).reshape(B, T, N_HEADS_B, QK_NOPE_DIM + QK_ROPE_DIM)
    q_nope, q_pe = q[..., :QK_NOPE_DIM], q[..., QK_NOPE_DIM:]
    q_pe = apply_rope(q_pe, cos_b, sin_b)
    kv = (rmsnorm(c_kv, g_kv_lat) @ w_ukv).reshape(B, T, N_HEADS_B, QK_NOPE_DIM + V_DIM_B)
    k_nope, v = kv[..., :QK_NOPE_DIM], kv[..., QK_NOPE_DIM:]
    k_pe = apply_rope(k_rope, cos_b, sin_b)

    def one_block(i):
        s0 = i * Q_BLOCK
        qn = block_slice(q_nope, s0)
        qp = block_slice(q_pe, s0)
        qpos = s0 + jnp.arange(Q_BLOCK)
        causal = key_pos[None, :] <= qpos[:, None]
        s = (jnp.einsum('bqhd,bshd->bhqs', qn, k_nope)
             + jnp.einsum('bqhr,bsr->bhqs', qp, k_pe)).astype(jnp.float32) * scale
        s = jnp.where(causal[None, None], s, -jnp.inf)
        p = jax.nn.softmax(s, axis=-1)
        return jnp.einsum('bhqs,bshd->bqhd', p.astype(v.dtype), v)

    out = lax.map(one_block, jnp.arange(n_blocks))
    return jnp.moveaxis(out, 0, 1).reshape(B, T, N_HEADS_B * V_DIM_B)

def second_inputs(seed: int = 0) -> dict:
    key = jax.random.key(seed)
    ks = jax.random.split(key, 20)

    def w(k, shape, fan_in):
        return jax.random.normal(k, shape, jnp.float32) * (fan_in ** -0.5)

    def gain(k, shape):
        return 1.0 + 0.1 * jax.random.normal(k, shape, jnp.float32)

    L = DEPTH
    return {
        "x": jax.random.normal(ks[0], (BATCH, SEQ, D_MODEL), jnp.float32),
        "g_ffn1": gain(ks[1], (L, D_MODEL)),
        "w1_gate": w(ks[2], (L, D_MODEL, D_FF), D_MODEL),
        "w1_up": w(ks[3], (L, D_MODEL, D_FF), D_MODEL),
        "w1_down": w(ks[4], (L, D_FF, D_MODEL), D_FF),
        "g_mix": gain(ks[5], (L, D_MODEL)),
        "w_in": w(ks[6], (L, D_MODEL, D_PROJ), D_MODEL),
        "g_q_lat": gain(ks[7], (L, Q_LORA)),
        "g_kv_lat": gain(ks[8], (L, KV_LORA)),
        "w_uq": w(ks[9], (L, Q_LORA, N_HEADS_B * (QK_NOPE_DIM + QK_ROPE_DIM)), Q_LORA),
        "w_ukv": w(ks[10], (L, KV_LORA, N_HEADS_B * (QK_NOPE_DIM + V_DIM_B)), KV_LORA),
        "w_out": w(ks[11], (L, D_MIX, D_MODEL), D_MIX),
        "g_ffn2": gain(ks[12], (L, D_MODEL)),
        "w2_gate": w(ks[13], (L, D_MODEL, D_FF), D_MODEL),
        "w2_up": w(ks[14], (L, D_MODEL, D_FF), D_MODEL),
        "w2_down": w(ks[15], (L, D_FF, D_MODEL), D_FF),
        "g_final": gain(ks[16], (D_MODEL,)),
    }

def second_block(x, g_ffn1, w1_gate, w1_up, w1_down, g_mix, w_in, g_q_lat, g_kv_lat,
              w_uq, w_ukv, w_out, g_ffn2, w2_gate, w2_up, w2_down, g_final):
    B, T, _ = x.shape
    cos_a, sin_a = rope_tables(T, HEAD_DIM_A)
    cos_i, sin_i = rope_tables(T, IDX_DIM)
    cos_b, sin_b = rope_tables(T, QK_ROPE_DIM)
    split_points = [int(v) for v in np.cumsum(PROJ_SIZES)[:-1]]
    for l in range(DEPTH):
        x = x + 0.5 * swiglu(rmsnorm(x, g_ffn1[l]), w1_gate[l], w1_up[l], w1_down[l])
        h = rmsnorm(x, g_mix[l])
        p = h @ w_in[l]
        qa, ka, va, qi, ki, wi, cq, ckv, kr = jnp.split(p, split_points, axis=-1)
        qa = apply_rope(qa.reshape(B, T, N_HEADS_A, HEAD_DIM_A), cos_a, sin_a)
        ka = apply_rope(ka, cos_a, sin_a)
        qi = apply_rope(qi.reshape(B, T, N_IDX_HEADS, IDX_DIM), cos_i, sin_i)
        ki = apply_rope(ki, cos_i, sin_i)
        out_a = dsa_sparse_attention(qa, ka, va, qi, ki, wi)
        out_b = mla_attention(cq, ckv, kr, g_q_lat[l], g_kv_lat[l], w_uq[l], w_ukv[l], cos_b, sin_b)
        x = x + jnp.concatenate([out_a, out_b], axis=-1) @ w_out[l]
        x = x + 0.5 * swiglu(rmsnorm(x, g_ffn2[l]), w2_gate[l], w2_up[l], w2_down[l])
    return rmsnorm(x, g_final)


def setup_inputs(seed=0):
    out = dict(first_inputs(seed))
    for name, value in second_inputs(seed + 1).items():
        if name != "x":
            out[name + "_2"] = value
    return out


def reference(
    x, norm_mix_g, w_in, b_in, conv_w, conv_b, conv_ln_g, conv_ln_b, w_conv_out, b_conv_out,
    sg_ln_g, sg_ln_b, w_sg, b_sg, w_sg_out, b_sg_out, w_out, b_out, norm_ffn_g, w_router_group,
    b_router_group, w_router_expert, b_router_expert, w_expert_gate, w_expert_up, w_expert_down,
    norm_final_g, g_ffn1_2, w1_gate_2, w1_up_2, w1_down_2, g_mix_2, w_in_2, g_q_lat_2,
    g_kv_lat_2, w_uq_2, w_ukv_2, w_out_2, g_ffn2_2, w2_gate_2, w2_up_2, w2_down_2, g_final_2,
):
    x = first_block(
        x, norm_mix_g, w_in, b_in, conv_w, conv_b, conv_ln_g, conv_ln_b, w_conv_out, b_conv_out,
        sg_ln_g, sg_ln_b, w_sg, b_sg, w_sg_out, b_sg_out, w_out, b_out, norm_ffn_g,
        w_router_group, b_router_group, w_router_expert, b_router_expert, w_expert_gate,
        w_expert_up, w_expert_down, norm_final_g,
    )
    return second_block(
        x, g_ffn1_2, w1_gate_2, w1_up_2, w1_down_2, g_mix_2, w_in_2, g_q_lat_2, g_kv_lat_2,
        w_uq_2, w_ukv_2, w_out_2, g_ffn2_2, w2_gate_2, w2_up_2, w2_down_2, g_final_2,
    )


_drawn_inputs = setup_inputs


def setup_inputs(seed=0):
    import zlib

    import numpy as np

    out = dict(_drawn_inputs(seed))
    spreads = {}
    factors = {'conv_ln_g': 2.897,
     'sg_ln_g': 3.708,
     'sg_ln_b': 3.307,
     'b_sg': 4.55,
     'b_router_group': 3.818,
     'b_router_expert': 4.312,
     'g_q_lat_2': 5.801,
     'g_kv_lat_2': 3.269,
     'g_ffn2_2': 3.158}
    for name, (base, spread) in spreads.items():
        noise = np.random.default_rng([zlib.crc32(name.encode()), seed]).standard_normal(out[name].shape)
        drawn = base * np.exp(spread * noise) if base else spread * noise
        out[name] = __import__('jax').numpy.asarray(drawn.astype(out[name].dtype))
    for name, factor in factors.items():
        out[name] = (out[name] * factor).astype(out[name].dtype)
    return out
```

```python
from contextlib import ExitStack

import numpy as np

import concourse.bass as bass
from concourse import mybir

P = 128
T = 512
TT = T // P
D = 1024
KT = D // P
EPS = 1e-6
CONV_W = 31
PAD = CONV_W - 1
HEADS_SG = 8
SG_CHUNK = 64
GROUPS, PER_GROUP = 4, 8
EXPERTS = GROUPS * PER_GROUP
D_EXP = 512
TOP = 2
CAP = 64
PASSES = (TOP * T) // CAP + EXPERTS
FF = 2816
FT = FF // P
HALF = D // 2
BIG = 1.0e5
NEG = -1.0e30
FAR = -3.0e38
MARK = -3.3e38
HA, HDA, HI, HB = 8, 64, 16, 8
NOPE, ROPE, VB = 64, 32, 64
QL, KVL = 384, 256
C_QA, C_KA, C_VA, C_QI = 0, 512, 576, 640
C_KI, C_WI, C_CQ, C_CKV, C_KR = 1664, 1728, 1744, 2128, 2384
TOPK = 128

RAW, SPLIT = 4, 2
CK, CN = 2, 512

F32 = mybir.dt.float32
F32R = mybir.dt.float32r
I32 = mybir.dt.int32
ALU = mybir.AluOpType
ACT = mybir.ActivationFunctionType
AX = mybir.AxisListType

C_IN, G_IN, N_IN = 0, 0, 12
C_SGO, G_SGO = 48, 12
C_CVO, G_CVO = 56, 14
C_WO, G_WO = 64, 16
C_UP = [72, 166]
G_UP = [18, 38]
N_UP = 11
C_DN = [116, 210]
G_DN = [29, 49]
C_MIX, G_MIX, N_MIX = 138, 31, 5
C_MO, G_MO = 158, 36

K_ID, K_ONE, K_UP, K_RA, K_RB = 0, 128, 256, 384, 512
K_CB = 640
K_IOTA = 1152
K_TOK = 1216
K_HALF = 1220
K_CA = 1224
K_SA, K_CBT, K_SB = K_CA + T, K_CA + 2 * T, K_CA + 3 * T
K_N = K_CA + 4 * T


def constants():
    c = np.zeros((P, K_N), np.float32)
    p = np.arange(P)
    c[:, K_ID:K_ID + P] = np.eye(P)
    c[:, K_ONE:K_ONE + P] = 1
    c[:, K_UP:K_UP + P] = p[:, None] < p[None, :]

    def rotation(starts, half):
        m = np.zeros((P, P), np.float32)
        for s in starts:
            for j in range(half):
                m[s + half + j, s + j] = -1
                m[s + j, s + half + j] = 1
        return m

    c[:, K_RA:K_RA + P] = rotation((0, HDA), HDA // 2)
    c[:, K_RB:K_RB + P] = rotation((NOPE,), ROPE // 2)
    c[:, K_CB + 384:K_CB + 512] = np.where(p[None, :] <= p[:, None], 0, NEG)
    c[:, K_IOTA:K_IOTA + 64] = np.arange(64)
    c[:, K_TOK:K_TOK + TT] = p[:, None] + P * np.arange(TT)
    c[:, K_HALF] = p // CAP

    def angles(dim):
        inv = np.float32(10000.0) ** (-np.arange(0, dim, 2, dtype=np.float32) / np.float32(dim))
        return np.arange(T, dtype=np.float32)[None, :] * inv.astype(np.float32)[:, None]

    a = angles(HDA)[p % (HDA // 2)]
    c[:, K_CA:K_CA + T], c[:, K_SA:K_SA + T] = np.cos(a), np.sin(a)
    b = angles(ROPE)[p % (ROPE // 2)]
    rope = ((p >= NOPE) & (p < NOPE + ROPE))[:, None]
    c[:, K_CBT:K_CBT + T] = np.where(rope, np.cos(b), 1)
    c[:, K_SB:K_SB + T] = np.where(rope, np.sin(b), 0)
    return c


def program(nc, A, out):
    with ExitStack() as ctx:
        def sb(name, n, dt=F32):
            return ctx.enter_context(nc.sbuf_tensor(name, [P, n], dt))

        def sem(name):
            return ctx.enter_context(nc.semaphore(name))

        const = sb("const", K_N)
        xT_ = sb("xT", KT * T)
        raw_ = sb("w_raw", RAW * CK * CN)
        whi_ = sb("w_hi", SPLIT * CK * CN, F32R)
        wlo_ = sb("w_lo", SPLIT * CK * CN, F32R)
        stat_mean = sb("stat_mean", T)
        stat_std = sb("stat_std", T)
        eps_t = sb("eps", 1)
        eps_col = eps_t[:, 0:1]
        sq_ = sb("sq", 2 * T)
        vec = sb("vec", 424)

        def tiles(t, n=T):
            return t[:, :].rearrange("p (k n) -> p k n", n=n)

        xT, sq = tiles(xT_), tiles(sq_)
        raw = raw_[:, :].rearrange("p (s k n) -> p s k n", s=RAW, k=CK)
        whi = whi_[:, :].rearrange("p (s k n) -> p s k n", s=SPLIT, k=CK)
        wlo = wlo_[:, :].rearrange("p (s k n) -> p s k n", s=SPLIT, k=CK)
        ident, ones = const[:, K_ID:K_ID + P], const[:, K_ONE:K_ONE + P]

        at = {}
        n_vec = 0
        for name, n in (("b_in", 48), ("conv_b", 8), ("conv_ln_g", 8), ("conv_ln_b", 8), ("b_conv_out", 8),
                        ("sg_ln_g", 8), ("sg_ln_b", 8), ("b_sg_out", 8), ("b_out", 8), ("norm_mix_g", 8),
                        ("norm_ffn_g", 8), ("norm_final_g", 8), ("g_ffn1_2", 8), ("g_mix_2", 8), ("g_ffn2_2", 8),
                        ("g_final_2", 8), ("g_q_lat_2", 3), ("g_kv_lat_2", 2)):
            at[name] = (n_vec, n)
            n_vec += n
        n_conv = n_vec
        n_vec += 8 * CONV_W
        assert n_vec <= 424
        conv_w = vec[:, n_conv:n_conv + 8 * CONV_W].rearrange("p (c j) -> p c j", j=CONV_W)

        def col(name, k):
            o, n = at[name]
            return vec[:, o + k:o + k + 1]

        NR = GROUPS + EXPERTS
        wr_ = sb("w_router", KT * NR + NR)
        wr = wr_[:, 0:KT * NR].rearrange("p (k e) -> p k e", e=NR)
        br = wr_[:, KT * NR:KT * NR + NR]
        gather_row = sb("gather_row", PASSES + 2, I32)
        scatter_row = sb("scatter_row", PASSES + 2, I32)
        row_weight = sb("row_weight", PASSES + 2)
        S_PAIR, S_ODD, S_END = 0, PASSES, 2 * PASSES
        sched = sb("schedule", 2 * PASSES + EXPERTS, I32)
        g_cur = [sb(f"gather_now{b}", 1, I32) for b in range(2)]
        s_cur = [sb(f"scatter_now{b}", 1, I32) for b in range(2)]

        pos_i = sb("slot_of_token", TT * TOP, I32)
        e_int = sb("expert_of_pass", 2 * PASSES, I32)

        AR = 25600
        with ExitStack() as c1:
            hhi_ = c1.enter_context(nc.sbuf_tensor("h_hi", [P, KT * T], F32R))
            hlo_ = c1.enter_context(nc.sbuf_tensor("h_lo", [P, KT * T], F32R))
            with nc.sbuf_tensor("arena1", [P, AR], F32) as ar1:
                pass
            with ExitStack() as c2:
                ahi_ = c2.enter_context(nc.sbuf_tensor("act_hi", [P, FT * T], F32R))
                alo_ = c2.enter_context(nc.sbuf_tensor("act_lo", [P, FT * T], F32R))
                gated_ = c2.enter_context(nc.sbuf_tensor("gated", [P, 4 * T], F32))
            with nc.sbuf_tensor("arena3", [P, AR], F32) as ar3:
                pass
        with nc.sbuf_tensor("expert_input", [P, 2 * KT * T], F32) as hx_:
            pass
        hhi, hlo = tiles(hhi_), tiles(hlo_)
        ahi, alo = tiles(ahi_), tiles(alo_)
        gated = gated_[:, :].rearrange("p (s k n) -> p s k n", s=2, k=2)

        sig = tiles(ar1[:, 0:4096])
        conv = sig
        APW = PAD + T
        a_pad = ar1[:, 4096:4096 + KT * APW].rearrange("p (k n) -> p k n", n=APW)
        vtok = ar1[:, 4096:8192].rearrange("p (t d) -> p t d", d=D)
        v = tiles(ar1[:, 8448:12544])
        hF = v
        u = tiles(ar1[:, 12544:16640])
        wsg_in = ar1[:, 12544:12544 + 1024].rearrange("p (h k) -> p h k", k=P)
        ga = tiles(ar1[:, 16640:20736])
        x_tok = ar1[:, 16640:20736].rearrange("p (t d) -> p t d", d=D)
        vec_rows = ar1[:, 0:256].rearrange("p (r f) -> p r f", f=P)
        tap_rows = ar1[:, 256:1280]
        x_tok2 = ar1[:, 8448:12544].rearrange("p (t d) -> p t d", d=D)
        gb = xT
        wsgT = ar1[:, 20736:21760].rearrange("p (h q) -> p h q", q=P)
        bsg = ar1[:, 21760:22784].rearrange("p (h q) -> p h q", q=P)
        stat_mean2 = ar1[:, 23808:24320]
        sg_tmp = tiles(ar1[:, 22784:23808])
        wgu = [ar1[:, o:o + 8192].rearrange("p (k w n) -> p k w n", k=KT, w=2) for o in (0, 12288)]
        wd = [ar1[:, o:o + 4096].rearrange("p (k n) -> p k n", k=4) for o in (8192, 20480)]
        h2 = tiles(hx_[:, 0:4096])
        h_tok = hx_[:, 4096:8192].rearrange("p (t d) -> p t d", d=D)
        xg = [ar1[:, 24576 + b * 512:24576 + b * 512 + 512] for b in range(2)]
        y_tok = ar1[:, 0:8192].rearrange("p (t j d) -> p t j d", t=TT, j=TOP)
        y_sum = ar1[:, 8192:12288].rearrange("p (t d) -> p t d", d=D)
        xgT = [raw_[:, b * 512:b * 512 + 512].rearrange("p (c m) -> p c m", m=P) for b in range(2)]
        h_sg = [raw_[:, 1024 + b * 256:1280 + b * 256] for b in range(2)]
        heT = [raw_[:, 1536 + b * 256:1792 + b * 256].rearrange("p (c m) -> p c m", m=P) for b in range(2)]
        y_row = [raw_[:, 2048 + b * 512:2560 + b * 512] for b in range(2)]
        psum = ctx.enter_context(nc.psum_tensor("psum", [P, 8, T], F32))

        def bank(g, m):
            return psum[:, 4 * (g % 2) + m, :]

        consts_in = sem("consts_in")
        tables_in = sem("tables_in")
        vec_in = sem("vector_rows_in")
        vec_t = sem("vectors_transposed")
        vec_r = sem("vectors_ready")
        w_raw = [sem(f"w_raw{i}") for i in range(RAW)]
        w_raw2 = [sem(f"w_raw_up{i}") for i in range(RAW)]
        w_hi = sem("w_hi_ready")
        w_lo = sem("w_lo_ready")
        w_used = sem("w_used")
        evac = [sem("psum_group_read0"), sem("psum_group_read1")]

        x_in = sem("x_in")
        sg_in = sem("w_sg_in")
        x_t = sem("x_transposed")
        x_r = sem("x_ready")
        wsg_t = sem("w_sg_transposed")
        wsg_r = sem("w_sg_ready")
        pad_r = sem("conv_pad_ready")
        eps_r = sem("eps_ready")
        sq_r = sem("square_ready")
        sq_u = sem("square_summed")
        std_r = sem("root_ready")
        h_r = sem("normed_ready")
        hi_r = sem("act_hi_ready")
        lo_r = sem("act_lo_ready")
        dchain = sem("dve_step")
        conv_s = sem("conv_step")
        mm_r = sem("mean_summed")
        mean_r = sem("mean_ready")
        cen_r = sem("centred_ready")
        nrm_r = sem("layer_normed")
        vn_r = sem("v_ready")
        v_t = sem("v_transposed")
        vt_r = sem("v_on_tokens")
        sv_r = sem("spatial_sum_ready")
        s_r = sem("gate_product_ready")
        c_r = sem("conv_act_ready")
        m_r = sem("mix_ready")

        def group_read(eng, g):
            if g >= 0:
                eng.wait_ge(evac[g % 2], g // 2 + 1)

        chain = {"d": 0}

        def dlink(eng, ins):
            chain["d"] += 1
            ins.then_inc(dchain, 1)
            eng.wait_ge(dchain, chain["d"])

        cnt = dict.fromkeys(("sq_act", "sq_pe", "root", "inverse", "hi_act", "hi_dve", "h_dve", "x_dve"), 0)

        def squares(eng, src, tile_wait, n=KT):
            for k in range(n):
                if cnt["sq_act"] >= 2:
                    eng.wait_ge(sq_u, cnt["sq_act"] - 1)
                tile_wait(k)
                eng.activation(sq[:, cnt["sq_act"] % 2, :], src[:, k, :], ACT.Square).then_inc(sq_r, 1)
                cnt["sq_act"] += 1

        def sum_squares(eng, b, n=KT):
            for k in range(n):
                eng.wait_ge(sq_r, cnt["sq_pe"] + 1)
                eng.matmul(psum[:, b, :], ones, sq[:, cnt["sq_pe"] % 2, :], start=(k == 0),
                           stop=(k == n - 1)).then_inc(sq_u, 1)
                cnt["sq_pe"] += 1

        def root(eng, b, width=D):
            eng.wait_ge(sq_u, cnt["sq_act"])
            eng.activation(stat_std[:, :], psum[:, b, :], ACT.Sqrt, bias=eps_col, scale=1.0 / width).then_inc(std_r, 1)

        def inverse(eng):
            cnt["inverse"] += 1
            eng.wait_ge(std_r, cnt["inverse"])
            dlink(eng, eng.reciprocal(stat_std[:, :], stat_std[:, :]))

        def scale_rows(eng, dst, src, gain, sem_, n=KT):
            for k in range(n):
                eng.scalar_tensor_tensor(out=dst[:, k, :], in0=src[:, k, :], scalar=col(gain, k), in1=stat_std[:, :],
                                         op0=ALU.mult, op1=ALU.mult).then_inc(sem_, 1)

        def high_parts(eng, src, sem_, base, n=KT):
            for k in range(n):
                eng.wait_ge(sem_, base + k + 1)
                eng.activation(hhi[:, k, :], src[:, k, :], ACT.Copy).then_inc(hi_r, 1)

        def low_parts(eng, src, n=KT):
            for k in range(n):
                cnt["hi_dve"] += 1
                eng.wait_ge(hi_r, cnt["hi_dve"])
                eng.tensor_tensor(hlo[:, k, :], src[:, k, :], hhi[:, k, :].bitcast(F32), ALU.subtract).then_inc(lo_r, 1)

        def load_chunk(eng, c, slot, src, second=None, n2=0):
            if not isinstance(c, int) or c >= RAW:
                eng.wait_ge(w_lo, c - RAW + 1)
            if second is None:
                eng.dma_start(raw[:, slot, :, :], src).then_inc(w_raw[slot], 16)
            else:
                eng.dma_start(raw[:, slot, :, 0:CN // 2], src).then_inc(w_raw[slot], 16)
                eng.dma_start(raw[:, slot, :, CN // 2:CN], second).then_inc(w_raw2[slot], 16)

        def split_hi(eng, c0, k, i=0, step=0, up=None):
            slot = (c0 + k) % RAW
            eng.wait_ge(w_raw[slot], 16 * ((c0 + k) // RAW + 1) + i * (16 * step // RAW))
            if up is not None:
                eng.wait_ge(w_raw2[slot], 16 * (up // RAW + 1) + i * (16 * step // RAW))
            if step or c0 + k >= SPLIT:
                eng.wait_ge(w_used, c0 + k - SPLIT + 1 + i * step)
            eng.activation(whi[:, (c0 + k) % SPLIT, :, :], raw[:, slot, :, :], ACT.Copy).then_inc(w_hi, 1)

        def split_lo(eng, c0, k, i=0, step=0):
            slot, s = (c0 + k) % RAW, (c0 + k) % SPLIT
            eng.wait_ge(w_hi, c0 + k + 1 + i * step)
            eng.tensor_tensor(wlo[:, s, :, :], raw[:, slot, :, :], whi[:, s, :, :].bitcast(F32),
                              ALU.subtract).then_inc(w_lo, 1)

        def mm3(eng, o, w_h, w_l, x_h, x_l, first, last):
            eng.matmul(o, w_h, x_h, start=first, stop=False)
            eng.matmul(o, w_h, x_l, start=False, stop=False)
            return eng.matmul(o, w_l, x_h, start=False, stop=last)

        def mul_chunk(eng, c0, k, g, kts, xh, xl, first, last, i=0, step=0):
            s = (c0 + k) % SPLIT
            eng.wait_ge(w_lo, c0 + k + 1 + i * step)
            for a in range(CK):
                for m in range(4):
                    f = slice(m * P, m * P + P)
                    mm = mm3(eng, bank(g, m), whi[:, s, a, f], wlo[:, s, a, f], xh[:, kts[a], :], xl[:, kts[a], :],
                             first and a == 0, last and a == CK - 1)
            mm.then_inc(w_used, 1)

        def mul_group(eng, c0, g, xh, xl, i=0, step=0):
            if step or g >= 2:
                eng.wait_ge(evac[g % 2], g // 2 + i * (step // 8))
            for k in range(4):
                mul_chunk(eng, c0, k, g, (2 * k, 2 * k + 1), xh, xl, k == 0, k == 3, i, step)

        def mul_groups(eng, c0, g0, n, xh, xl):
            pairs = n // 2
            for j in range(2 if g0 < 2 else 0):
                mul_group(eng, c0 + 4 * j, g0 + j, xh, xl)
            lo = 1 if g0 < 2 else 0
            if pairs - lo > 1:
                with eng.Fori(lo, pairs) as i:
                    for j in range(2):
                        mul_group(eng, c0 + 4 * j, g0 + j, xh, xl, i, 8)
            else:
                for q in range(lo, pairs):
                    for j in range(2):
                        mul_group(eng, c0 + 8 * q + 4 * j, g0 + 2 * q + j, xh, xl)
            if n % 2:
                mul_group(eng, c0 + 4 * (n - 1), g0 + n - 1, xh, xl)

        w_in_v = A["w_in"].rearrange("o (k p) n -> p (o k) n", p=P)
        order = [1024, 1536, 0, 512, 3072, 3584, 2048, 2560, 4096, 4608, 5120, 5632]
        def sp_block1(sp):
            sp.dma_start(const[:, 0:K_CB], A["consts"][:, 0:K_CB]).then_inc(consts_in, 16)
            sp.dma_start(x_tok, A["x"].rearrange("o (t p) d -> p (o t) d", p=P)).then_inc(x_in, 16)
            sp.dma_start(wsg_in, A["w_sg"].rearrange("o h q k -> q (o h) k")).then_inc(sg_in, 16)
            sp.dma_start(bsg.rearrange("p h q -> p (h q)"),
                         A["b_sg"].rearrange("o h q -> o (h q)").to_broadcast([P, HEADS_SG * P])).then_inc(sg_in, 16)
            sp.dma_start(const[:, K_CB:K_N], A["consts"][:, K_CB:K_N]).then_inc(tables_in, 16)
            for g in range(N_IN):
                for k in range(4):
                    load_chunk(sp, C_IN + 4 * g + k, k, w_in_v[:, 2 * k:2 * k + 2, order[g]:order[g] + CN])
            for c0, name in ((C_SGO, "w_sg_out"), (C_CVO, "w_conv_out"), (C_WO, "w_out")):
                wv = A[name].rearrange("o (k p) n -> p (o k) n", p=P)
                for g in range(2):
                    for k in range(4):
                        load_chunk(sp, c0 + 4 * g + k, k, wv[:, 2 * k:2 * k + 2, CN * g:CN * g + CN])
                if c0 == C_SGO:
                    sp.wait_ge(vt_r, TT)
                    sp.dma_start(x_tok2, A["x"].rearrange("o (t p) d -> p (o t) d", p=P)).then_inc(x_in, 16)

        def act_vectors(act):
            for name, (o, n) in at.items():
                src = A[name]
                src = src.rearrange("(k p) -> k p", p=P) if len(src.shape) == 1 else \
                    src.rearrange("o (k p) -> (o k) p", p=P)
                act.dma_start(vec_rows[o % P:o % P + n, o // P, :], src).then_inc(vec_in, 16)
            act.dma_start(tap_rows[0:CONV_W, :], A["conv_w"][0]).then_inc(vec_in, 16)

        def pool_block1(pool):
            pool.memset(eps_t[:, :], EPS).then_inc(eps_r, 1)
            pool.memset(a_pad[:, :, 0:PAD], 0.0).then_inc(pad_r, 1)
            pool.memset(wsgT[:, :, :], 0.0).then_inc(pad_r, 1)

        def transpose_x(pe, src):
            for k in range(KT):
                for t in range(TT):
                    mm = pe.transpose(psum[:, k, t * P:(t + 1) * P], src[:, t, k * P:(k + 1) * P], ident)
                mm.then_inc(x_t, 1)

        def pe_block1(pe):
            pe.wait_ge(consts_in, 16)
            pe.wait_ge(x_in, 16)
            transpose_x(pe, x_tok)
            pe.wait_ge(vec_in, 16 * (len(at) + 1))
            pe.wait_ge(x_r, KT)
            for o in range(0, n_conv, P):
                n = min(P, n_conv - o)
                pe.transpose(psum[:, 5, o:o + n], vec_rows[0:n, o // P, :], ident[0:n, 0:n])
            for c in range(KT):
                o = n_conv + c * CONV_W
                mm = pe.transpose(psum[:, 5, o:o + CONV_W], tap_rows[0:CONV_W, c * P:(c + 1) * P],
                                  ident[0:CONV_W, 0:CONV_W])
            mm.then_inc(vec_t, 1)
            pe.wait_ge(sg_in, 32)
            for h in range(HEADS_SG):
                mm = pe.transpose(psum[:, 6 + h // 4, (h % 4) * P:(h % 4 + 1) * P], wsg_in[:, h, :], ident)
            mm.then_inc(wsg_t, 1)
            sum_squares(pe, 0)
            pe.wait_ge(wsg_r, 2)
            pe.wait_ge(lo_r, KT)
            mul_groups(pe, C_IN, G_IN, N_IN, hhi, hlo)
            group_read(pe, 10)
            group_read(pe, 11)
            for k in range(KT):
                mm = pe.matmul(psum[:, 0, :], ones, v[:, k, :], start=(k == 0), stop=(k == KT - 1))
            mm.then_inc(mm_r, 1)
            pe.wait_ge(conv_s, KT * CONV_W)
            for k in range(KT):
                mm = pe.matmul(psum[:, 1, :], ones, conv[:, k, :], start=(k == 0), stop=(k == KT - 1))
            mm.then_inc(mm_r, 1)
            sum_squares(pe, 2)
            pe.wait_ge(mean_r, 2)
            pe.wait_ge(vn_r, KT)
            for t in range(TT):
                for k in range(KT):
                    mm = pe.transpose(psum[:, 2 * t + k // 4, (k % 4) * P:(k % 4 + 1) * P],
                                      v[:, k, t * P:(t + 1) * P], ident)
                mm.then_inc(v_t, 1)
            pe.wait_ge(vt_r, TT)
            for h in range(HEADS_SG):
                for t in range(TT):
                    mm = pe.matmul(psum[:, h, t * P:(t + 1) * P], vtok[:, t, h * P:(h + 1) * P], wsgT[:, h, :],
                                   start=True, stop=True)
                mm.then_inc(sv_r, 1)
            pe.wait_ge(s_r, HEADS_SG)
            sum_squares(pe, 7)
            pe.wait_ge(std_r, 3)
            pe.wait_ge(lo_r, 2 * KT)
            mul_groups(pe, C_SGO, G_SGO, 2, hhi, hlo)
            pe.wait_ge(lo_r, 3 * KT)
            mul_groups(pe, C_CVO, G_CVO, 2, hhi, hlo)
            group_read(pe, G_CVO)
            group_read(pe, G_CVO + 1)
            pe.wait_ge(x_in, 32)
            transpose_x(pe, x_tok2)
            pe.wait_ge(x_r, 2 * KT)
            pe.wait_ge(lo_r, 4 * KT)
            mul_groups(pe, C_WO, G_WO, 2, hhi, hlo)

        kinds = [ACT.Sigmoid] * 2 + [None] * 2 + [ACT.Gelu] * 4 + [ACT.Sigmoid] * 4
        goal = [sig] * 2 + [a_pad] * 2 + [v] * 2 + [u] * 2 + [ga] * 2 + [gb] * 2

        def act_block1(act):
            def read_group(g):
                if kinds[g] is None:
                    return
                act.wait_ge(w_used, C_IN + 4 * g + 4)
                for m in range(4):
                    ins = act.activation(goal[g][:, 4 * (g % 2) + m, :], bank(g, m), kinds[g],
                                         bias=col("b_in", order[g] // P + m))
                ins.then_inc(evac[g % 2], 1)

            act_vectors(act)
            act.wait_ge(eps_r, 1)
            squares(act, xT, lambda k: act.wait_ge(x_r, k + 1))
            root(act, 0)
            act.wait_ge(vec_r, 1)
            high_parts(act, hF, h_r, 0)
            for g in range(N_IN):
                for k in range(4):
                    if k == 2 and g:
                        read_group(g - 1)
                    split_hi(act, C_IN + 4 * g, k)
            for k in range(SPLIT):
                split_hi(act, C_SGO, k)
            read_group(N_IN - 1)
            for j, dst in enumerate((stat_mean, stat_mean2)):
                act.wait_ge(mm_r, j + 1)
                act.activation(dst[:, :], psum[:, j, :], ACT.Identity, scale=1.0 / D).then_inc(mean_r, 1)
            squares(act, v, lambda k: act.wait_ge(cen_r, k + 1))
            root(act, 2)
            for k in range(KT):
                act.wait_ge(nrm_r, k + 1)
                act.activation(v[:, k, :], v[:, k, :], ACT.Identity, bias=col("sg_ln_b", k),
                               scale=col("sg_ln_g", k)).then_inc(vn_r, 1)
            for t in range(TT):
                act.wait_ge(v_t, t + 1)
                act.activation(vtok[:, t, :], psum[:, 2 * t:2 * t + 2, :].rearrange("p b n -> p (b n)"),
                               ACT.Copy).then_inc(vt_r, 1)
            high_parts(act, u, s_r, 0)
            squares(act, conv, lambda k: act.wait_ge(cen_r, KT + k + 1))
            root(act, 7)
            for k in range(2, 4):
                split_hi(act, C_SGO, k)
            for k in range(KT):
                act.wait_ge(nrm_r, KT + k + 1)
                act.activation(conv[:, k, :], conv[:, k, :], ACT.Silu, bias=col("conv_ln_b", k),
                               scale=col("conv_ln_g", k)).then_inc(c_r, 1)
            for k in range(4, 8):
                split_hi(act, C_SGO, k)
            for k in range(SPLIT):
                split_hi(act, C_CVO, k)
            act.wait_ge(w_used, C_CVO)
            high_parts(act, conv, c_r, 0)
            for k in range(2, 8):
                split_hi(act, C_CVO, k)
            for k in range(SPLIT):
                split_hi(act, C_WO, k)
            high_parts(act, ga, m_r, 0)
            for k in range(2, 8):
                split_hi(act, C_WO, k)

        def dve_block1(dve):
            for k in range(KT):
                dve.wait_ge(x_t, k + 1)
                dve.tensor_copy(xT[:, k, :], psum[:, k, :]).then_inc(x_r, 1)
            dve.wait_ge(vec_t, 1)
            dve.tensor_copy(vec[:, 0:n_vec], psum[:, 5, 0:n_vec]).then_inc(vec_r, 1)
            dve.wait_ge(wsg_t, 1)
            dve.wait_ge(pad_r, 2)
            wsg_ps = psum[:, 6:8, :].rearrange("p b (h q) -> p (b h) q", q=P)
            dve.tensor_copy(wsgT[0:SG_CHUNK, :, :], wsg_ps[0:SG_CHUNK, :, :]).then_inc(wsg_r, 1)
            dve.tensor_copy(wsgT[SG_CHUNK:P, :, SG_CHUNK:P], wsg_ps[SG_CHUNK:P, :, SG_CHUNK:P]).then_inc(wsg_r, 1)
            inverse(dve)
            dve.wait_ge(vec_r, 1)
            scale_rows(dve, hF, xT, "norm_mix_g", h_r)
            low_parts(dve, hF)

            def read_glu(g):
                dve.wait_ge(w_used, C_IN + 4 * g + 4)
                if g == 2:
                    group_read(dve, 0)
                    group_read(dve, 1)
                for m in range(4):
                    k = 4 * (g % 2) + m
                    ins = dve.scalar_tensor_tensor(out=a_pad[:, k, PAD:APW], in0=bank(g, m),
                                                   scalar=col("b_in", order[g] // P + m), in1=sig[:, k, :],
                                                   op0=ALU.add, op1=ALU.mult)
                ins.then_inc(evac[g % 2], 1)

            for g in range(4):
                for k in range(4):
                    if k == 2 and g == 3:
                        read_glu(2)
                    split_lo(dve, C_IN + 4 * g, k)
            split_lo(dve, C_IN + 16, 0)
            split_lo(dve, C_IN + 16, 1)
            read_glu(3)
            group_read(dve, 3)
            dve.wait_ge(pad_r, 1)
            per = 2 * CONV_W
            with dve.Fori(0, KT // 2) as i:
                for n in range(per):
                    j, q = n // 2, n % 2
                    if n >= 2:
                        dve.wait_ge(conv_s, per * i + n - 1)
                    c = 2 * i + q
                    src = a_pad[:, bass.ds(c, 1), j:j + T].rearrange("p o n -> p (o n)")
                    dst = conv[:, bass.ds(c, 1), :].rearrange("p o n -> p (o n)")
                    tap = conv_w[:, bass.ds(c, 1), j]
                    if j == 0:
                        bias = vec[:, bass.ds(at["conv_b"][0] + c, 1)]
                        dve.tensor_scalar(dst, src, tap, bias, ALU.mult, ALU.add).then_inc(conv_s, 1)
                    else:
                        dve.scalar_tensor_tensor(out=dst, in0=src, scalar=tap, in1=dst, op0=ALU.mult,
                                                 op1=ALU.add).then_inc(conv_s, 1)
                    if n % 8 == 7 or n == per - 1:
                        split_lo(dve, C_IN + 16, 2 + n // 8, i, 8)
            dve.wait_ge(mean_r, 1)
            group_read(dve, 4)
            group_read(dve, 5)
            for k in range(KT):
                dve.tensor_tensor(v[:, k, :], v[:, k, :], stat_mean[:, :], ALU.subtract).then_inc(cen_r, 1)
            inverse(dve)
            dve.wait_ge(cen_r, KT)
            for k in range(KT):
                dve.tensor_tensor(v[:, k, :], v[:, k, :], stat_std[:, :], ALU.mult).then_inc(nrm_r, 1)
            dve.wait_ge(mean_r, 2)
            for k in range(KT):
                dve.tensor_tensor(conv[:, k, :], conv[:, k, :], stat_mean2[:, :], ALU.subtract).then_inc(cen_r, 1)
            group_read(dve, 6)
            group_read(dve, 7)
            dve.wait_ge(sg_in, 32)
            for h in range(HEADS_SG):
                dve.wait_ge(sv_r, h + 1)
                dlink(dve, dve.tensor_tensor(
                    sg_tmp[:, h % 2, :].rearrange("p (t q) -> p t q", q=P),
                    psum[:, h, :].rearrange("p (t q) -> p t q", q=P),
                    bsg[:, h, :].unsqueeze(1).to_broadcast([P, TT, P]), ALU.add))
                dve.tensor_tensor(u[:, h, :], u[:, h, :], sg_tmp[:, h % 2, :], ALU.mult).then_inc(s_r, 1)
            low_parts(dve, u)
            inverse(dve)
            dve.wait_ge(cen_r, 2 * KT)
            for k in range(2, 4):
                split_lo(dve, C_SGO, k)
            for k in range(KT):
                dve.tensor_tensor(conv[:, k, :], conv[:, k, :], stat_std[:, :], ALU.mult).then_inc(nrm_r, 1)

            def read_gated(g, name, gate):
                dve.wait_ge(w_used, 4 * g + 4)
                group_read(dve, 8 if gate is ga else 10)
                group_read(dve, 9 if gate is ga else 11)
                for m in range(4):
                    k = 4 * (g % 2) + m
                    ins = dve.scalar_tensor_tensor(out=gate[:, k, :], in0=bank(g, m), scalar=col(name, k),
                                                   in1=gate[:, k, :], op0=ALU.add, op1=ALU.mult)
                ins.then_inc(evac[g % 2], 1)

            for k in range(4, 8):
                split_lo(dve, C_SGO, k)
            read_gated(G_SGO, "b_sg_out", gb)
            for k in range(SPLIT):
                split_lo(dve, C_CVO, k)
            read_gated(G_SGO + 1, "b_sg_out", gb)
            low_parts(dve, conv)
            for k in range(2, 6):
                split_lo(dve, C_CVO, k)
            read_gated(G_CVO, "b_conv_out", ga)
            for k in range(6, 8):
                split_lo(dve, C_CVO, k)
            for k in range(SPLIT):
                split_lo(dve, C_WO, k)
            read_gated(G_CVO + 1, "b_conv_out", ga)
            group_read(dve, G_CVO)
            group_read(dve, G_CVO + 1)
            for k in range(KT):
                dve.tensor_tensor(ga[:, k, :], ga[:, k, :], gb[:, k, :], ALU.add).then_inc(m_r, 1)
            low_parts(dve, ga)
            dve.wait_ge(m_r, KT)
            for k in range(KT):
                dve.wait_ge(x_t, KT + k + 1)
                dve.tensor_copy(xT[:, k, :], psum[:, k, :]).then_inc(x_r, 1)
            dve.wait_ge(x_r, 2 * KT)
            for g in (G_WO, G_WO + 1):
                for k in range(2, 6) if g == G_WO else range(6, 8):
                    split_lo(dve, C_WO, k)
                dve.wait_ge(w_used, 4 * g + 4)
                for m in range(4):
                    k = 4 * (g % 2) + m
                    ins = dve.scalar_tensor_tensor(out=xT[:, k, :], in0=bank(g, m), scalar=col("b_out", k),
                                                   in1=xT[:, k, :], op0=ALU.add, op1=ALU.add)
                ins.then_inc(evac[g % 2], 1)

        moe = {n: sem("moe_" + n) for n in (
            "table_init", "h_tok", "h_dram", "logits", "logits_read", "exp_in", "exp", "onehot", "rank", "pos", "placed", "table",
            "tables", "x_t", "x", "gu", "act", "prod", "h_t", "h", "y_sum", "y", "pass", "done", "y_in", "begun", "sum_t", "sums")}
        gathered = [sem(f"moe_gathered{b}") for b in range(2)]
        scattered = [sem(f"moe_scattered{b}") for b in range(2)]
        w_gu = [sem(f"moe_gate_up_in{b}") for b in range(2)]
        w_dn = [sem(f"moe_down_in{b}") for b in range(2)]
        idx_r = sem("moe_index_ready")
        wr_in = sem("router_in")
        h_dram = nc.dram_tensor("normed_rows", (2 * T, HALF), F32, kind="Internal").ap()
        y_dram = nc.dram_tensor("expert_rows", (2 * TOP * T, HALF), F32, kind="Internal").ap()
        table = nc.dram_tensor("slot_table", ((PASSES + 2) * CAP, 4), F32, kind="Internal").ap()
        tbl = y_row[0][:, 0:(PASSES + 2) * 4].rearrange("p (n f) -> p n f", f=4)
        SC = [0]

        def scratch(*dims):
            n = int(np.prod(dims))
            o = SC[0]
            SC[0] += n
            assert SC[0] <= 2048
            t = raw_[:, o:o + n]
            if len(dims) == 2:
                t = t.rearrange("p (a b) -> p a b", b=dims[1])
            if len(dims) == 3:
                t = t.rearrange("p (a b c) -> p a b c", b=dims[1], c=dims[2])
            return t

        lg = scratch(TT, NR)
        g_max, g_sel, g_w, v1, v2, i1, i2, den = (scratch(TT, 1) for _ in range(8))
        g_tmp, g_hot = scratch(TT, GROUPS), scratch(TT, GROUPS)
        e_all = scratch(TT, GROUPS, PER_GROUP)
        es, e_tmp, e_hot = scratch(TT, PER_GROUP), scratch(TT, PER_GROUP), scratch(TT, PER_GROUP)
        ex = scratch(TT, GROUPS + 1)
        hot = [scratch(TT, EXPERTS) for _ in range(TOP)]
        hots, place = scratch(TT, EXPERTS), scratch(TT, EXPERTS)
        w_tok = [scratch(TT, 1) for _ in range(TOP)]
        pos_f = scratch(TT, TOP)
        n_pass, p_end, p_base = scratch(EXPERTS), scratch(EXPERTS), scratch(EXPERTS)
        pay = scratch(TT, TOP, 4)
        init_row = ar1[:, 24576:24576 + 200].rearrange("p (r f) -> p r f", f=4)
        over = scratch(EXPERTS, T // CAP)
        e_of = scratch(PASSES)
        late = raw_[:, 2560:2560 + PASSES * EXPERTS].rearrange("p (n e) -> p n e", e=EXPERTS)
        pos = pos_i[:, :].rearrange("p (t j) -> p t j", j=TOP)

        def iota(n):
            return const[:, K_IOTA:K_IOTA + n]

        def load_expert(sp, e, b):
            def rows(name, k):
                src = A[name].rearrange("o e (k p) n -> (o e) p k n", p=P)
                return src[e] if isinstance(e, int) else src[bass.ds(e, 1)].rearrange("o p k n -> p (o k) n")

            sp.dma_start(wgu[b][:, :, 0, :], rows("w_expert_gate", KT)).then_inc(w_gu[b], 16)
            sp.dma_start(wgu[b][:, :, 1, :], rows("w_expert_up", KT)).then_inc(w_gu[b], 16)
            sp.dma_start(wd[b], rows("w_expert_down", 4)).then_inc(w_dn[b], 16)

        def sp_router(sp):
            wv = A["w_router_group"].rearrange("o (k p) e -> p (o k) e", p=P)
            we = A["w_router_expert"].rearrange("o (k p) e -> p (o k) e", p=P)
            with nc.allow_non_contiguous_dma(reason="router weights"):
                sp.dma_start(wr[:, :, 0:GROUPS], wv).then_inc(wr_in, 16)
                sp.dma_start(wr[:, :, GROUPS:NR], we).then_inc(wr_in, 16)
                sp.dma_start(br[:, 0:GROUPS], A["b_router_group"].to_broadcast([P, GROUPS])).then_inc(wr_in, 16)
                sp.dma_start(br[:, GROUPS:NR], A["b_router_expert"].to_broadcast([P, EXPERTS])).then_inc(wr_in, 16)

        def sp_moe(sp):
            sp.wait_ge(x_t, 2 * KT)
            sp.wait_ge(w_used, C_WO)
            load_expert(sp, 0, 0)
            sp.wait_ge(lo_r, 4 * KT)
            load_expert(sp, 1, 1)
            for t in range(TT):
                sp.wait_ge(moe["h_tok"], t + 1)
                sp.dma_start(h_dram[2 * P * t:2 * P * (t + 1), :].rearrange("(p h) d -> p (h d)", h=2),
                             h_tok[:, t, :]).then_inc(moe["h_dram"], 16)
            sp.wait_ge(moe["placed"], 16 * TT * TOP)
            tv = table.rearrange("(n s) f -> s n f", s=CAP)
            sp.dma_start(tbl[0:CAP], tv).then_inc(moe["table"], 16)
            sp.dma_start(tbl[CAP:P], tv).then_inc(moe["table"], 16)
            sp.wait_ge(moe["h_dram"], 16 * TT)
            sp.wait_ge(moe["tables"], 1)
            with sp.Fori(1, EXPERTS // 2) as i:
                for b in range(2):
                    end = sp.value_load(sched[0:1, bass.ds(S_END + 2 * i - 2 + b, 1)], min_val=0, max_val=PASSES)
                    sp.wait_ge(moe["pass"], end + 1)
                    load_expert(sp, 2 * i + b, b)
            sp.wait_ge(moe["done"], 1)
            sp.dma_start(y_tok.rearrange("p t j d -> p t (j d)"),
                         y_dram.rearrange("(t p r) d -> p t (r d)", p=P, r=2 * TOP)).then_inc(moe["y_in"], 16)

        def pe_moe(pe):
            sum_squares(pe, 0)
            pe.wait_ge(wr_in, 64)
            for t in range(TT):
                for k in range(KT):
                    pe.wait_ge(h_r, KT + k + 1)
                    mm = pe.matmul(psum[:, 1, t * 64:t * 64 + NR], h2[:, k, t * P:(t + 1) * P], wr[:, k, :],
                                   start=(k == 0), stop=(k == KT - 1))
            mm.then_inc(moe["logits"], 1)
            for t in range(TT):
                if t == 3:
                    pe.wait_ge(moe["h_tok"], 1)
                for k in range(KT):
                    mm = pe.transpose(psum[:, 2 + 2 * (t % 3) + k // 4, (k % 4) * P:(k % 4 + 1) * P],
                                      h2[:, k, t * P:(t + 1) * P], ident)
                mm.then_inc(moe["x_t"], 1)
            pe.wait_ge(moe["onehot"], 1)
            for t in range(TT):
                for q in range(t):
                    pe.matmul(psum[:, 1, t * 32:t * 32 + 32], ones, hots[:, q, :], start=(q == 0), stop=False)
                pe.matmul(psum[:, 1, t * 32:t * 32 + 32], const[:, K_UP:K_UP + P], hots[:, t, :], start=(t == 0),
                          stop=True)
            for t in range(TT):
                mm = pe.matmul(psum[:, 1, P:P + 32], ones, hots[:, t, :], start=(t == 0), stop=(t == TT - 1))
            mm.then_inc(moe["rank"], 1)

            def turn(n, b):
                pe.wait_ge(gathered[b], 16 * (n // 2 + 1) if isinstance(n, int) else n * 8 + (16 - 8 * b))
                if not isinstance(n, int) or n >= 2:
                    pe.wait_ge(moe["x"], n - 1)
                for c in range(4):
                    mm = pe.transpose(psum[:, b, c * P:(c + 1) * P], xg[b][:, c * P:(c + 1) * P], ident)
                mm.then_inc(moe["x_t"], 1)

            def gate_up(n, b, w):
                for k in range(KT):
                    for q in range(2):
                        mm = pe.matmul(psum[q * CAP:(q + 1) * CAP, 2 + b, :].rearrange("p (w n) -> p w n", w=2),
                                       xgT[b][:, k % 4, (k // 4) * CAP:(k // 4 + 1) * CAP],
                                       wgu[w][:, k, :, q * 256:(q + 1) * 256], start=(k == 0), stop=(k == KT - 1))
                mm.then_inc(moe["gu"], 1)

            def down(n, b, w):
                for k in range(4):
                    for q in range(2):
                        mm = pe.matmul(psum[q * CAP:(q + 1) * CAP, 6 + b, :],
                                       heT[b][:, k % 2, (k // 2) * CAP:(k // 2 + 1) * CAP],
                                       wd[w][:, k, q * T:(q + 1) * T], start=(k == 0), stop=(k == 3))
                mm.then_inc(moe["pass"], 1)

            def pass_(n, b):
                pair = pe.value_load(sched[0:1, n:n + 1] if isinstance(n, int) else sched[0:1, bass.ds(S_PAIR + n, 1)],
                                     min_val=0, max_val=EXPERTS // 2 - 1)
                odd = pe.value_load(sched[0:1, S_ODD + n:S_ODD + n + 1] if isinstance(n, int)
                                    else sched[0:1, bass.ds(S_ODD + n, 1)], min_val=0, max_val=1)
                pe.wait_ge(moe["x"], n + 1)
                if not isinstance(n, int) or n >= 2:
                    pe.wait_ge(moe["y"], n - 1)
                with pe.If(odd < 1):
                    pe.wait_ge(w_gu[0], pair * 32 + 32)
                    gate_up(n, b, 0)
                with pe.Else():
                    pe.wait_ge(w_gu[1], pair * 32 + 32)
                    gate_up(n, b, 1)
                if b == 0:
                    turn(n + 1, 1)
                pe.wait_ge(moe["prod"], n + 1)
                for c in range(2):
                    mm = pe.transpose(psum[:, 4 + b, c * P:(c + 1) * P], h_sg[b][:, c * P:(c + 1) * P], ident)
                mm.then_inc(moe["h_t"], 1)
                pe.wait_ge(moe["h"], n + 1)
                with pe.If(odd < 1):
                    pe.wait_ge(w_dn[0], pair * 16 + 16)
                    down(n, b, 0)
                with pe.Else():
                    pe.wait_ge(w_dn[1], pair * 16 + 16)
                    down(n, b, 1)

            def two(i):
                turn(2 * i, 0)
                for b in range(2):
                    pass_(2 * i + b, b)

            pe.wait_ge(moe["tables"], 1)
            pe.sem_inc(moe["pass"], 1)
            two(0)
            total = pe.value_load(sched[0:1, S_END + EXPERTS - 1:S_END + EXPERTS], min_val=1, max_val=PASSES)
            with pe.Fori(1, PASSES // 2) as i:
                with pe.If(i * 2 < total):
                    two(i)
            pe.wait_ge(moe["sums"], TT)
            for k in range(KT):
                for t in range(TT):
                    mm = pe.transpose(psum[:, k, t * P:(t + 1) * P], y_sum[:, t, k * P:(k + 1) * P], ident)
                mm.then_inc(moe["sum_t"], 1)

        def act_moe(act):
            squares(act, xT, lambda k: group_read(act, G_WO + k // 4))
            root(act, 0)
            for t in range(TT):
                act.wait_ge(moe["x_t"], t + 1)
                act.activation(h_tok[:, t, :], psum[:, 2 + 2 * (t % 3):4 + 2 * (t % 3), :].rearrange(
                    "p b n -> p (b n)"), ACT.Copy).then_inc(moe["h_tok"], 1)
            act.wait_ge(moe["exp_in"], 2)
            act.activation(ex, ex, ACT.Exp).then_inc(moe["exp"], 1)

            def pass_(n, b):
                act.wait_ge(moe["x_t"], n + 1 + TT)
                act.activation(xgT[b], psum[:, b, :].rearrange("p (c m) -> p c m", m=P), ACT.Copy).then_inc(
                    moe["x"], 1)

            def pass2(n, b):
                act.wait_ge(moe["gu"], n + 1)
                if not isinstance(n, int) or n >= 2:
                    act.wait_ge(moe["h_t"], n - 1)
                act.activation(h_sg[b], psum[:, 2 + b, 0:256], ACT.Silu).then_inc(moe["act"], 1)

            def two(i):
                pass_(2 * i, 0)
                pass2(2 * i, 0)
                pass_(2 * i + 1, 1)
                pass2(2 * i + 1, 1)

            act.wait_ge(moe["tables"], 1)
            two(0)
            total = act.value_load(sched[0:1, S_END + EXPERTS - 1:S_END + EXPERTS], min_val=1, max_val=PASSES)
            with act.Fori(1, PASSES // 2) as i:
                with act.If(i * 2 < total):
                    two(i)

        def dve_moe(dve):
            dve.wait_ge(tables_in, 16)
            inverse(dve)
            group_read(dve, G_WO)
            group_read(dve, G_WO + 1)
            scale_rows(dve, h2, xT, "norm_ffn_g", h_r)
            dve.wait_ge(moe["logits"], 1)
            dve.wait_ge(wr_in, 64)

            def bc(t, n):
                return t.to_broadcast([P, TT, n])

            def row(n):
                return iota(n).unsqueeze(1).to_broadcast([P, TT, n])

            def link(ins):
                dlink(dve, ins)

            def first_max(vals, n, best, where, one_hot, tmp):
                link(dve.tensor_reduce(best, vals, AX.X, ALU.max))
                link(dve.tensor_tensor(tmp, vals, bc(best, n), ALU.is_equal))
                link(dve.tensor_scalar(tmp, tmp, -99.0, 99.0, ALU.mult, ALU.add))
                link(dve.tensor_tensor(tmp, tmp, row(n), ALU.add))
                link(dve.tensor_reduce(where, tmp, AX.X, ALU.min))
                link(dve.tensor_tensor(one_hot, row(n), bc(where, n), ALU.is_equal))

            lg_ps = psum[:, 1, 0:TT * 64].rearrange("p (t e) -> p t e", e=64)[:, :, 0:NR]
            link(dve.tensor_tensor(lg, lg_ps, br.unsqueeze(1).to_broadcast([P, TT, NR]), ALU.add))
            gl = lg[:, :, 0:GROUPS]
            first_max(gl, GROUPS, g_max, g_sel, g_hot, g_tmp)
            dve.tensor_tensor(ex[:, :, 0:GROUPS], gl, bc(g_max, GROUPS), ALU.subtract).then_inc(moe["exp_in"], 1)
            link(dve.tensor_tensor(e_all, lg[:, :, GROUPS:NR].rearrange("p t (g j) -> p t g j", g=GROUPS),
                                   g_hot.unsqueeze(3).to_broadcast([P, TT, GROUPS, PER_GROUP]), ALU.mult))
            link(dve.tensor_reduce(es, e_all.rearrange("p t g j -> p t j g"), AX.X, ALU.add))
            first_max(es, PER_GROUP, v1, i1, e_hot, e_tmp)
            link(dve.scalar_tensor_tensor(out=es, in0=e_hot, scalar=FAR, in1=es, op0=ALU.mult, op1=ALU.add))
            first_max(es, PER_GROUP, v2, i2, e_hot, e_tmp)
            dve.tensor_tensor(ex[:, :, GROUPS:GROUPS + 1], v2, v1, ALU.subtract).then_inc(moe["exp_in"], 1)
            for j, i_ in enumerate((i1, i2)):
                link(dve.scalar_tensor_tensor(out=i_, in0=g_sel, scalar=float(PER_GROUP), in1=i_, op0=ALU.mult,
                                              op1=ALU.add))
                link(dve.tensor_tensor(hot[j], row(EXPERTS), bc(i_, EXPERTS), ALU.is_equal))
            dve.tensor_tensor(hots, hot[0], hot[1], ALU.add).then_inc(moe["onehot"], 1)
            dve.wait_ge(moe["exp"], 1)
            link(dve.tensor_reduce(g_w, ex[:, :, 0:GROUPS], AX.X, ALU.add))
            link(dve.tensor_scalar(den, ex[:, :, GROUPS:GROUPS + 1], 1.0, None, ALU.add))
            link(dve.tensor_tensor(den, den, g_w, ALU.mult))
            link(dve.reciprocal(w_tok[0], den))
            link(dve.tensor_tensor(w_tok[1], w_tok[0], ex[:, :, GROUPS:GROUPS + 1], ALU.mult))
            dve.wait_ge(moe["rank"], 1)
            link(dve.tensor_scalar(over, iota(T // CAP).unsqueeze(1).to_broadcast([P, EXPERTS, T // CAP]), float(CAP), None,
                                   ALU.mult))
            link(dve.tensor_tensor(over, psum[:, 1, P:P + EXPERTS].unsqueeze(2).to_broadcast([P, EXPERTS, T // CAP]),
                                   over, ALU.is_gt))
            link(dve.tensor_reduce(n_pass, over, AX.X, ALU.add))
            link(dve.tensor_tensor_scan(p_end, ones[:, 0:EXPERTS], n_pass, 0.0, ALU.mult, ALU.add))
            link(dve.tensor_tensor(p_base, p_end, n_pass, ALU.subtract))
            link(dve.tensor_scalar(p_base, p_base, float(CAP), None, ALU.mult))
            link(dve.tensor_tensor(place, psum[:, 1, 0:TT * EXPERTS].rearrange("p (t e) -> p t e", e=EXPERTS),
                                   p_base.unsqueeze(1).to_broadcast([P, TT, EXPERTS]), ALU.add))
            for j in range(TOP):
                link(dve.tensor_tensor(hot[j], hot[j], place, ALU.mult))
                link(dve.tensor_reduce(pos_f[:, :, j:j + 1], hot[j], AX.X, ALU.add))
                tok = const[:, K_TOK:K_TOK + TT].unsqueeze(2)
                dve.tensor_scalar(pay[:, :, j, 0:1], tok, 2.0, None, ALU.mult)
                dve.tensor_scalar(pay[:, :, j, 1:2], tok, 4.0, 2.0 * j, ALU.mult, ALU.add)
                dve.tensor_copy(pay[:, :, j, 2:3], w_tok[j])
                dve.memset(pay[:, :, j, 3:4], 0.0)
            dve.tensor_copy(pos, pos_f).then_inc(moe["pos"], 1)
            link(dve.tensor_tensor(late, p_end.unsqueeze(1).to_broadcast([P, PASSES, EXPERTS]),
                                   iota(PASSES).unsqueeze(2).to_broadcast([P, PASSES, EXPERTS]), ALU.is_le))
            link(dve.tensor_reduce(e_of, late, AX.X, ALU.add))
            link(dve.tensor_scalar(e_int[:, 0:PASSES], e_of, float(EXPERTS - 1), None, ALU.min))
            link(dve.tensor_scalar(sched[:, S_PAIR:S_PAIR + PASSES], e_int[:, 0:PASSES], 1, None, ALU.arith_shift_right))
            link(dve.tensor_scalar(sched[:, S_ODD:S_ODD + PASSES], e_int[:, 0:PASSES], 1, None, ALU.bitwise_and))
            link(dve.tensor_copy(sched[:, S_END:S_END + EXPERTS], p_end))
            dve.wait_ge(moe["table"], 32)
            half = const[:, K_HALF:K_HALF + 1]
            link(dve.tensor_scalar(gather_row[:, :], tbl[:, :, 0], half, None, ALU.add))
            link(dve.tensor_scalar(scatter_row[:, :], tbl[:, :, 1], half, None, ALU.add))
            dve.tensor_copy(row_weight[:, :], tbl[:, :, 2]).then_inc(moe["tables"], 1)
            dve.wait_ge(moe["tables"], 1)

            def pass_(n, b):
                dve.wait_ge(moe["act"], n + 1)
                dve.tensor_tensor(h_sg[b], h_sg[b], psum[:, 2 + b, 256:512], ALU.mult).then_inc(moe["prod"], 1)
                dve.wait_ge(moe["h_t"], n + 1)
                dve.tensor_copy(heT[b], psum[:, 4 + b, 0:256].rearrange("p (c m) -> p c m", m=P)).then_inc(moe["h"], 1)
                dve.wait_ge(moe["pass"], n + 2)
                if not isinstance(n, int) or n >= 2:
                    dve.wait_ge(scattered[b], (n - b) * 8)
                w = row_weight[:, n:n + 1] if isinstance(n, int) else row_weight[:, bass.ds(n, 1)]
                dve.tensor_scalar(y_row[b], psum[:, 6 + b, :], w, None, ALU.mult).then_inc(moe["y"], 1)

            for b in range(2):
                pass_(b, b)
            total = dve.value_load(sched[0:1, S_END + EXPERTS - 1:S_END + EXPERTS], min_val=1, max_val=PASSES)
            with dve.Fori(1, PASSES // 2) as i:
                with dve.If(i * 2 < total):
                    for b in range(2):
                        pass_(2 * i + b, b)
            dve.wait_ge(moe["y_in"], 16)
            for t in range(TT):
                dve.tensor_tensor(y_sum[:, t, :], y_tok[:, t, 0, :], y_tok[:, t, 1, :], ALU.add).then_inc(moe["sums"], 1)
            for k in range(KT):
                dve.wait_ge(moe["sum_t"], k + 1)
                dve.tensor_tensor(xT[:, k, :], xT[:, k, :], psum[:, k, :], ALU.add).then_inc(x_r, 1)

        def pool_moe(pool):
            pool.wait_ge(s_r, HEADS_SG)
            pool.wait_ge(lo_r, 2 * KT)
            pool.memset(ar1[:, 24576:25600], 0.0).then_inc(idx_r, 1)
            pool.wait_ge(idx_r, 1)
            pool.memset(init_row[:, :, 0:2], BIG).then_inc(idx_r, 1)
            pool.wait_ge(idx_r, 2)
            pool.dma_start(table[:, :].rearrange("(p r) f -> p (r f)", r=25), init_row[:, 0:25, :].rearrange(
                "p r f -> p (r f)")).then_inc(moe["table_init"], 16)
            pool.wait_ge(moe["table_init"], 16)
            pool.wait_ge(moe["pos"], 1)
            for t in range(TT):
                for j in range(TOP):
                    pool.indirect_dma_start(
                        table[:, :], bass.IndirectOffsetOnAxis(ap=pos[:, t, j:j + 1], axis=0), pay[:, t, j, :], None,
                        bounds_check=(PASSES + 2) * CAP - 1, oob_is_err=False).then_inc(moe["placed"], 16)
            pool.wait_ge(moe["tables"], 1)
            pool.wait_ge(moe["h_dram"], 16 * TT)

            def gather(n, b):
                if not isinstance(n, int) or n >= 2:
                    pool.wait_ge(moe["x_t"], n - 1 + TT)
                g = gather_row[:, n:n + 1] if isinstance(n, int) else gather_row[:, bass.ds(n, 1)]
                pool.tensor_copy(g_cur[b][:, :], g).then_inc(idx_r, 1)
                first = isinstance(n, int) and n < 2
                pool.wait_ge(idx_r, 3 + n if first else 2 * n + 1)
                pool.sem_inc(moe["begun"], 1)
                pool.indirect_dma_start(xg[b], None, h_dram[:, :], bass.IndirectOffsetOnAxis(ap=g_cur[b][:, 0:1], axis=0),
                                        bounds_check=2 * T - 1, oob_is_err=False).then_inc(gathered[b], 16)

            def scatter(n, b):
                s = scatter_row[:, n:n + 1] if isinstance(n, int) else scatter_row[:, bass.ds(n, 1)]
                if not isinstance(n, int) or n >= 2:
                    pool.wait_ge(scattered[b], (n - b) * 8)
                pool.tensor_copy(s_cur[b][:, :], s).then_inc(idx_r, 1)
                pool.wait_ge(idx_r, 2 * n + 6)
                pool.wait_ge(moe["y"], n + 1)
                pool.sem_inc(moe["begun"], 1)
                pool.indirect_dma_start(y_dram[:, :], bass.IndirectOffsetOnAxis(ap=s_cur[b][:, 0:1], axis=0), y_row[b], None,
                                        bounds_check=2 * TOP * T - 1, oob_is_err=False).then_inc(scattered[b], 16)

            gather(0, 0)
            gather(1, 1)

            def two(i):
                for b in range(2):
                    gather(2 * i + 2 + b, b)
                    scatter(2 * i + b, b)

            two(0)
            total = pool.value_load(sched[0:1, S_END + EXPERTS - 1:S_END + EXPERTS], min_val=1, max_val=PASSES)
            with pool.Fori(1, PASSES // 2) as i:
                with pool.If(i * 2 < total):
                    two(i)
            written = (total + 1) // 2 * 16
            landed = written + 16
            for b in range(2):
                pool.wait_ge(scattered[b], written)
                pool.wait_ge(gathered[b], landed)
            pool.sem_inc(moe["done"], 1)

        fgate_r = sem("ffn_gate_ready")
        fhi_r = sem("ffn_hi_ready")
        flo_r = sem("ffn_lo_ready")
        hF2 = tiles(ar3[:, 0:4096])
        hF_mix = tiles(ar3[:, 18688:22784])

        def sp_ffn(sp, j):
            gate = A[f"w{j + 1}_gate_2"].rearrange("o (k p) n -> p (o k) n", p=P)
            up = A[f"w{j + 1}_up_2"].rearrange("o (k p) n -> p (o k) n", p=P)
            down = A[f"w{j + 1}_down_2"].rearrange("o (k p) n -> p (o k) n", p=P)
            H = CN // 2

            def load_group(g, i=0):
                c = (g + 2 * i) * H
                cols = slice(c, c + H) if isinstance(c, int) else bass.ds(c, H)
                for k in range(4):
                    load_chunk(sp, C_UP[j] + 4 * g + k + 8 * i, (C_UP[j] + k) % RAW, gate[:, 2 * k:2 * k + 2, cols],
                               up[:, 2 * k:2 * k + 2, cols])

            with sp.Fori(0, N_UP // 2) as i:
                for g in range(2):
                    load_group(g, i)
            load_group(N_UP - 1)

            def load_down(kp, i=0):
                r = 2 * kp + 4 * i
                rows = slice(r, r + 2) if isinstance(r, int) else bass.ds(r, 2)
                for half in range(2):
                    load_chunk(sp, C_DN[j] + 2 * kp + half + 4 * i, (C_DN[j] + 2 * kp + half) % RAW,
                               down[:, rows, half * CN:half * CN + CN])

            with sp.Fori(0, N_UP // 2) as i:
                for kp in range(2):
                    load_down(kp, i)
            load_down(N_UP - 1)

        def pe_ffn(pe, j):
            mul_groups(pe, C_UP[j], G_UP[j], N_UP, hhi, hlo)
            group_read(pe, G_DN[j] - 2)

            def down(kp, i=0):
                pe.wait_ge(flo_r, N_UP * j + kp + 1 + 2 * i)
                for half in range(2):
                    if kp == 0 and half == 1:
                        group_read(pe, G_DN[j] - 1)
                    c0, g = C_DN[j] + 2 * kp + half, G_DN[j] + half
                    s = c0 % SPLIT
                    pe.wait_ge(w_lo, c0 + 1 + 4 * i)
                    for a in range(CK):
                        kt = 2 * kp + a + 4 * i
                        if isinstance(kt, int):
                            x_h, x_l = ahi[:, kt, :], alo[:, kt, :]
                        else:
                            x_h = ahi[:, bass.ds(kt, 1), :].rearrange("p o n -> p (o n)")
                            x_l = alo[:, bass.ds(kt, 1), :].rearrange("p o n -> p (o n)")
                        for m in range(4):
                            f = slice(m * P, m * P + P)
                            mm = mm3(pe, bank(g, m), whi[:, s, a, f], wlo[:, s, a, f], x_h, x_l,
                                     kp == 0 and a == 0, kp == N_UP - 1 and a == CK - 1)
                    mm.then_inc(w_used, 1)

            down(0)
            with pe.Fori(0, (N_UP - 3) // 2) as i:
                for kp in (1, 2):
                    down(kp, i)
            down(N_UP - 2)
            down(N_UP - 1)

        def act_ffn(act, j):
            def gate(g, i=0):
                act.wait_ge(w_used, C_UP[j] + 4 * g + 4 + 8 * i)
                if g >= 2 or not isinstance(i, int):
                    act.wait_ge(flo_r, N_UP * j + g - 1 + 2 * i)
                b = 4 * ((G_UP[j] + g) % 2)
                act.activation(gated[:, g % 2, :, :], psum[:, b:b + 2, :], ACT.Silu).then_inc(fgate_r, 1)

            def group(g, i=0, step=0):
                for k in range(4):
                    if k == 2 and g:
                        gate(g - 1, i)
                    split_hi(act, C_UP[j] + 4 * g, k, i, step, up=4 * N_UP * j + 4 * g + k)

            for g in range(3):
                group(g)
            with act.Fori(1, (N_UP - 1) // 2) as i:
                for g in (1, 2):
                    group(g, i, 8)
            for k in range(2):
                split_hi(act, C_DN[j], k)
            gate(N_UP - 1)
            with act.Fori(0, (N_UP - 1) // 2) as i:
                for k in range(4):
                    split_hi(act, C_DN[j] + 2, k, i, 4)

        def dve_ffn(dve, j):
            def products(g, i=0):
                dve.wait_ge(fgate_r, N_UP * j + g + 1 + 2 * i)
                b = 4 * ((G_UP[j] + g) % 2) + 2
                dve.tensor_tensor(gated[:, g % 2, :, :], gated[:, g % 2, :, :], psum[:, b:b + 2, :],
                                  ALU.mult).then_inc(evac[g % 2], 1)

            def pair(g, i):
                kt = 2 * g + 4 * i
                return slice(kt, kt + 2) if isinstance(kt, int) else bass.ds(kt, 2)

            def products_hi(g, i=0):
                dve.wait_ge(evac[g % 2], (G_UP[j] + g) // 2 + 1 + i)
                dve.tensor_scalar(ahi[:, pair(g, i), :], gated[:, g % 2, :, :], 1.0, None, ALU.mult).then_inc(fhi_r, 1)

            def products_lo(g, i=0):
                dve.wait_ge(fhi_r, N_UP * j + g + 1 + 2 * i)
                dve.tensor_tensor(alo[:, pair(g, i), :], gated[:, g % 2, :, :], ahi[:, pair(g, i), :].bitcast(F32),
                                  ALU.subtract).then_inc(flo_r, 1)

            def group(g, i=0, step=0):
                for k in range(4):
                    split_lo(dve, C_UP[j] + 4 * g, k, i, step)
                    if g and k == 1:
                        products(g - 1, i)
                    if g and k == 2:
                        products_hi(g - 1, i)
                if g:
                    products_lo(g - 1, i)

            for g in range(3):
                group(g)
            with dve.Fori(1, (N_UP - 1) // 2) as i:
                for g in (1, 2):
                    group(g, i, 8)
            split_lo(dve, C_DN[j], 0)
            split_lo(dve, C_DN[j], 1)
            products(N_UP - 1)
            products_hi(N_UP - 1)
            products_lo(N_UP - 1)
            with dve.Fori(0, (N_UP - 1) // 2) as i:
                for k in range(4):
                    split_lo(dve, C_DN[j] + 2, k, i, 4)
            for half in range(2):
                g = G_DN[j] + half
                dve.wait_ge(w_used, C_DN[j] + 2 * (N_UP - 1) + half + 1)
                for m in range(4):
                    k = 4 * half + m
                    ins = dve.scalar_tensor_tensor(out=xT[:, k, :], in0=bank(g, m), scalar=0.5, in1=xT[:, k, :],
                                                   op0=ALU.mult, op1=ALU.add)
                ins.then_inc(evac[g % 2], 1)

        def pe_between(pe):
            sum_squares(pe, 0)
            sum_squares(pe, 0)
            pe.wait_ge(lo_r, 5 * KT)
            pe_ffn(pe, 0)

        def act_between(act):
            squares(act, xT, lambda k: act.wait_ge(x_r, 2 * KT + k + 1))
            root(act, 0)
            squares(act, xT, lambda k: act.wait_ge(h_r, 2 * KT + k + 1))
            root(act, 0)
            high_parts(act, hF2, h_r, 3 * KT)
            act_ffn(act, 0)

        def dve_between(dve):
            inverse(dve)
            scale_rows(dve, xT, xT, "norm_final_g", h_r)
            inverse(dve)
            scale_rows(dve, hF2, xT, "g_ffn1_2", h_r)
            low_parts(dve, hF2)
            dve_ffn(dve, 0)

        mx = {n: sem("mix_" + n) for n in (
            "w_uq_in", "w_ukv_in", "k_zero", "rot", "rot_read", "cos", "rope", "kv_t", "kv_tok", "idx", "relu", "acc",
            "lat", "q", "q_raw", "q_rot", "q_rot_read", "q_cos", "q_rope", "k_nope", "k_nope_in", "k_pe", "v", "v_in",
            "best", "marked", "hi", "lo")}
        at_ = {n: sem("att_" + n) for n in ("score", "score_read", "max", "exp", "inverse", "p_pool", "p_act", "p_dve", "p_t", "p_t_in", "out")}
        kv_cols = [sem(f"mix_columns_in{k}") for k in range(4)]

        qa = tiles(ar3[:, 0:2048])
        mixb = tiles(ar3[:, 2048:6144])
        KA, KI, KV, CKV, CQ = 0, 1, 2, 3, 5
        kz = tiles(ar3[:, 6144:8192])
        w_uq = ar3[:, 8192:10496].rearrange("p (k n) -> p k n", k=3)
        w_ukv = ar3[:, 10496:12544].rearrange("p (k n) -> p k n", k=2)
        kB = tiles(ar3[:, 12544:16640])
        vB = tiles(ar3[:, 16640:18688])
        qi = tiles(ar3[:, 18688:22784])
        qB = qi
        sc_at = {1: 22784, 2: 23040, 3: 23424}
        sc = {b: ar3[:, o:o + P * (b + 1)] for b, o in sc_at.items()}
        pr = tiles(ar3[:, 23936:25472])
        p_buf = [pr[:, 0, :], pr[:, 1, :], pr[:, 2, :], mixb[:, KI, :]] + [mixb[:, CQ + k, :] for k in range(3)]
        pT_buf = [sq[:, 0, :], sq[:, 1, :], mixb[:, CKV, :], mixb[:, CKV + 1, :]]
        NP, NT = len(p_buf), len(pT_buf)
        neg_max, p_sum, p_inv = (stat_mean[:, o:o + NP] for o in (32, 48, 64))
        wi_tok = ar3[:, 25472:25536].rearrange("p (t h) -> p t h", h=HI)
        kv_tok = ar3[:, 2048:2560].rearrange("p (t f) -> p t f", f=P)
        best = stat_mean[:, 0:24].rearrange("p (b e) -> p b e", e=8)
        ropes = [(mixb[:, KI, :], "A", (2, 3)), (mixb[:, KA, :], "A", (0, 1)), (mixb[:, KV, :], "B", None)]
        ropes += [(qi[:, k, :], "A", None) for k in range(8)] + [(qa[:, k, :], "A", None) for k in range(4)]
        R_KI, R_KA, R_KV, R_QI, R_QA = 1, 2, 3, 3, 11
        rot_of = {"A": const[:, K_RA:K_RA + P], "B": const[:, K_RB:K_RB + P]}
        cos_of = {"A": const[:, K_CA:K_CA + T], "B": const[:, K_CBT:K_CBT + T]}
        sin_of = {"A": const[:, K_SA:K_SA + T], "B": const[:, K_SB:K_SB + T]}
        HQ = NOPE + ROPE
        pe_rows = slice(NOPE, HQ)
        idx_units = [(h, b) for h in range(HI) for b in (3, 2, 1)]
        units = [("B", 2 * q + j, b) for q in range(HB // 2) for b in range(TT) for j in range(2)]
        units += [("A", h, b) for b in range(TT) for h in range(HA)]
        NB = HB * TT
        ROUNDS = TOPK // 8
        EARLY, MID = 2, 8

        def sp_mix(sp):
            wv = A["w_in_2"].rearrange("o (k p) n -> p (o k) n", p=P)

            def cols(k, dst, src, n, s):
                slot = (C_MIX + k) % RAW
                sp.dma_start(raw[:, slot, :, dst:dst + n], wv[:, 2 * (k % 4):2 * (k % 4) + 2, src:src + n]).then_inc(s, 16)

            for g, c in enumerate((C_QA, C_QI, C_QI + CN)):
                for k in range(4):
                    load_chunk(sp, C_MIX + 4 * g + k, (C_MIX + k) % RAW, wv[:, 2 * k:2 * k + 2, c:c + CN])
            with nc.allow_non_contiguous_dma(reason="narrow columns"):
                for k in range(12, 16):
                    sp.wait_ge(w_lo, C_MIX + k - RAW + 1)
                    cols(k, 0, C_KA, 64, w_raw[(C_MIX + k) % RAW])
                    for dst, src, n in ((64, C_KA, 64), (128, C_KI, 64), (192, C_KI, 64), (256, C_VA, 64),
                                        (320, C_KR, ROPE), (352, C_WI, HI), (368, C_WI, HI), (384, C_CKV, P)):
                        cols(k, dst, src, n, kv_cols[k % 4])
            for k in range(16, 20):
                sp.wait_ge(w_lo, C_MIX + k - RAW + 1)
                cols(k, 0, C_CKV + P, P, w_raw[(C_MIX + k) % RAW])
                cols(k, P, C_CQ, QL, kv_cols[k % 4])
            sp.wait_ge(w_used, C_MIX)
            sp.dma_start(w_uq, A["w_uq_2"].rearrange("o (k p) n -> p (o k) n", p=P)).then_inc(mx["w_uq_in"], 16)
            sp.dma_start(w_ukv, A["w_ukv_2"].rearrange("o (k p) n -> p (o k) n", p=P)).then_inc(mx["w_ukv_in"], 16)
            wo = A["w_out_2"].rearrange("o (k p) n -> p (o k) n", p=P)
            for g in range(2):
                for k in range(4):
                    load_chunk(sp, C_MO + 4 * g + k, (C_MO + k) % RAW, wo[:, 2 * k:2 * k + 2, CN * g:CN * g + CN])

        def scores(pe, u):
            kind, h, b = units[u]
            S = P * (b + 1)
            if u == 0:
                pe.wait_ge(mx["v_in"], TT)
                pe.wait_ge(mx["q_rot_read"], HB)
                pe.wait_ge(mx["k_pe"], HB)
            if kind == "B" and b == 0:
                pe.wait_ge(mx["q_rope"], h + 1)
            if u >= 2:
                pe.wait_ge(at_["score_read"], u - 1)
            if kind == "B":
                lhs, rhs = qB[0:HQ, h, b * P:b * P + P], kB[0:HQ, h, 0:S]
            else:
                lhs, rhs = qa[:, h // 2, b * P:b * P + P], kz[:, h % 2, 0:S]
            pe.matmul(psum[:, u % 2, 0:S], lhs, rhs, start=True, stop=True).then_inc(at_["score"], 1)

        def p_done(u):
            if u % 2 == 0:
                return at_["p_pool"], u // 2 + 1
            return (at_["p_act"], u // 2 + 1) if u < NB else (at_["p_dve"], (u - NB) // 2 + 1)

        def turn_p(pe, u):
            b = units[u][2]
            s, n = p_done(u)
            pe.wait_ge(s, n)
            if u >= 2:
                pe.wait_ge(at_["p_t_in"], u - 1)
            for t in range(b + 1):
                mm = pe.transpose(psum[:, 2 + u % 2, t * P:t * P + P], p_buf[u % NP][:, t * P:t * P + P], ident)
            mm.then_inc(at_["p_t"], 1)

        def weigh(pe, u):
            kind, h, b = units[u]
            if u == NB:
                pe.wait_ge(mx["lo"], 1)
            pe.wait_ge(at_["p_t_in"], u + 2)
            for t in range(b + 1):
                for j in range(2):
                    o = j * 64
                    lhs = vB[:, t, (h + j) * VB:(h + j + 1) * VB] if kind == "B" else kv_tok[:, t, 0:HDA]
                    mm = pe.matmul(psum[o:o + 64, 4 + h // 2, b * P:b * P + P], lhs, pT_buf[(u + j) % NT][:, t * P:t * P + P],
                                   start=(t == 0), stop=(t == b))
            mm.then_inc(at_["out"], 2)

        def pe_mix(pe):
            sum_squares(pe, 7)
            pe.wait_ge(lo_r, 6 * KT)
            mul_groups(pe, C_MIX, G_MIX, N_MIX, hhi, hlo)
            for g in range(N_MIX):
                group_read(pe, G_MIX + g)
            for r, (src, kind, _) in enumerate(ropes):
                if r >= 4:
                    pe.wait_ge(mx["rot_read"], r - 3)
                pe.matmul(psum[:, r % 4, :], rot_of[kind], src, start=True, stop=True).then_inc(mx["rot"], 1)
            pe.wait_ge(mx["rope"], R_KV)
            for t in range(TT):
                mm = pe.transpose(psum[:, 4, t * P:t * P + P], mixb[:, KV, t * P:t * P + P], ident)
            mm.then_inc(mx["kv_t"], 1)
            sum_squares(pe, 5, 3)
            sum_squares(pe, 6, 2)
            pe.wait_ge(mx["rot_read"], len(ropes))
            pe.wait_ge(mx["k_zero"], 4)
            for v_, (h, b) in enumerate(idx_units):
                S = P * (b + 1)
                if b == 3 and h % 2 == 0:
                    pe.wait_ge(mx["rope"], R_QI + h // 2 + 1)
                if v_ >= 4:
                    pe.wait_ge(mx["relu"], v_ - 3)
                pe.matmul(psum[:, v_ % 4, 0:S], qi[:, h // 2, b * P:b * P + P], kz[:, 2 + h % 2, 0:S], start=True,
                          stop=True).then_inc(mx["idx"], 1)
            pe.wait_ge(mx["w_uq_in"], 16)
            pe.wait_ge(mx["lat"], 3)
            pe.wait_ge(mx["kv_tok"], 2)

            def rotate(h):
                pe.wait_ge(mx["q_raw"], h + 1)
                if h >= 2:
                    pe.wait_ge(mx["q_rot_read"], h - 1)
                pe.matmul(psum[0:HQ, 6 + h % 2, :], const[0:HQ, K_RB:K_RB + HQ], qB[0:HQ, h, :], start=True,
                          stop=True).then_inc(mx["q_rot"], 1)

            for h in range(HB):
                if h >= 2:
                    pe.wait_ge(mx["q_raw"], h - 1)
                for k in range(3):
                    mm = pe.matmul(psum[0:HQ, 4 + h % 2, :], w_uq[:, k, h * HQ:h * HQ + HQ], mixb[:, CQ + k, :],
                                   start=(k == 0), stop=(k == 2))
                mm.then_inc(mx["q"], 1)
                if h:
                    rotate(h - 1)
            rotate(HB - 1)
            pe.wait_ge(mx["w_ukv_in"], 16)
            pe.wait_ge(mx["lat"], 5)
            pe.wait_ge(mx["relu"], len(idx_units))
            for h in range(HB):
                if h >= 4:
                    pe.wait_ge(mx["k_nope_in"], h - 3)
                for k in range(2):
                    mm = pe.matmul(psum[0:NOPE, h % 4, :], w_ukv[:, k, h * P:h * P + NOPE], mixb[:, CKV + k, :],
                                   start=(k == 0), stop=(k == 1))
                mm.then_inc(mx["k_nope"], 1)
            for t in range(TT):
                pe.wait_ge(mx["k_nope_in"], 5 + t)
                for k in range(2):
                    wv = w_ukv[:, k, :].rearrange("p (h f) -> p h f", f=P)[:, :, NOPE:P]
                    mm = pe.matmul(psum[:, t, :].rearrange("p (h f) -> p h f", f=VB), mixb[:, CKV + k, t * P:t * P + P],
                                   wv, start=(k == 0), stop=(k == 1))
                mm.then_inc(mx["v"], 1)
            for u in range(len(units) + 6):
                if u < len(units):
                    scores(pe, u)
                if 5 <= u < len(units) + 5:
                    turn_p(pe, u - 5)
                if u >= 7 and u % 2 == 1:
                    weigh(pe, u - 7)
            pe.wait_ge(mx["lo"], 2)
            mul_groups(pe, C_MO, G_MO, 2, hhi, hlo)

        def act_mix(act):
            squares(act, xT, lambda k: group_read(act, G_DN[0] + k // 4))
            root(act, 7)
            high_parts(act, hF_mix, h_r, 4 * KT)
            dsts = [ar3[:, 0:2048], ar3[:, 18688:20736], ar3[:, 20736:22784], ar3[:, 2048:4096], ar3[:, 4096:6144]]

            def read_group(g):
                act.wait_ge(w_used, C_MIX + 4 * g + 4)
                b = 4 * ((G_MIX + g) % 2)
                act.activation(dsts[g], psum[:, b:b + 4, :].rearrange("p b n -> p (b n)"), ACT.Copy).then_inc(
                    evac[(G_MIX + g) % 2], 1)

            for g in range(N_MIX):
                for k in range(4):
                    if k == 2 and g:
                        read_group(g - 1)
                    if g >= 3:
                        act.wait_ge(kv_cols[k], 16 * 8 if g == 3 else 16 * 9)
                    split_hi(act, C_MIX + 4 * g, k)
            for k in range(SPLIT):
                split_hi(act, C_MO, k)
            read_group(N_MIX - 1)
            group_read(act, G_MIX + N_MIX - 1)
            squares(act, mixb[:, CQ:CQ + 3, :], lambda k: None, 3)
            root(act, 5, QL)
            act.wait_ge(mx["kv_t"], 1)
            act.wait_ge(mx["rope"], R_KA)
            kv_ps = psum[:, 4, :].rearrange("p (t f) -> p t f", f=P)
            act.activation(kv_tok, kv_ps, ACT.Copy).then_inc(mx["kv_tok"], 1)
            act.activation(wi_tok, kv_ps[:, :, HQ:HQ + HI], ACT.Copy, scale=float(HI * 64) ** -0.5).then_inc(
                mx["kv_tok"], 1)
            squares(act, mixb[:, CKV:CKV + 2, :], lambda k: None, 2)
            act.wait_ge(mx["lat"], 3)
            root(act, 6, KVL)
            act.wait_ge(mx["rope"], len(ropes))
            for v_, (h, b) in enumerate(idx_units):
                act.wait_ge(mx["idx"], v_ + 1)
                if v_ >= 3:
                    act.wait_ge(mx["acc"], v_ - 2)
                S = P * (b + 1)
                act.activation(pr[:, v_ % 3, 0:S], psum[:, v_ % 4, 0:S], ACT.Relu).then_inc(mx["relu"], 1)
            for h in range(HB):
                act.wait_ge(mx["q"], h + 1)
                act.activation(qB[0:HQ, h, :], psum[0:HQ, 4 + h % 2, :], ACT.Copy).then_inc(mx["q_raw"], 1)
            for h in range(HB):
                act.wait_ge(mx["k_nope"], h + 1)
                act.activation(kB[0:NOPE, h, :], psum[0:NOPE, h % 4, :], ACT.Copy).then_inc(mx["k_nope_in"], 1)
            for t in range(TT):
                act.wait_ge(mx["v"], t + 1)
                act.activation(vB[:, t, :], psum[:, t, :], ACT.Copy).then_inc(mx["v_in"], 1)

            def exp(u):
                b = units[u][2]
                act.wait_ge(at_["max"], u + 1)
                act.activation(p_buf[u % NP][:, 0:P * (b + 1)], p_buf[u % NP][:, 0:P * (b + 1)], ACT.Exp,
                               bias=neg_max[:, u % NP:u % NP + 1], accum_out=p_sum[:, u % NP:u % NP + 1]).then_inc(
                    at_["exp"], 1)

            def divide(u):
                act.wait_ge(at_["inverse"], u + 1)
                part = p_buf[u % NP][:, 0:P * (units[u][2] + 1)]
                act.activation(part, part, ACT.Identity, scale=p_inv[:, u % NP:u % NP + 1]).then_inc(at_["p_act"], 1)

            def p_t(u):
                b = units[u][2]
                act.wait_ge(at_["p_t"], u + 1)
                if u >= NT:
                    act.wait_ge(at_["out"], u - NT + 1)
                act.activation(pT_buf[u % NT][:, 0:P * (b + 1)], psum[:, 2 + u % 2, 0:P * (b + 1)], ACT.Copy).then_inc(
                    at_["p_t_in"], 1)

            def high(n, k):
                act.wait_ge(at_["out"], n)
                act.activation(hhi_[:, k * T:(k + 4) * T], psum[:, 4:8, :].rearrange("p b n -> p (b n)"),
                               ACT.Copy).then_inc(mx["hi"], 1)

            for u in range(len(units) + 5):
                if u >= 5:
                    p_t(u - 5)
                if 1 <= u < len(units) + 1:
                    exp(u - 1)
                if u % 2 == 0 and 4 <= u < NB + 4:
                    divide(u - 3)
                if u == NB + 5:
                    high(NB, 4)
            high(len(units), 0)
            for k in range(SPLIT, 8):
                split_hi(act, C_MO, k)

        def dve_mix(dve):
            inverse(dve)
            scale_rows(dve, hF_mix, xT, "g_mix_2", h_r)
            low_parts(dve, hF_mix)
            for k in range(20):
                split_lo(dve, C_MIX, k)

            def sine(r):
                kind = ropes[r][1]
                dve.wait_ge(mx["rot"], r + 1)
                if r >= 3:
                    dve.wait_ge(mx["rope"], r - 2)
                dve.tensor_tensor(pr[:, r % 3, :], psum[:, r % 4, :], sin_of[kind], ALU.mult).then_inc(mx["rot_read"], 1)

            def rotated(r):
                src, kind, halves = ropes[r]
                dve.wait_ge(mx["rot_read"], r + 1)
                dve.wait_ge(mx["cos"], r + 1)
                if halves is None:
                    dve.tensor_tensor(src, src, pr[:, r % 3, :], ALU.add).then_inc(mx["rope"], 1)
                else:
                    dve.tensor_tensor(kz[0:64, halves[0], :], src[0:64], pr[0:64, r % 3, :], ALU.add)
                    dve.tensor_tensor(kz[64:P, halves[1], :], src[64:P], pr[64:P, r % 3, :], ALU.add).then_inc(
                        mx["rope"], 1)

            for r in range(len(ropes) + 1):
                if r < len(ropes):
                    sine(r)
                if r:
                    rotated(r - 1)
            for k in range(SPLIT):
                split_lo(dve, C_MO, k)
            inverse(dve)
            for k in range(3):
                dve.scalar_tensor_tensor(out=mixb[:, CQ + k, :], in0=mixb[:, CQ + k, :], scalar=col("g_q_lat_2", k),
                                         in1=stat_std[:, :], op0=ALU.mult, op1=ALU.mult).then_inc(mx["lat"], 1)
            inverse(dve)
            for k in range(2):
                dve.scalar_tensor_tensor(out=mixb[:, CKV + k, :], in0=mixb[:, CKV + k, :], scalar=col("g_kv_lat_2", k),
                                         in1=stat_std[:, :], op0=ALU.mult, op1=ALU.mult).then_inc(mx["lat"], 1)
            dve.wait_ge(mx["kv_tok"], 2)
            for v_, (h, b) in enumerate(idx_units):
                dve.wait_ge(mx["relu"], v_ + 1)
                part, w = pr[:, v_ % 3, 0:P * (b + 1)], wi_tok[:, b, h:h + 1]
                if h == 0:
                    dve.tensor_scalar(sc[b], part, w, None, ALU.mult).then_inc(mx["acc"], 1)
                else:
                    dve.wait_ge(mx["acc"], v_ - 2)
                    dve.scalar_tensor_tensor(out=sc[b], in0=part, scalar=w, in1=sc[b], op0=ALU.mult,
                                             op1=ALU.add).then_inc(mx["acc"], 1)
            triangle = const[:, K_CB + 384:K_CB + 512]
            dve.wait_ge(mx["acc"], len(idx_units))
            for b in (1, 2, 3):
                dlink(dve, dve.tensor_tensor(sc[b][:, b * P:b * P + P], sc[b][:, b * P:b * P + P], triangle, ALU.add))

            def choose(r):
                for b in (1, 2, 3):
                    dve.max(best[:, b - 1, :], sc[b]).then_inc(mx["best"], 1)
                for b in (1, 2, 3):
                    dve.wait_ge(mx["best"], 3 * r + b)
                    dve.match_replace(sc[b], best[:, b - 1, :], sc[b], MARK).then_inc(mx["marked"], 1)
                dve.wait_ge(mx["marked"], 3 * r + 3)
                if r == ROUNDS - 1:
                    for b in (1, 2, 3):
                        dlink(dve, dve.tensor_scalar(sc[b], sc[b], MARK, NEG, ALU.not_equal, ALU.mult))

            done = 0

            def choose_to(n):
                nonlocal done
                while done < n:
                    choose(done)
                    done += 1

            choose_to(EARLY)
            for h in range(HB):
                dve.wait_ge(mx["q_rot"], h + 1)
                if h >= 3:
                    dve.wait_ge(mx["q_rope"], h - 2)
                dve.tensor_tensor(pr[pe_rows, h % 3, :], psum[pe_rows, 6 + h % 2, :], sin_of["B"][pe_rows],
                                  ALU.mult).then_inc(mx["q_rot_read"], 1)
                dve.wait_ge(mx["q_rot_read"], h + 1)
                dve.wait_ge(mx["q_cos"], h + 1)
                dve.tensor_tensor(qB[pe_rows, h, :], qB[pe_rows, h, :], pr[pe_rows, h % 3, :], ALU.add).then_inc(
                    mx["q_rope"], 1)
                choose_to(EARLY + (h + 1) * MID // HB)
            dve.wait_ge(mx["q_rope"], HB)

            def softmax_in(u):
                kind, h, b = units[u]
                S = P * (b + 1)
                if kind == "B":
                    bias, scale = const[:, K_CB + 384 - P * b:K_CB + 512], float(HQ) ** -0.5
                else:
                    bias, scale = triangle if b == 0 else sc[b], float(HDA) ** -0.5
                dve.wait_ge(at_["score"], u + 1)
                if u >= NP:
                    dve.wait_ge(at_["p_t"], u - NP + 1)
                dve.scalar_tensor_tensor(out=p_buf[u % NP][:, 0:S], in0=psum[:, u % 2, 0:S], scalar=scale, in1=bias,
                                         op0=ALU.mult, op1=ALU.add).then_inc(at_["score_read"], 1)

            def maximum(u):
                S = P * (units[u][2] + 1)
                dve.wait_ge(at_["score_read"], u + 1)
                dve.tensor_reduce(neg_max[:, u % NP:u % NP + 1], p_buf[u % NP][:, 0:S], AX.X, ALU.max,
                                  negate=True).then_inc(at_["max"], 1)

            def low(k, n):
                dve.wait_ge(mx["hi"], n)
                part = slice(k * T, (k + 4) * T)
                dve.tensor_tensor(hlo_[:, part], psum[:, 4:8, :].rearrange("p b n -> p (b n)"), hhi_[:, part].bitcast(F32),
                                  ALU.subtract).then_inc(mx["lo"], 1)

            def invert(u):
                dve.wait_ge(at_["exp"], u + 1)
                dve.reciprocal(p_inv[:, u % NP:u % NP + 1], p_sum[:, u % NP:u % NP + 1]).then_inc(at_["inverse"], 1)

            def divide(u):
                dve.wait_ge(at_["inverse"], u + 1)
                part = p_buf[u % NP][:, 0:P * (units[u][2] + 1)]
                dve.tensor_scalar(part, part, p_inv[:, u % NP:u % NP + 1], None, ALU.mult).then_inc(at_["p_dve"], 1)

            choose_to(ROUNDS)
            for u in range(len(units) + 3):
                if 1 <= u < len(units) + 1:
                    maximum(u - 1)
                if u < len(units):
                    softmax_in(u)
                if 2 <= u < len(units) + 2:
                    invert(u - 2)
                if u % 2 == 0 and u >= NB + 4:
                    divide(u - 3)
                if u == NB + 5:
                    low(4, 1)
            low(0, 2)
            for g in (G_MO, G_MO + 1):
                for k in range(2, 6) if g == G_MO else range(6, 8):
                    split_lo(dve, C_MO, k)
                dve.wait_ge(w_used, C_MO + 4 * (g - G_MO) + 4)
                for m in range(4):
                    k = 4 * (g - G_MO) + m
                    ins = dve.tensor_tensor(xT[:, k, :], bank(g, m), xT[:, k, :], ALU.add)
                ins.then_inc(evac[g % 2], 1)

        def pool_mix(pool):
            pool.wait_ge(tables_in, 16)
            pool.wait_ge(w_used, C_MIX)
            for n in range(4):
                if n:
                    pool.wait_ge(mx["k_zero"], n)
                pool.memset(kz[64:P, n, :] if n % 2 == 0 else kz[0:64, n, :], 0.0).then_inc(mx["k_zero"], 1)
            pool.wait_ge(mx["k_zero"], 4)
            for r, (src, kind, _) in enumerate(ropes):
                pool.wait_ge(mx["rot"], r + 1)
                pool.tensor_tensor(src, src, cos_of[kind], ALU.mult).then_inc(mx["cos"], 1)
            pool.wait_ge(mx["rope"], R_KV)
            pool.wait_ge(mx["cos"], len(ropes))
            for h in range(HB):
                pool.tensor_copy(kB[pe_rows, h, :], mixb[pe_rows, KV, :]).then_inc(mx["k_pe"], 1)
            for h in range(HB):
                pool.wait_ge(mx["q_rot"], h + 1)
                pool.tensor_tensor(qB[pe_rows, h, :], qB[pe_rows, h, :], cos_of["B"][pe_rows], ALU.mult).then_inc(
                    mx["q_cos"], 1)
            pool.wait_ge(mx["q_cos"], HB)
            for u in range(0, len(units), 2):
                b = units[u][2]
                pool.wait_ge(at_["inverse"], u + 1)
                p_u = p_buf[u % NP][:, 0:P * (b + 1)]
                pool.tensor_scalar(p_u, p_u, p_inv[:, u % NP:u % NP + 1], None, ALU.mult).then_inc(at_["p_pool"], 1)

        o_r = sem("out_transposed")
        o_in = sem("out_on_tokens")
        stored = sem("out_stored")
        o_tok = ar3[:, 0:4096].rearrange("p (t d) -> p t d", d=D)

        def sp_last(sp):
            sp_ffn(sp, 1)
            for t in range(TT):
                sp.wait_ge(o_in, t + 1)
                sp.dma_start(out[0, t * P:t * P + P, :], o_tok[:, t, :]).then_inc(stored, 16)
            sp.wait_ge(stored, 16 * TT)

        def pe_last(pe):
            sum_squares(pe, 0)
            pe.wait_ge(lo_r, 7 * KT)
            pe_ffn(pe, 1)
            sum_squares(pe, 7)
            for t in range(TT):
                for k in range(KT):
                    pe.wait_ge(h_r, 6 * KT + k + 1)
                    if t == 3:
                        pe.wait_ge(o_in, 1)
                    mm = pe.transpose(psum[:, 2 * (t % 3) + k // 4, (k % 4) * P:(k % 4 + 1) * P],
                                      xT[:, k, t * P:t * P + P], ident)
                mm.then_inc(o_r, 1)

        def act_last(act):
            squares(act, xT, lambda k: group_read(act, G_MO + k // 4))
            root(act, 0)
            high_parts(act, hF2, h_r, 5 * KT)
            act_ffn(act, 1)
            squares(act, xT, lambda k: group_read(act, G_DN[1] + k // 4))
            root(act, 7)
            for t in range(TT):
                act.wait_ge(o_r, t + 1)
                act.activation(o_tok[:, t, :], psum[:, 2 * (t % 3):2 * (t % 3) + 2, :].rearrange("p b n -> p (b n)"),
                               ACT.Copy).then_inc(o_in, 1)

        def dve_last(dve):
            inverse(dve)
            scale_rows(dve, hF2, xT, "g_ffn2_2", h_r)
            low_parts(dve, hF2)
            dve_ffn(dve, 1)
            inverse(dve)
            scale_rows(dve, xT, xT, "g_final_2", h_r)

        block = ctx.enter_context(nc.Block())

        @block.sync
        def _(sp):
            sp_router(sp)
            sp_block1(sp)
            sp_moe(sp)
            sp_ffn(sp, 0)
            sp_mix(sp)
            sp_last(sp)

        @block.gpsimd
        def _(pool):
            pool_block1(pool)
            pool_moe(pool)
            pool_mix(pool)

        @block.tensor
        def _(pe):
            pe_block1(pe)
            pe_moe(pe)
            pe_between(pe)
            pe_mix(pe)
            pe_last(pe)

        @block.scalar
        def _(act):
            act_block1(act)
            act_moe(act)
            act_between(act)
            act_mix(act)
            act_last(act)

        @block.vector
        def _(dve):
            dve_block1(dve)
            dve_moe(dve)
            dve_between(dve)
            dve_mix(dve)
            dve_last(dve)


_INS = [
    "x", "norm_mix_g", "w_in", "b_in", "conv_w", "conv_b", "conv_ln_g", "conv_ln_b", "w_conv_out", "b_conv_out",
    "sg_ln_g", "sg_ln_b", "w_sg", "b_sg", "w_sg_out", "b_sg_out", "w_out", "b_out", "norm_ffn_g", "w_router_group",
    "b_router_group", "w_router_expert", "b_router_expert", "w_expert_gate", "w_expert_up", "w_expert_down",
    "norm_final_g", "g_ffn1_2", "w1_gate_2", "w1_up_2", "w1_down_2", "g_mix_2", "w_in_2", "g_q_lat_2",
    "g_kv_lat_2", "w_uq_2", "w_ukv_2", "w_out_2", "g_ffn2_2", "w2_gate_2", "w2_up_2", "w2_down_2", "g_final_2",
]
_OUTS = [((1, T, D), "float32")]


def kernel(**inputs):
    import concourse.bacc as _bacc
    from concourse.bass_utils import run_bass_kernel_spmd as _run

    nc = _bacc.Bacc("TRN2", target_bir_lowering=False, num_devices=1)
    arrays, args = {}, {}
    for name, a in [(n, inputs[n]) for n in _INS] + [("consts", constants())]:
        a = np.ascontiguousarray(a)
        arrays[f"in_{name}_dram"] = a
        args[name] = nc.dram_tensor(f"in_{name}_dram", a.shape, mybir.dt.from_np(a.dtype), kind="ExternalInput").ap()
    (shape, dtype), = _OUTS
    out = nc.dram_tensor("out_0_dram", shape, mybir.dt.from_np(np.dtype(dtype)), kind="ExternalOutput").ap()
    program(nc, args, out)
    r = _run(nc, [arrays], core_ids=[0])
    return r.results[0]["out_0_dram"]
```

```python
from contextlib import ExitStack

import numpy as np

import concourse.bass as bass
from concourse import mybir

P = 128
T = 512
TT = T // P
D = 1024
KT = D // P
EPS = 1e-6
CONV_W = 31
PAD = CONV_W - 1
HEADS_SG = 8
DVE_CONV = 6
N_OWN = D // P - DVE_CONV
SG_CHUNK = 64
GROUPS, PER_GROUP = 4, 8
EXPERTS = GROUPS * PER_GROUP
D_EXP = 512
TOP = 2
CAP, CAP_BITS = 64, 6
PASSES = (TOP * T) // CAP + EXPERTS
FF = 2816
FT = FF // P
HALF = D // 2
BIG = 1.0e5
NEG = -1.0e30
FAR = -3.0e38
MARK = -3.3e38
HA, HDA, HI, HB = 8, 64, 16, 8
NOPE, ROPE, VB = 64, 32, 64
QL, KVL = 384, 256
C_QA, C_KA, C_VA, C_QI = 0, 512, 576, 640
C_KI, C_WI, C_CQ, C_CKV, C_KR = 1664, 1728, 1744, 2128, 2384
TOPK = 128

RAW, SPLIT = 4, 2
CK, CN = 2, 512

F32 = mybir.dt.float32
F32R = mybir.dt.float32r
I32 = mybir.dt.int32
ALU = mybir.AluOpType
ACT = mybir.ActivationFunctionType
AX = mybir.AxisListType

C_IN, G_IN, N_IN = 0, 0, 12
C_SGO, G_SGO = 48, 12
C_CVO, G_CVO = 56, 14
C_WO, G_WO = 64, 16
C_UP = [72, 166]
G_UP = [18, 38]
N_UP = 11
C_DN = [116, 210]
G_DN = [29, 49]
C_MIX, G_MIX, N_MIX = 138, 31, 5
C_MO, G_MO = 158, 36

K_ID, K_ONE, K_UP, K_RA, K_RB = 0, 128, 256, 384, 512
K_CB = 640
K_IOTA = 1152
K_TOK = 1216
K_HALF = 1220
K_CA = 1224
K_SA, K_CBT, K_SB = K_CA + T, K_CA + 2 * T, K_CA + 3 * T
K_N = K_CA + 4 * T


def constants():
    c = np.zeros((P, K_N), np.float32)
    p = np.arange(P)
    c[:, K_ID:K_ID + P] = np.eye(P)
    c[:, K_ONE:K_ONE + P] = 1
    c[:, K_UP:K_UP + P] = p[:, None] < p[None, :]

    def rotation(starts, half):
        m = np.zeros((P, P), np.float32)
        for s in starts:
            for j in range(half):
                m[s + half + j, s + j] = -1
                m[s + j, s + half + j] = 1
        return m

    c[:, K_RA:K_RA + P] = rotation((0, HDA), HDA // 2)
    c[:, K_RB:K_RB + P] = rotation((NOPE,), ROPE // 2)
    c[:, K_CB + 384:K_CB + 512] = np.where(p[None, :] <= p[:, None], 0, NEG)
    c[:, K_IOTA:K_IOTA + 64] = np.arange(64)
    c[:, K_TOK:K_TOK + TT] = p[:, None] + P * np.arange(TT)
    c[:, K_HALF] = p // CAP

    def angles(dim):
        inv = np.float32(10000.0) ** (-np.arange(0, dim, 2, dtype=np.float32) / np.float32(dim))
        return np.arange(T, dtype=np.float32)[None, :] * inv.astype(np.float32)[:, None]

    a = angles(HDA)[p % (HDA // 2)]
    c[:, K_CA:K_CA + T], c[:, K_SA:K_SA + T] = np.cos(a), np.sin(a)
    b = angles(ROPE)[p % (ROPE // 2)]
    rope = ((p >= NOPE) & (p < NOPE + ROPE))[:, None]
    c[:, K_CBT:K_CBT + T] = np.where(rope, np.cos(b), 1)
    c[:, K_SB:K_SB + T] = np.where(rope, np.sin(b), 0)
    return c


def program(nc, A, out):
    with ExitStack() as ctx:
        def sb(name, n, dt=F32):
            return ctx.enter_context(nc.sbuf_tensor(name, [P, n], dt))

        def sem(name):
            return ctx.enter_context(nc.semaphore(name))

        const = sb("const", K_N)
        xT_ = sb("xT", KT * T)
        raw_ = sb("w_raw", RAW * CK * CN)
        whi_ = sb("w_hi", SPLIT * CK * CN, F32R)
        wlo_ = sb("w_lo", SPLIT * CK * CN, F32R)
        stat_mean = sb("stat_mean", T)
        stat_std = sb("stat_std", T)
        eps_t = sb("eps", 1)
        eps_col = eps_t[:, 0:1]
        sq_ = sb("sq", 2 * T)
        vec = sb("vec", 432)

        def tiles(t, n=T):
            return t[:, :].rearrange("p (k n) -> p k n", n=n)

        xT, sq = tiles(xT_), tiles(sq_)
        raw = raw_[:, :].rearrange("p (s k n) -> p s k n", s=RAW, k=CK)
        whi = whi_[:, :].rearrange("p (s k n) -> p s k n", s=SPLIT, k=CK)
        wlo = wlo_[:, :].rearrange("p (s k n) -> p s k n", s=SPLIT, k=CK)
        ident, ones = const[:, K_ID:K_ID + P], const[:, K_ONE:K_ONE + P]

        at = {}
        n_vec = 0
        for name, n in (("b_in", 48), ("conv_b", 8), ("conv_ln_g", 8), ("conv_ln_b", 8), ("b_conv_out", 8),
                        ("sg_ln_g", 8), ("sg_ln_b", 8), ("b_sg_out", 8), ("b_out", 8), ("norm_mix_g", 8),
                        ("norm_ffn_g", 8), ("norm_final_g", 8), ("g_ffn1_2", 8), ("g_mix_2", 8), ("g_ffn2_2", 8),
                        ("g_final_2", 8), ("g_q_lat_2", 3), ("g_kv_lat_2", 2)):
            at[name] = (n_vec, n)
            n_vec += n
        n_conv = n_vec
        n_vec += 8 * CONV_W
        assert n_vec <= 424
        conv_w = vec[:, n_conv:n_conv + 8 * CONV_W].rearrange("p (c j) -> p c j", j=CONV_W)

        def gain_of(name):
            o, n = at[name]
            return vec[:, o:o + n]

        def col(name, k):
            o, n = at[name]
            return vec[:, o + k:o + k + 1]

        both_gains = vec[:, 424:432]

        NR = GROUPS + EXPERTS
        wr_ = sb("w_router", KT * NR + NR)
        wr = wr_[:, 0:KT * NR].rearrange("p (k e) -> p k e", e=NR)
        br = wr_[:, KT * NR:KT * NR + NR]
        gather_row = sb("gather_row", PASSES + 2, I32)
        scatter_row = sb("scatter_row", PASSES + 2, I32)
        row_weight = sb("row_weight", PASSES + 2)
        S_PAIR, S_ODD, S_END = 0, PASSES, 2 * PASSES
        sched = sb("schedule", 2 * PASSES + EXPERTS, I32)
        g_cur = [sb(f"gather_now{b}", 1, I32) for b in range(2)]
        s_cur = [sb(f"scatter_now{b}", 1, I32) for b in range(2)]

        pos_i = sb("slot_of_token", TT * TOP, I32)
        e_int = sb("expert_of_pass", 2 * PASSES, I32)

        AR = 25600
        with ExitStack() as c1:
            hhi_ = c1.enter_context(nc.sbuf_tensor("h_hi", [P, KT * T], F32R))
            hlo_ = c1.enter_context(nc.sbuf_tensor("h_lo", [P, KT * T], F32R))
            with nc.sbuf_tensor("arena1", [P, AR], F32) as ar1:
                pass
            with ExitStack() as c2:
                ahi_ = c2.enter_context(nc.sbuf_tensor("act_hi", [P, FT * T], F32R))
                alo_ = c2.enter_context(nc.sbuf_tensor("act_lo", [P, FT * T], F32R))
                gated_ = c2.enter_context(nc.sbuf_tensor("gated", [P, 4 * T], F32))
            with nc.sbuf_tensor("arena3", [P, AR], F32) as ar3:
                pass
        with nc.sbuf_tensor("expert_input", [P, 2 * KT * T], F32) as hx_:
            pass
        hhi, hlo = tiles(hhi_), tiles(hlo_)
        ahi, alo = tiles(ahi_), tiles(alo_)
        gated = gated_[:, :].rearrange("p (s k n) -> p s k n", s=2, k=2)

        sig = tiles(ar1[:, 0:4096])
        conv = sig
        APW = PAD + T
        a_pad = ar1[:, 4096:4096 + KT * APW].rearrange("p (k n) -> p k n", n=APW)
        vtok = ar1[:, 4096:8192].rearrange("p (t d) -> p t d", d=D)
        v = tiles(ar1[:, 8448:12544])
        hF = v
        u = tiles(ar1[:, 12544:16640])
        wsg_in = ar1[:, 12544:12544 + 1024].rearrange("p (h k) -> p h k", k=P)
        ga = tiles(ar1[:, 16640:20736])
        x_tok = ar1[:, 16640:20736].rearrange("p (t d) -> p t d", d=D)
        vec_rows = ar1[:, 0:256].rearrange("p (r f) -> p r f", f=P)
        tap_rows = ar1[:, 256:1280]
        x_tok2 = ar1[:, 8448:12544].rearrange("p (t d) -> p t d", d=D)
        gb = xT
        wsgT = ar1[:, 20736:21760].rearrange("p (h q) -> p h q", q=P)
        bsg = ar1[:, 21760:22784].rearrange("p (h q) -> p h q", q=P)
        stat_mean2 = ar1[:, 23808:24320]
        conv_tmp = tiles(ar1[:, 24320:25344])
        v_squares, conv_squares = conv_tmp[:, 0, :], conv_tmp[:, 1, :]
        sg_tmp = tiles(ar1[:, 22784:23808])
        wgu = [ar1[:, o:o + 8192].rearrange("p (k w n) -> p k w n", k=KT, w=2) for o in (0, 12288)]
        wd = [ar1[:, o:o + 4096].rearrange("p (k n) -> p k n", k=4) for o in (8192, 20480)]
        h2 = tiles(hx_[:, 0:4096])
        h_tok = hx_[:, 4096:8192].rearrange("p (t d) -> p t d", d=D)
        xg = [ar1[:, 24576 + b * 512:24576 + b * 512 + 512] for b in range(2)]
        y_tok = ar1[:, 0:8192].rearrange("p (t j d) -> p t j d", t=TT, j=TOP)
        y_sum = ar1[:, 8192:12288].rearrange("p (t d) -> p t d", d=D)
        xgT = [raw_[:, b * 512:b * 512 + 512].rearrange("p (c m) -> p c m", m=P) for b in range(2)]
        h_sg = [raw_[:, 1024 + b * 256:1280 + b * 256] for b in range(2)]
        heT = [raw_[:, 1536 + b * 256:1792 + b * 256].rearrange("p (c m) -> p c m", m=P) for b in range(2)]
        y_row = [raw_[:, 2048 + b * 512:2560 + b * 512] for b in range(2)]
        psum = ctx.enter_context(nc.psum_tensor("psum", [P, 8, T], F32))

        def bank(g, m):
            return psum[:, 4 * (g % 2) + m, :]

        consts_in = sem("consts_in")
        tables_in = sem("tables_in")
        vec_in = sem("vector_rows_in")
        vec_t = sem("vectors_transposed")
        vec_r = sem("vectors_ready")
        w_raw = [sem(f"w_raw{i}") for i in range(RAW)]
        w_raw2 = [sem(f"w_raw_up{i}") for i in range(RAW)]
        w_hi = sem("w_hi_ready")
        w_lo = sem("w_lo_ready")
        w_used = sem("w_used")
        evac = [sem("psum_group_read0"), sem("psum_group_read1")]

        x_in = sem("x_in")
        sg_in = sem("w_sg_in")
        x_t = sem("x_transposed")
        x_r = sem("x_ready")
        wsg_t = sem("w_sg_transposed")
        wsg_r = sem("w_sg_ready")
        pad_r = sem("conv_pad_ready")
        eps_r = sem("eps_ready")
        sq_r = sem("square_ready")
        sq_u = sem("square_summed")
        tot_r = sem("squares_total")
        gain_r = sem("gains_ready")
        std_r = sem("root_ready")
        h_r = sem("normed_ready")
        hi_r = sem("act_hi_ready")
        lo_r = sem("act_lo_ready")
        dchain = sem("dve_step")
        conv_s = sem("conv_step")
        conv_p = sem("conv_step_of_gpsimd")
        conv_m = sem("conv_product_of_gpsimd")
        mm_r = sem("mean_summed")
        mean_r = sem("mean_ready")
        cen_r = sem("centred_ready")
        nrm_r = sem("layer_normed")
        vn_r = sem("v_ready")
        v_t = sem("v_transposed")
        vt_r = sem("v_on_tokens")
        sv_r = sem("spatial_sum_ready")
        s_r = sem("gate_product_ready")
        c_r = sem("conv_act_ready")
        m_r = sem("mix_ready")

        def group_read(eng, g):
            if g >= 0:
                eng.wait_ge(evac[g % 2], g // 2 + 1)

        chain = {"d": 0}

        def dlink(eng, ins):
            chain["d"] += 1
            ins.then_inc(dchain, 1)
            eng.wait_ge(dchain, chain["d"])

        cnt = dict.fromkeys(("sq_act", "sq_pe", "root", "inverse", "hi_act", "hi_dve", "h_dve", "x_dve"), 0)

        def square(eng, src, gain=1.0):
            if cnt["sq_act"] >= 2:
                eng.wait_ge(sq_u, cnt["sq_act"] - 1)
            eng.activation(sq[:, cnt["sq_act"] % 2, :], src, ACT.Square, scale=gain).then_inc(sq_r, 1)
            cnt["sq_act"] += 1

        def squares(eng, src, tile_wait, n=KT, gain=None):
            for k in range(n):
                tile_wait(k)
                square(eng, src[:, k, :], 1.0 if gain is None else gain[:, k:k + 1])

        def sum_squares(eng, b, n=KT):
            for k in range(n):
                eng.wait_ge(sq_r, cnt["sq_pe"] + 1)
                eng.matmul(psum[:, b, :], ones, sq[:, cnt["sq_pe"] % 2, :], start=(k == 0),
                           stop=(k == n - 1)).then_inc(sq_u, 1)
                cnt["sq_pe"] += 1

        def root(eng, b, width=D):
            eng.wait_ge(sq_u, cnt["sq_act"])
            eng.activation(stat_std[:, :], psum[:, b, :], ACT.Sqrt, bias=eps_col, scale=1.0 / width).then_inc(std_r, 1)

        def inverse(eng):
            cnt["inverse"] += 1
            eng.wait_ge(std_r, cnt["inverse"])
            dlink(eng, eng.reciprocal(stat_std[:, :], stat_std[:, :]))

        def scale_rows(eng, dst, src, gain, sem_, n=KT):
            for k in range(n):
                eng.scalar_tensor_tensor(out=dst[:, k, :], in0=src[:, k, :], scalar=col(gain, k), in1=stat_std[:, :],
                                         op0=ALU.mult, op1=ALU.mult).then_inc(sem_, 1)

        def high_parts(eng, src, sem_, base, n=KT):
            for k in range(n):
                eng.wait_ge(sem_, base + k + 1)
                eng.activation(hhi[:, k, :], src[:, k, :], ACT.Copy).then_inc(hi_r, 1)

        def low_parts(eng, src, n=KT):
            for k in range(n):
                cnt["hi_dve"] += 1
                eng.wait_ge(hi_r, cnt["hi_dve"])
                eng.tensor_tensor(hlo[:, k, :], src[:, k, :], hhi[:, k, :].bitcast(F32), ALU.subtract).then_inc(lo_r, 1)

        def gained_high(eng, gain, tile_wait):
            for k in range(KT):
                tile_wait(k)
                eng.activation(hhi[:, k, :], xT[:, k, :], ACT.Identity, scale=gain[:, k:k + 1]).then_inc(hi_r, 1)

        def gained_low(eng, gain, ks):
            for k in ks:
                cnt["hi_dve"] += 1
                eng.wait_ge(hi_r, cnt["hi_dve"])
                eng.scalar_tensor_tensor(out=hlo[:, k, :], in0=xT[:, k, :], scalar=gain[:, k:k + 1],
                                         in1=hhi[:, k, :].bitcast(F32), op0=ALU.mult, op1=ALU.subtract).then_inc(lo_r, 1)

        def add_squares(eng, base, acc):
            eng.wait_ge(sq_r, base + 2)
            eng.tensor_tensor(acc, sq[:, 0, :], sq[:, 1, :], ALU.add).then_inc(sq_u, 2)
            for k in range(2, KT):
                eng.wait_ge(sq_r, base + k + 1)
                eng.wait_ge(sq_u, base + k)
                eng.tensor_tensor(acc, acc, sq[:, (base + k) % 2, :], ALU.add).then_inc(sq_u, 1)

        def total_squares(eng, acc, b):
            cnt["sq_pe"] += KT
            eng.wait_ge(sq_u, cnt["sq_pe"])
            eng.matmul(psum[:, b, :], ones, acc, start=True, stop=True).then_inc(tot_r, 1)

        def root_of_total(eng, dst, b):
            cnt["root"] += 1
            eng.wait_ge(tot_r, cnt["root"])
            eng.activation(dst, psum[:, b, :], ACT.Sqrt, bias=eps_col, scale=1.0 / D).then_inc(std_r, 1)

        def load_chunk(eng, c, slot, src, second=None, n2=0):
            if not isinstance(c, int) or c >= RAW:
                eng.wait_ge(w_lo, c - RAW + 1)
            if second is None:
                eng.dma_start(raw[:, slot, :, :], src).then_inc(w_raw[slot], 16)
            else:
                eng.dma_start(raw[:, slot, :, 0:CN // 2], src).then_inc(w_raw[slot], 16)
                eng.dma_start(raw[:, slot, :, CN // 2:CN], second).then_inc(w_raw2[slot], 16)

        def split_hi(eng, c0, k, i=0, step=0, up=None):
            slot = (c0 + k) % RAW
            eng.wait_ge(w_raw[slot], 16 * ((c0 + k) // RAW + 1) + i * (16 * step // RAW))
            if up is not None:
                eng.wait_ge(w_raw2[slot], 16 * (up // RAW + 1) + i * (16 * step // RAW))
            if step or c0 + k >= SPLIT:
                eng.wait_ge(w_used, c0 + k - SPLIT + 1 + i * step)
            eng.activation(whi[:, (c0 + k) % SPLIT, :, :], raw[:, slot, :, :], ACT.Copy).then_inc(w_hi, 1)

        def split_lo(eng, c0, k, i=0, step=0):
            slot, s = (c0 + k) % RAW, (c0 + k) % SPLIT
            eng.wait_ge(w_hi, c0 + k + 1 + i * step)
            eng.tensor_tensor(wlo[:, s, :, :], raw[:, slot, :, :], whi[:, s, :, :].bitcast(F32),
                              ALU.subtract).then_inc(w_lo, 1)

        def mm3(eng, o, w_h, w_l, x_h, x_l, first, last):
            eng.matmul(o, w_h, x_h, start=first, stop=False)
            eng.matmul(o, w_h, x_l, start=False, stop=False)
            return eng.matmul(o, w_l, x_h, start=False, stop=last)

        def mul_first(eng, c0, g, base):
            group_read(eng, g - 2)
            for k in range(4):
                eng.wait_ge(lo_r, base + 2 * k + 2)
                mul_chunk(eng, c0, k, g, (2 * k, 2 * k + 1), hhi, hlo, k == 0, k == 3)

        def mul_chunk(eng, c0, k, g, kts, xh, xl, first, last, i=0, step=0):
            s = (c0 + k) % SPLIT
            eng.wait_ge(w_lo, c0 + k + 1 + i * step)
            for a in range(CK):
                for m in range(4):
                    f = slice(m * P, m * P + P)
                    mm = mm3(eng, bank(g, m), whi[:, s, a, f], wlo[:, s, a, f], xh[:, kts[a], :], xl[:, kts[a], :],
                             first and a == 0, last and a == CK - 1)
            mm.then_inc(w_used, 1)

        def mul_group(eng, c0, g, xh, xl, i=0, step=0):
            if step or g >= 2:
                eng.wait_ge(evac[g % 2], g // 2 + i * (step // 8))
            for k in range(4):
                mul_chunk(eng, c0, k, g, (2 * k, 2 * k + 1), xh, xl, k == 0, k == 3, i, step)

        def mul_groups(eng, c0, g0, n, xh, xl):
            pairs = n // 2
            for j in range(2 if g0 < 2 else 0):
                mul_group(eng, c0 + 4 * j, g0 + j, xh, xl)
            lo = 1 if g0 < 2 else 0
            if pairs - lo > 1:
                with eng.Fori(lo, pairs) as i:
                    for j in range(2):
                        mul_group(eng, c0 + 4 * j, g0 + j, xh, xl, i, 8)
            else:
                for q in range(lo, pairs):
                    for j in range(2):
                        mul_group(eng, c0 + 8 * q + 4 * j, g0 + 2 * q + j, xh, xl)
            if n % 2:
                mul_group(eng, c0 + 4 * (n - 1), g0 + n - 1, xh, xl)

        w_in_v = A["w_in"].rearrange("o (k p) n -> p (o k) n", p=P)
        order = [1024, 1536, 0, 512, 3072, 3584, 2048, 2560, 4096, 4608, 5120, 5632]
        def sp_block1(sp):
            sp.dma_start(const[:, 0:K_CB], A["consts"][:, 0:K_CB]).then_inc(consts_in, 16)
            sp.dma_start(x_tok, A["x"].rearrange("o (t p) d -> p (o t) d", p=P)).then_inc(x_in, 16)
            sp.dma_start(wsg_in, A["w_sg"].rearrange("o h q k -> q (o h) k")).then_inc(sg_in, 16)
            sp.dma_start(bsg.rearrange("p h q -> p (h q)"),
                         A["b_sg"].rearrange("o h q -> o (h q)").to_broadcast([P, HEADS_SG * P])).then_inc(sg_in, 16)
            sp.dma_start(const[:, K_CB:K_N], A["consts"][:, K_CB:K_N]).then_inc(tables_in, 16)
            for g in range(N_IN):
                for k in range(4):
                    load_chunk(sp, C_IN + 4 * g + k, k, w_in_v[:, 2 * k:2 * k + 2, order[g]:order[g] + CN])
            for c0, name in ((C_SGO, "w_sg_out"), (C_CVO, "w_conv_out"), (C_WO, "w_out")):
                wv = A[name].rearrange("o (k p) n -> p (o k) n", p=P)
                for g in range(2):
                    for k in range(4):
                        load_chunk(sp, c0 + 4 * g + k, k, wv[:, 2 * k:2 * k + 2, CN * g:CN * g + CN])
                if c0 == C_SGO:
                    sp.wait_ge(vt_r, TT)
                    sp.dma_start(x_tok2, A["x"].rearrange("o (t p) d -> p (o t) d", p=P)).then_inc(x_in, 16)

        def act_vectors(act):
            for name, (o, n) in at.items():
                src = A[name]
                src = src.rearrange("(k p) -> k p", p=P) if len(src.shape) == 1 else \
                    src.rearrange("o (k p) -> (o k) p", p=P)
                act.dma_start(vec_rows[o % P:o % P + n, o // P, :], src).then_inc(vec_in, 16)
            act.dma_start(tap_rows[0:CONV_W, :], A["conv_w"][0]).then_inc(vec_in, 16)

        def pool_block1(pool):
            pool.memset(eps_t[:, :], EPS).then_inc(eps_r, 1)
            pool.memset(a_pad[:, :, 0:PAD], 0.0).then_inc(pad_r, 1)
            pool.memset(wsgT[:, :, :], 0.0).then_inc(pad_r, 1)
            group_read(pool, 3)
            pool.wait_ge(vec_r, 1)
            for n in range(CONV_W * N_OWN):
                j, c = n // N_OWN, DVE_CONV + n % N_OWN
                if j == 0:
                    pool.tensor_scalar(conv[:, c, :], a_pad[:, c, 0:T], conv_w[:, c, 0:1], col("conv_b", c), ALU.mult,
                                       ALU.add).then_inc(conv_p, 1)
                else:
                    pool.wait_ge(conv_m, n - N_OWN + 1)
                    pool.wait_ge(conv_p, n - N_OWN + 1)
                    pool.tensor_tensor(conv[:, c, :], conv[:, c, :], conv_tmp[:, n % N_OWN, :],
                                       ALU.add).then_inc(conv_p, 1)

            pool.wait_ge(conv_p, N_OWN * CONV_W)
            add_squares(pool, KT, v_squares)
            pool.wait_ge(sq_u, 2 * KT)
            add_squares(pool, 2 * KT, conv_squares)

        def conv_products(act, j):
            for q in range(N_OWN):
                c = DVE_CONV + q
                if j == 1 and q == 0:
                    group_read(act, 3)
                if j >= 2:
                    act.wait_ge(conv_p, N_OWN * (j - 1) + q + 1)
                act.activation(conv_tmp[:, q, :], a_pad[:, c, j:j + T], ACT.Identity,
                               scale=conv_w[:, c, j:j + 1]).then_inc(conv_m, 1)

        def transpose_x(pe, src):
            for k in range(KT):
                for t in range(TT):
                    mm = pe.transpose(psum[:, k, t * P:(t + 1) * P], src[:, t, k * P:(k + 1) * P], ident)
                mm.then_inc(x_t, 1)

        def pe_block1(pe):
            pe.wait_ge(consts_in, 16)
            pe.wait_ge(x_in, 16)
            transpose_x(pe, x_tok)
            pe.wait_ge(vec_in, 16 * (len(at) + 1))
            pe.wait_ge(x_r, KT)
            for o in range(0, n_conv, P):
                n = min(P, n_conv - o)
                pe.transpose(psum[:, 5, o:o + n], vec_rows[0:n, o // P, :], ident[0:n, 0:n])
            for c in range(KT):
                o = n_conv + c * CONV_W
                mm = pe.transpose(psum[:, 5, o:o + CONV_W], tap_rows[0:CONV_W, c * P:(c + 1) * P],
                                  ident[0:CONV_W, 0:CONV_W])
            mm.then_inc(vec_t, 1)
            pe.wait_ge(sg_in, 32)
            for h in range(HEADS_SG):
                mm = pe.transpose(psum[:, 6 + h // 4, (h % 4) * P:(h % 4 + 1) * P], wsg_in[:, h, :], ident)
            mm.then_inc(wsg_t, 1)
            sum_squares(pe, 0)
            pe.wait_ge(wsg_r, 2)
            pe.wait_ge(lo_r, KT)
            mul_groups(pe, C_IN, G_IN, 8, hhi, hlo)
            for g in (4, 5, 6):
                group_read(pe, g)
            for k in range(KT):
                mm = pe.matmul(psum[:, 0, :], ones, v[:, k, :], start=(k == 0), stop=(k == KT - 1))
            mm.then_inc(mm_r, 1)
            pe.wait_ge(mean_r, 1)
            mul_groups(pe, C_IN + 32, G_IN + 8, 2, hhi, hlo)
            group_read(pe, 8)
            total_squares(pe, v_squares, 0)
            pe.wait_ge(std_r, 2)
            mul_groups(pe, C_IN + 40, G_IN + 10, 2, hhi, hlo)
            group_read(pe, 10)
            group_read(pe, 11)
            pe.wait_ge(conv_s, DVE_CONV * CONV_W)
            pe.wait_ge(conv_p, N_OWN * CONV_W)
            for k in range(KT):
                mm = pe.matmul(psum[:, 1, :], ones, conv[:, k, :], start=(k == 0), stop=(k == KT - 1))
            mm.then_inc(mm_r, 1)
            pe.wait_ge(mean_r, 2)
            pe.wait_ge(vn_r, KT)
            for t in range(TT):
                for k in range(KT):
                    mm = pe.transpose(psum[:, 2 * t + k // 4, (k % 4) * P:(k % 4 + 1) * P],
                                      v[:, k, t * P:(t + 1) * P], ident)
                mm.then_inc(v_t, 1)
            pe.wait_ge(vt_r, TT)
            for h in range(HEADS_SG):
                for t in range(TT):
                    mm = pe.matmul(psum[:, h, t * P:(t + 1) * P], vtok[:, t, h * P:(h + 1) * P], wsgT[:, h, :],
                                   start=True, stop=True)
                mm.then_inc(sv_r, 1)
            pe.wait_ge(s_r, HEADS_SG)
            total_squares(pe, conv_squares, 7)
            pe.wait_ge(lo_r, 2 * KT)
            mul_group(pe, C_SGO, G_SGO, hhi, hlo)
            pe.wait_ge(std_r, 3)
            mul_group(pe, C_SGO + 4, G_SGO + 1, hhi, hlo)
            pe.wait_ge(lo_r, 3 * KT)
            mul_groups(pe, C_CVO, G_CVO, 2, hhi, hlo)
            group_read(pe, G_CVO)
            group_read(pe, G_CVO + 1)
            pe.wait_ge(x_in, 32)
            transpose_x(pe, x_tok2)
            pe.wait_ge(x_r, 2 * KT)
            pe.wait_ge(lo_r, 4 * KT)
            mul_groups(pe, C_WO, G_WO, 2, hhi, hlo)

        kinds = [ACT.Sigmoid] * 2 + [None] * 2 + [ACT.Gelu] * 4 + [ACT.Sigmoid] * 4
        goal = [sig] * 2 + [a_pad] * 2 + [v] * 2 + [u] * 2 + [ga] * 2 + [gb] * 2

        def act_block1(act):
            def read_group(g):
                if kinds[g] is None:
                    return
                act.wait_ge(w_used, C_IN + 4 * g + 4)
                for m in range(4):
                    ins = act.activation(goal[g][:, 4 * (g % 2) + m, :], bank(g, m), kinds[g],
                                         bias=col("b_in", order[g] // P + m))
                ins.then_inc(evac[g % 2], 1)

            def scale_mean(j, dst):
                act.wait_ge(mm_r, j + 1)
                act.activation(dst[:, :], psum[:, j, :], ACT.Identity, scale=1.0 / D).then_inc(mean_r, 1)

            act_vectors(act)
            act.wait_ge(eps_r, 1)
            squares(act, xT, lambda k: act.wait_ge(x_r, k + 1))
            root(act, 0)
            act.wait_ge(vec_r, 1)
            high_parts(act, hF, h_r, 0)
            tap = 1
            for g in range(N_IN):
                for k in range(4):
                    if k == 2 and g:
                        read_group(g - 1)
                    split_hi(act, C_IN + 4 * g, k)
                    if 4 * g + k >= 18:
                        for _ in range(2):
                            if tap < CONV_W:
                                conv_products(act, tap)
                                tap += 1
                    c = 4 * g + k
                    if c == 33:
                        scale_mean(0, stat_mean)
                    if 34 <= c < 38:
                        for m in (2 * (c - 34), 2 * (c - 34) + 1):
                            act.wait_ge(cen_r, m + 1)
                            square(act, v[:, m, :])
                    if c == 41:
                        root_of_total(act, stat_std[:, :], 0)
                    if 44 <= c < 48:
                        for m in (2 * (c - 44), 2 * (c - 44) + 1):
                            act.wait_ge(nrm_r, m + 1)
                            act.activation(v[:, m, :], v[:, m, :], ACT.Identity, bias=col("sg_ln_b", m),
                                           scale=col("sg_ln_g", m)).then_inc(vn_r, 1)
            for k in range(SPLIT):
                split_hi(act, C_SGO, k)
            read_group(N_IN - 1)
            scale_mean(1, stat_mean2)
            for t in range(TT):
                act.wait_ge(v_t, t + 1)
                act.activation(vtok[:, t, :], psum[:, 2 * t:2 * t + 2, :].rearrange("p b n -> p (b n)"),
                               ACT.Copy).then_inc(vt_r, 1)
            squares(act, conv, lambda k: act.wait_ge(cen_r, KT + k + 1))
            high_parts(act, u, s_r, 0)
            root_of_total(act, stat_std[:, :], 7)
            for k in range(2, 4):
                split_hi(act, C_SGO, k)
            for k in range(KT):
                act.wait_ge(nrm_r, KT + k + 1)
                act.activation(conv[:, k, :], conv[:, k, :], ACT.Silu, bias=col("conv_ln_b", k),
                               scale=col("conv_ln_g", k)).then_inc(c_r, 1)
            for k in range(4, 8):
                split_hi(act, C_SGO, k)
            for k in range(SPLIT):
                split_hi(act, C_CVO, k)
            act.wait_ge(w_used, C_CVO)
            high_parts(act, conv, c_r, 0)
            for k in range(2, 8):
                split_hi(act, C_CVO, k)
            for k in range(SPLIT):
                split_hi(act, C_WO, k)
            high_parts(act, ga, m_r, 0)
            for k in range(2, 8):
                split_hi(act, C_WO, k)

        def dve_block1(dve):
            for k in range(KT):
                dve.wait_ge(x_t, k + 1)
                dve.tensor_copy(xT[:, k, :], psum[:, k, :]).then_inc(x_r, 1)
            dve.wait_ge(vec_t, 1)
            dve.tensor_copy(vec[:, 0:n_vec], psum[:, 5, 0:n_vec]).then_inc(vec_r, 1)
            dve.wait_ge(wsg_t, 1)
            dve.wait_ge(pad_r, 2)
            wsg_ps = psum[:, 6:8, :].rearrange("p b (h q) -> p (b h) q", q=P)
            dve.tensor_copy(wsgT[0:SG_CHUNK, :, :], wsg_ps[0:SG_CHUNK, :, :]).then_inc(wsg_r, 1)
            dve.tensor_copy(wsgT[SG_CHUNK:P, :, SG_CHUNK:P], wsg_ps[SG_CHUNK:P, :, SG_CHUNK:P]).then_inc(wsg_r, 1)
            inverse(dve)
            dve.wait_ge(vec_r, 1)
            scale_rows(dve, hF, xT, "norm_mix_g", h_r)
            low_parts(dve, hF)

            def read_glu(g):
                dve.wait_ge(w_used, C_IN + 4 * g + 4)
                if g == 2:
                    group_read(dve, 0)
                    group_read(dve, 1)
                for m in range(4):
                    k = 4 * (g % 2) + m
                    ins = dve.scalar_tensor_tensor(out=a_pad[:, k, PAD:APW], in0=bank(g, m),
                                                   scalar=col("b_in", order[g] // P + m), in1=sig[:, k, :],
                                                   op0=ALU.add, op1=ALU.mult)
                ins.then_inc(evac[g % 2], 1)

            for g in range(4):
                for k in range(4):
                    if k == 2 and g == 3:
                        read_glu(2)
                    split_lo(dve, C_IN + 4 * g, k)
            split_lo(dve, C_IN + 16, 0)
            split_lo(dve, C_IN + 16, 1)
            read_glu(3)
            group_read(dve, 3)
            dve.wait_ge(pad_r, 1)
            n_split = 16

            def convolve(i):
                for n in range(3 * CONV_W):
                    j, c = n // 3, 3 * i + n % 3
                    if n >= 3:
                        dve.wait_ge(conv_s, 3 * CONV_W * i + n - 2)
                    src, tap = a_pad[:, c, j:j + T], conv_w[:, c, j:j + 1]
                    if j == 0:
                        dve.tensor_scalar(conv[:, c, :], src, tap, col("conv_b", c), ALU.mult, ALU.add).then_inc(conv_s, 1)
                    else:
                        dve.scalar_tensor_tensor(out=conv[:, c, :], in0=src, scalar=tap, in1=conv[:, c, :], op0=ALU.mult,
                                                 op1=ALU.add).then_inc(conv_s, 1)
                    k = (n + 1) * n_split // (3 * CONV_W)
                    if k > n * n_split // (3 * CONV_W):
                        split_lo(dve, C_IN + 16, 1 + k + i * n_split)
                        if i == 1 and k == 8:
                            scale_v()

            def scale_v():
                inverse(dve)
                dve.wait_ge(cen_r, KT)
                for k in range(KT):
                    dve.tensor_tensor(v[:, k, :], v[:, k, :], stat_std[:, :], ALU.mult).then_inc(nrm_r, 1)

            convolve(0)
            dve.wait_ge(mean_r, 1)
            group_read(dve, 4)
            group_read(dve, 5)
            for k in range(KT):
                dve.tensor_tensor(v[:, k, :], v[:, k, :], stat_mean[:, :], ALU.subtract).then_inc(cen_r, 1)
            convolve(1)
            dve.wait_ge(mean_r, 2)
            for k in range(KT):
                dve.tensor_tensor(conv[:, k, :], conv[:, k, :], stat_mean2[:, :], ALU.subtract).then_inc(cen_r, 1)
            group_read(dve, 6)
            group_read(dve, 7)
            dve.wait_ge(sg_in, 32)
            for h in range(HEADS_SG):
                dve.wait_ge(sv_r, h + 1)
                dlink(dve, dve.tensor_tensor(
                    sg_tmp[:, h % 2, :].rearrange("p (t q) -> p t q", q=P),
                    psum[:, h, :].rearrange("p (t q) -> p t q", q=P),
                    bsg[:, h, :].unsqueeze(1).to_broadcast([P, TT, P]), ALU.add))
                dve.tensor_tensor(u[:, h, :], u[:, h, :], sg_tmp[:, h % 2, :], ALU.mult).then_inc(s_r, 1)
            low_parts(dve, u)
            inverse(dve)
            dve.wait_ge(cen_r, 2 * KT)
            for k in range(2, 4):
                split_lo(dve, C_SGO, k)
            for k in range(KT):
                dve.tensor_tensor(conv[:, k, :], conv[:, k, :], stat_std[:, :], ALU.mult).then_inc(nrm_r, 1)

            def read_gated(g, name, gate):
                dve.wait_ge(w_used, 4 * g + 4)
                group_read(dve, 8 if gate is ga else 10)
                group_read(dve, 9 if gate is ga else 11)
                for m in range(4):
                    k = 4 * (g % 2) + m
                    ins = dve.scalar_tensor_tensor(out=gate[:, k, :], in0=bank(g, m), scalar=col(name, k),
                                                   in1=gate[:, k, :], op0=ALU.add, op1=ALU.mult)
                ins.then_inc(evac[g % 2], 1)

            for k in range(4, 8):
                split_lo(dve, C_SGO, k)
            read_gated(G_SGO, "b_sg_out", gb)
            for k in range(SPLIT):
                split_lo(dve, C_CVO, k)
            read_gated(G_SGO + 1, "b_sg_out", gb)
            low_parts(dve, conv)
            for k in range(2, 6):
                split_lo(dve, C_CVO, k)
            read_gated(G_CVO, "b_conv_out", ga)
            for k in range(6, 8):
                split_lo(dve, C_CVO, k)
            for k in range(SPLIT):
                split_lo(dve, C_WO, k)
            read_gated(G_CVO + 1, "b_conv_out", ga)
            group_read(dve, G_CVO)
            group_read(dve, G_CVO + 1)
            for k in range(KT):
                dve.tensor_tensor(ga[:, k, :], ga[:, k, :], gb[:, k, :], ALU.add).then_inc(m_r, 1)
            low_parts(dve, ga)
            dve.wait_ge(m_r, KT)
            for k in range(KT):
                dve.wait_ge(x_t, KT + k + 1)
                dve.tensor_copy(xT[:, k, :], psum[:, k, :]).then_inc(x_r, 1)
            dve.wait_ge(x_r, 2 * KT)
            for g in (G_WO, G_WO + 1):
                for k in range(2, 6) if g == G_WO else range(6, 8):
                    split_lo(dve, C_WO, k)
                dve.wait_ge(w_used, 4 * g + 4)
                for m in range(4):
                    k = 4 * (g % 2) + m
                    ins = dve.scalar_tensor_tensor(out=xT[:, k, :], in0=bank(g, m), scalar=col("b_out", k),
                                                   in1=xT[:, k, :], op0=ALU.add, op1=ALU.add)
                ins.then_inc(evac[g % 2], 1)

        moe = {n: sem("moe_" + n) for n in (
            "h_tok", "h_dram", "logits", "logits_read", "exp_in", "exp", "onehot", "rank", "pos", "table",
            "tables", "x_t", "x", "gu", "act", "prod", "h_t", "h", "y_sum", "y", "pass", "done", "begun", "sum_t", "sums")}
        gathered = [sem(f"moe_gathered{b}") for b in range(2)]
        scattered = [sem(f"moe_scattered{b}") for b in range(2)]
        w_gu = [sem(f"moe_gate_up_in{b}") for b in range(2)]
        w_dn = [sem(f"moe_down_in{b}") for b in range(2)]
        y_in = [sem(f"expert_rows_in{t}") for t in range(TT)]
        idx_r = sem("moe_index_ready")
        wr_in = sem("router_in")
        h_dram = nc.dram_tensor("normed_rows", (2 * T, HALF), F32, kind="Internal").ap()
        y_dram = nc.dram_tensor("expert_rows", (2 * TOP * T, HALF), F32, kind="Internal").ap()
        SC = [0]

        def scratch(*dims):
            n = int(np.prod(dims))
            o = SC[0]
            SC[0] += n
            assert SC[0] <= 2560
            t = raw_[:, o:o + n]
            if len(dims) == 2:
                t = t.rearrange("p (a b) -> p a b", b=dims[1])
            if len(dims) == 3:
                t = t.rearrange("p (a b c) -> p a b c", b=dims[1], c=dims[2])
            return t

        lg = scratch(TT, NR)
        g_max, g_sel, g_w, v1, v2, i1, i2, den = (scratch(TT, 1) for _ in range(8))
        g_tmp, g_hot = scratch(TT, GROUPS), scratch(TT, GROUPS)
        e_all = scratch(TT, GROUPS, PER_GROUP)
        es, e_tmp, e_hot = scratch(TT, PER_GROUP), scratch(TT, PER_GROUP), scratch(TT, PER_GROUP)
        ex = scratch(TT, GROUPS + 1)
        hot = [scratch(TT, EXPERTS) for _ in range(TOP)]
        hots, place = scratch(TT, EXPERTS), scratch(TT, EXPERTS)
        w_tok = [scratch(TT, 1) for _ in range(TOP)]
        pos_f = scratch(TT, TOP)
        n_pass, p_end, p_base = scratch(EXPERTS), scratch(EXPERTS), scratch(EXPERTS)
        NA, NPS = TT * TOP, PASSES + 2
        slot_f, pass_f, choice = scratch(TT, TOP), scratch(TT, TOP), scratch(TT, TOP)
        held = scratch(NA, 2, NPS)
        slot_hot = sq_[:, :].rearrange("p (a s) -> p a s", s=P)
        pass_hot = stat_mean[:, 0:NA * NPS].rearrange("p (a n) -> p a n", n=NPS)
        over = scratch(EXPERTS, T // CAP)
        e_of = scratch(PASSES)
        late = raw_[:, 2560:2560 + PASSES * EXPERTS].rearrange("p (n e) -> p n e", e=EXPERTS)
        pos = pos_i[:, :].rearrange("p (t j) -> p t j", j=TOP)

        def iota(n):
            return const[:, K_IOTA:K_IOTA + n]

        def load_expert(sp, e, b):
            def rows(name, k):
                src = A[name].rearrange("o e (k p) n -> (o e) p k n", p=P)
                return src[e] if isinstance(e, int) else src[bass.ds(e, 1)].rearrange("o p k n -> p (o k) n")

            sp.dma_start(wgu[b][:, :, 0, :], rows("w_expert_gate", KT)).then_inc(w_gu[b], 16)
            sp.dma_start(wgu[b][:, :, 1, :], rows("w_expert_up", KT)).then_inc(w_gu[b], 16)
            sp.dma_start(wd[b], rows("w_expert_down", 4)).then_inc(w_dn[b], 16)

        def sp_router(sp):
            wv = A["w_router_group"].rearrange("o (k p) e -> p (o k) e", p=P)
            we = A["w_router_expert"].rearrange("o (k p) e -> p (o k) e", p=P)
            with nc.allow_non_contiguous_dma(reason="router weights"):
                sp.dma_start(wr[:, :, 0:GROUPS], wv).then_inc(wr_in, 16)
                sp.dma_start(wr[:, :, GROUPS:NR], we).then_inc(wr_in, 16)
                sp.dma_start(br[:, 0:GROUPS], A["b_router_group"].to_broadcast([P, GROUPS])).then_inc(wr_in, 16)
                sp.dma_start(br[:, GROUPS:NR], A["b_router_expert"].to_broadcast([P, EXPERTS])).then_inc(wr_in, 16)

        def sp_moe(sp):
            sp.wait_ge(x_t, 2 * KT)
            sp.wait_ge(w_used, C_WO)
            load_expert(sp, 0, 0)
            sp.wait_ge(lo_r, 4 * KT)
            load_expert(sp, 1, 1)
            for t in range(TT):
                sp.wait_ge(moe["h_tok"], t + 1)
                sp.dma_start(h_dram[2 * P * t:2 * P * (t + 1), :].rearrange("(p h) d -> p (h d)", h=2),
                             h_tok[:, t, :]).then_inc(moe["h_dram"], 16)
            sp.wait_ge(moe["h_dram"], 16 * TT)
            sp.wait_ge(moe["tables"], 1)
            with sp.Fori(1, EXPERTS // 2) as i:
                for b in range(2):
                    end = sp.value_load(sched[0:1, bass.ds(S_END + 2 * i - 2 + b, 1)], min_val=0, max_val=PASSES)
                    sp.wait_ge(moe["pass"], end + 1)
                    load_expert(sp, 2 * i + b, b)
            sp.wait_ge(moe["done"], 1)
            for t in range(TT):
                sp.dma_start(y_tok[:, t, :, :].rearrange("p j d -> p (j d)"),
                             y_dram[2 * TOP * P * t:2 * TOP * P * (t + 1), :].rearrange(
                                 "(p r) d -> p (r d)", r=2 * TOP)).then_inc(y_in[t], 16)

        def pe_moe(pe):
            sum_squares(pe, 0)
            pe.wait_ge(wr_in, 64)
            for t in range(TT):
                for k in range(KT):
                    pe.wait_ge(h_r, KT + k + 1)
                    mm = pe.matmul(psum[:, 1, t * 64:t * 64 + NR], h2[:, k, t * P:(t + 1) * P], wr[:, k, :],
                                   start=(k == 0), stop=(k == KT - 1))
            mm.then_inc(moe["logits"], 1)
            for t in range(TT):
                if t == 3:
                    pe.wait_ge(moe["h_tok"], 1)
                for k in range(KT):
                    mm = pe.transpose(psum[:, 2 + 2 * (t % 3) + k // 4, (k % 4) * P:(k % 4 + 1) * P],
                                      h2[:, k, t * P:(t + 1) * P], ident)
                mm.then_inc(moe["x_t"], 1)
            pe.wait_ge(moe["onehot"], 1)
            for t in range(TT):
                for q in range(t):
                    pe.matmul(psum[:, 1, t * 32:t * 32 + 32], ones, hots[:, q, :], start=(q == 0), stop=False)
                pe.matmul(psum[:, 1, t * 32:t * 32 + 32], const[:, K_UP:K_UP + P], hots[:, t, :], start=(t == 0),
                          stop=True)
            for t in range(TT):
                mm = pe.matmul(psum[:, 1, P:P + 32], ones, hots[:, t, :], start=(t == 0), stop=(t == TT - 1))
            mm.then_inc(moe["rank"], 1)
            pe.wait_ge(moe["pos"], 1)
            for a in range(NA):
                mm = pe.matmul(psum[:, 1, 256:256 + 2 * NPS], slot_hot[:, a, :], held[:, a, :, :].rearrange(
                    "p f n -> p (f n)"), start=(a == 0), stop=(a == NA - 1))
            mm.then_inc(moe["table"], 1)

            def turn(n, b):
                pe.wait_ge(gathered[b], 16 * (n // 2 + 1) if isinstance(n, int) else n * 8 + (16 - 8 * b))
                if not isinstance(n, int) or n >= 2:
                    pe.wait_ge(moe["x"], n - 1)
                for c in range(4):
                    mm = pe.transpose(psum[:, b, c * P:(c + 1) * P], xg[b][:, c * P:(c + 1) * P], ident)
                mm.then_inc(moe["x_t"], 1)

            def gate_up(n, b, w):
                for k in range(KT):
                    for q in range(2):
                        mm = pe.matmul(psum[q * CAP:(q + 1) * CAP, 2 + b, :].rearrange("p (w n) -> p w n", w=2),
                                       xgT[b][:, k % 4, (k // 4) * CAP:(k // 4 + 1) * CAP],
                                       wgu[w][:, k, :, q * 256:(q + 1) * 256], start=(k == 0), stop=(k == KT - 1))
                mm.then_inc(moe["gu"], 1)

            def down(n, b, w):
                for k in range(4):
                    for q in range(2):
                        mm = pe.matmul(psum[q * CAP:(q + 1) * CAP, 6 + b, :],
                                       heT[b][:, k % 2, (k // 2) * CAP:(k // 2 + 1) * CAP],
                                       wd[w][:, k, q * T:(q + 1) * T], start=(k == 0), stop=(k == 3))
                mm.then_inc(moe["pass"], 1)

            def pass_(n, b):
                pair = pe.value_load(sched[0:1, n:n + 1] if isinstance(n, int) else sched[0:1, bass.ds(S_PAIR + n, 1)],
                                     min_val=0, max_val=EXPERTS // 2 - 1)
                odd = pe.value_load(sched[0:1, S_ODD + n:S_ODD + n + 1] if isinstance(n, int)
                                    else sched[0:1, bass.ds(S_ODD + n, 1)], min_val=0, max_val=1)
                pe.wait_ge(moe["x"], n + 1)
                if not isinstance(n, int) or n >= 2:
                    pe.wait_ge(moe["y"], n - 1)
                with pe.If(odd < 1):
                    pe.wait_ge(w_gu[0], pair * 32 + 32)
                    gate_up(n, b, 0)
                with pe.Else():
                    pe.wait_ge(w_gu[1], pair * 32 + 32)
                    gate_up(n, b, 1)
                if b == 0:
                    turn(n + 1, 1)
                pe.wait_ge(moe["prod"], n + 1)
                for c in range(2):
                    mm = pe.transpose(psum[:, 4 + b, c * P:(c + 1) * P], h_sg[b][:, c * P:(c + 1) * P], ident)
                mm.then_inc(moe["h_t"], 1)
                pe.wait_ge(moe["h"], n + 1)
                with pe.If(odd < 1):
                    pe.wait_ge(w_dn[0], pair * 16 + 16)
                    down(n, b, 0)
                with pe.Else():
                    pe.wait_ge(w_dn[1], pair * 16 + 16)
                    down(n, b, 1)

            def two(i):
                turn(2 * i, 0)
                for b in range(2):
                    pass_(2 * i + b, b)

            pe.wait_ge(moe["tables"], 1)
            pe.sem_inc(moe["pass"], 1)
            two(0)
            total = pe.value_load(sched[0:1, S_END + EXPERTS - 1:S_END + EXPERTS], min_val=1, max_val=PASSES)
            with pe.Fori(1, PASSES // 2) as i:
                with pe.If(i * 2 < total):
                    two(i)
            for t in range(TT):
                pe.wait_ge(moe["sums"], t + 1)
                for k in range(KT):
                    mm = pe.transpose(psum[:, k, t * P:(t + 1) * P], y_sum[:, t, k * P:(k + 1) * P], ident)
                    if t == TT - 1:
                        mm.then_inc(moe["sum_t"], 1)

        def act_moe(act):
            squares(act, xT, lambda k: group_read(act, G_WO + k // 4))
            root(act, 0)
            for t in range(TT):
                act.wait_ge(moe["x_t"], t + 1)
                act.activation(h_tok[:, t, :], psum[:, 2 + 2 * (t % 3):4 + 2 * (t % 3), :].rearrange(
                    "p b n -> p (b n)"), ACT.Copy).then_inc(moe["h_tok"], 1)
            act.wait_ge(moe["exp_in"], 2)
            act.activation(ex, ex, ACT.Exp).then_inc(moe["exp"], 1)

            def pass_(n, b):
                act.wait_ge(moe["x_t"], n + 1 + TT)
                act.activation(xgT[b], psum[:, b, :].rearrange("p (c m) -> p c m", m=P), ACT.Copy).then_inc(
                    moe["x"], 1)

            def pass2(n, b):
                act.wait_ge(moe["gu"], n + 1)
                if not isinstance(n, int) or n >= 2:
                    act.wait_ge(moe["h_t"], n - 1)
                act.activation(h_sg[b], psum[:, 2 + b, 0:256], ACT.Silu).then_inc(moe["act"], 1)

            def two(i):
                pass_(2 * i, 0)
                pass2(2 * i, 0)
                pass_(2 * i + 1, 1)
                pass2(2 * i + 1, 1)

            act.wait_ge(moe["tables"], 1)
            two(0)
            total = act.value_load(sched[0:1, S_END + EXPERTS - 1:S_END + EXPERTS], min_val=1, max_val=PASSES)
            with act.Fori(1, PASSES // 2) as i:
                with act.If(i * 2 < total):
                    two(i)

        def dve_moe(dve):
            dve.wait_ge(tables_in, 16)
            dve.tensor_tensor(both_gains, gain_of("norm_final_g"), gain_of("g_ffn1_2"), ALU.mult).then_inc(gain_r, 1)
            inverse(dve)
            group_read(dve, G_WO)
            group_read(dve, G_WO + 1)
            scale_rows(dve, h2, xT, "norm_ffn_g", h_r)
            dve.wait_ge(moe["logits"], 1)
            dve.wait_ge(wr_in, 64)

            def bc(t, n):
                return t.to_broadcast([P, TT, n])

            def row(n):
                return iota(n).unsqueeze(1).to_broadcast([P, TT, n])

            def link(ins):
                dlink(dve, ins)

            def first_max(vals, n, best, where, one_hot, tmp):
                link(dve.tensor_reduce(best, vals, AX.X, ALU.max))
                link(dve.tensor_tensor(tmp, vals, bc(best, n), ALU.is_equal))
                link(dve.tensor_scalar(tmp, tmp, -99.0, 99.0, ALU.mult, ALU.add))
                link(dve.tensor_tensor(tmp, tmp, row(n), ALU.add))
                link(dve.tensor_reduce(where, tmp, AX.X, ALU.min))
                link(dve.tensor_tensor(one_hot, row(n), bc(where, n), ALU.is_equal))

            lg_ps = psum[:, 1, 0:TT * 64].rearrange("p (t e) -> p t e", e=64)[:, :, 0:NR]
            link(dve.tensor_tensor(lg, lg_ps, br.unsqueeze(1).to_broadcast([P, TT, NR]), ALU.add))
            gl = lg[:, :, 0:GROUPS]
            first_max(gl, GROUPS, g_max, g_sel, g_hot, g_tmp)
            dve.tensor_tensor(ex[:, :, 0:GROUPS], gl, bc(g_max, GROUPS), ALU.subtract).then_inc(moe["exp_in"], 1)
            link(dve.tensor_tensor(e_all, lg[:, :, GROUPS:NR].rearrange("p t (g j) -> p t g j", g=GROUPS),
                                   g_hot.unsqueeze(3).to_broadcast([P, TT, GROUPS, PER_GROUP]), ALU.mult))
            link(dve.tensor_reduce(es, e_all.rearrange("p t g j -> p t j g"), AX.X, ALU.add))
            first_max(es, PER_GROUP, v1, i1, e_hot, e_tmp)
            link(dve.scalar_tensor_tensor(out=es, in0=e_hot, scalar=FAR, in1=es, op0=ALU.mult, op1=ALU.add))
            first_max(es, PER_GROUP, v2, i2, e_hot, e_tmp)
            dve.tensor_tensor(ex[:, :, GROUPS:GROUPS + 1], v2, v1, ALU.subtract).then_inc(moe["exp_in"], 1)
            for j, i_ in enumerate((i1, i2)):
                link(dve.scalar_tensor_tensor(out=i_, in0=g_sel, scalar=float(PER_GROUP), in1=i_, op0=ALU.mult,
                                              op1=ALU.add))
                link(dve.tensor_tensor(hot[j], row(EXPERTS), bc(i_, EXPERTS), ALU.is_equal))
            dve.tensor_tensor(hots, hot[0], hot[1], ALU.add).then_inc(moe["onehot"], 1)
            dve.wait_ge(moe["exp"], 1)
            link(dve.tensor_reduce(g_w, ex[:, :, 0:GROUPS], AX.X, ALU.add))
            link(dve.tensor_scalar(den, ex[:, :, GROUPS:GROUPS + 1], 1.0, None, ALU.add))
            link(dve.tensor_tensor(den, den, g_w, ALU.mult))
            link(dve.reciprocal(w_tok[0], den))
            link(dve.tensor_tensor(w_tok[1], w_tok[0], ex[:, :, GROUPS:GROUPS + 1], ALU.mult))
            dve.wait_ge(moe["rank"], 1)
            link(dve.tensor_scalar(over, iota(T // CAP).unsqueeze(1).to_broadcast([P, EXPERTS, T // CAP]), float(CAP), None,
                                   ALU.mult))
            link(dve.tensor_tensor(over, psum[:, 1, P:P + EXPERTS].unsqueeze(2).to_broadcast([P, EXPERTS, T // CAP]),
                                   over, ALU.is_gt))
            link(dve.tensor_reduce(n_pass, over, AX.X, ALU.add))
            link(dve.tensor_tensor_scan(p_end, ones[:, 0:EXPERTS], n_pass, 0.0, ALU.mult, ALU.add))
            link(dve.tensor_tensor(p_base, p_end, n_pass, ALU.subtract))
            link(dve.tensor_scalar(p_base, p_base, float(CAP), None, ALU.mult))
            link(dve.tensor_tensor(place, psum[:, 1, 0:TT * EXPERTS].rearrange("p (t e) -> p t e", e=EXPERTS),
                                   p_base.unsqueeze(1).to_broadcast([P, TT, EXPERTS]), ALU.add))
            for j in range(TOP):
                link(dve.tensor_tensor(hot[j], hot[j], place, ALU.mult))
                link(dve.tensor_reduce(pos_f[:, :, j:j + 1], hot[j], AX.X, ALU.add))
                link(dve.tensor_scalar(choice[:, :, j:j + 1], const[:, K_TOK:K_TOK + TT].unsqueeze(2), float(TOP),
                                       j - BIG, ALU.mult, ALU.add))
            link(dve.tensor_copy(pos, pos_f))
            link(dve.tensor_scalar(e_int[:, 0:NA], pos_i[:, :], CAP - 1, None, ALU.bitwise_and))
            link(dve.tensor_scalar(e_int[:, NA:2 * NA], pos_i[:, :], CAP_BITS, None, ALU.arith_shift_right))
            flat = "p t j -> p (t j)"
            link(dve.tensor_copy(slot_f.rearrange(flat), e_int[:, 0:NA]))
            link(dve.tensor_copy(pass_f.rearrange(flat), e_int[:, NA:2 * NA]))
            for q in range(P // CAP):
                dve.tensor_tensor(slot_hot[:, :, q * CAP:(q + 1) * CAP], iota(CAP).unsqueeze(1).to_broadcast([P, NA, CAP]),
                                  slot_f.rearrange(flat).unsqueeze(2).to_broadcast([P, NA, CAP]), ALU.is_equal)
            link(dve.tensor_tensor(pass_hot, iota(NPS).unsqueeze(1).to_broadcast([P, NA, NPS]),
                                   pass_f.rearrange(flat).unsqueeze(2).to_broadcast([P, NA, NPS]), ALU.is_equal))
            dve.tensor_tensor(held[:, :, 0, :], pass_hot, choice.rearrange(flat).unsqueeze(2).to_broadcast([P, NA, NPS]),
                              ALU.mult)
            for j in range(TOP):
                ins = dve.tensor_tensor(
                    held[:, :, 1, :].rearrange("p (t j) n -> p t j n", j=TOP)[:, :, j, :],
                    pass_hot.rearrange("p (t j) n -> p t j n", j=TOP)[:, :, j, :],
                    w_tok[j].to_broadcast([P, TT, NPS]), ALU.mult)
            ins.then_inc(moe["pos"], 1)
            link(dve.tensor_tensor(late, p_end.unsqueeze(1).to_broadcast([P, PASSES, EXPERTS]),
                                   iota(PASSES).unsqueeze(2).to_broadcast([P, PASSES, EXPERTS]), ALU.is_le))
            link(dve.tensor_reduce(e_of, late, AX.X, ALU.add))
            link(dve.tensor_scalar(e_int[:, 0:PASSES], e_of, float(EXPERTS - 1), None, ALU.min))
            link(dve.tensor_scalar(sched[:, S_PAIR:S_PAIR + PASSES], e_int[:, 0:PASSES], 1, None, ALU.arith_shift_right))
            link(dve.tensor_scalar(sched[:, S_ODD:S_ODD + PASSES], e_int[:, 0:PASSES], 1, None, ALU.bitwise_and))
            link(dve.tensor_copy(sched[:, S_END:S_END + EXPERTS], p_end))
            dve.wait_ge(moe["table"], 1)
            half = const[:, K_HALF:K_HALF + 1]
            slots = psum[:, 1, 256:256 + 2 * NPS].rearrange("p (f n) -> p f n", f=2)
            link(dve.tensor_scalar(e_int[:, 0:NPS], slots[:, 0, :], BIG, None, ALU.add))
            link(dve.tensor_scalar(scatter_row[:, :], e_int[:, 0:NPS], 2.0, half, ALU.mult, ALU.add))
            link(dve.tensor_scalar(e_int[:, 0:NPS], e_int[:, 0:NPS], 1, None, ALU.arith_shift_right))
            link(dve.tensor_scalar(gather_row[:, :], e_int[:, 0:NPS], 2.0, half, ALU.mult, ALU.add))
            dve.tensor_copy(row_weight[:, :], slots[:, 1, :]).then_inc(moe["tables"], 1)
            dve.wait_ge(moe["tables"], 1)

            def pass_(n, b):
                dve.wait_ge(moe["act"], n + 1)
                dve.tensor_tensor(h_sg[b], h_sg[b], psum[:, 2 + b, 256:512], ALU.mult).then_inc(moe["prod"], 1)
                dve.wait_ge(moe["h_t"], n + 1)
                dve.tensor_copy(heT[b], psum[:, 4 + b, 0:256].rearrange("p (c m) -> p c m", m=P)).then_inc(moe["h"], 1)
                dve.wait_ge(moe["pass"], n + 2)
                if not isinstance(n, int) or n >= 2:
                    dve.wait_ge(scattered[b], (n - b) * 8)
                w = row_weight[:, n:n + 1] if isinstance(n, int) else row_weight[:, bass.ds(n, 1)]
                dve.tensor_scalar(y_row[b], psum[:, 6 + b, :], w, None, ALU.mult).then_inc(moe["y"], 1)

            for b in range(2):
                pass_(b, b)
            total = dve.value_load(sched[0:1, S_END + EXPERTS - 1:S_END + EXPERTS], min_val=1, max_val=PASSES)
            with dve.Fori(1, PASSES // 2) as i:
                with dve.If(i * 2 < total):
                    for b in range(2):
                        pass_(2 * i + b, b)
            for t in range(TT):
                dve.wait_ge(y_in[t], 16)
                dve.tensor_tensor(y_sum[:, t, :], y_tok[:, t, 0, :], y_tok[:, t, 1, :], ALU.add).then_inc(moe["sums"], 1)
            for k in range(KT):
                dve.wait_ge(moe["sum_t"], k + 1)
                dve.tensor_tensor(xT[:, k, :], xT[:, k, :], psum[:, k, :], ALU.add).then_inc(x_r, 1)

        def pool_moe(pool):
            pool.wait_ge(s_r, HEADS_SG)
            pool.wait_ge(lo_r, 2 * KT)
            pool.wait_ge(std_r, 3)
            pool.memset(ar1[:, 24576:25600], 0.0).then_inc(idx_r, 1)
            pool.wait_ge(moe["tables"], 1)
            pool.wait_ge(moe["h_dram"], 16 * TT)

            def gather(n, b):
                if not isinstance(n, int) or n >= 2:
                    pool.wait_ge(moe["x_t"], n - 1 + TT)
                g = gather_row[:, n:n + 1] if isinstance(n, int) else gather_row[:, bass.ds(n, 1)]
                pool.tensor_copy(g_cur[b][:, :], g).then_inc(idx_r, 1)
                first = isinstance(n, int) and n < 2
                pool.wait_ge(idx_r, 2 + n if first else 2 * n)
                pool.sem_inc(moe["begun"], 1)
                pool.indirect_dma_start(xg[b], None, h_dram[:, :], bass.IndirectOffsetOnAxis(ap=g_cur[b][:, 0:1], axis=0),
                                        bounds_check=2 * T - 1, oob_is_err=False).then_inc(gathered[b], 16)

            def scatter(n, b):
                s = scatter_row[:, n:n + 1] if isinstance(n, int) else scatter_row[:, bass.ds(n, 1)]
                if not isinstance(n, int) or n >= 2:
                    pool.wait_ge(scattered[b], (n - b) * 8)
                pool.tensor_copy(s_cur[b][:, :], s).then_inc(idx_r, 1)
                pool.wait_ge(idx_r, 2 * n + 5)
                pool.wait_ge(moe["y"], n + 1)
                pool.sem_inc(moe["begun"], 1)
                pool.indirect_dma_start(y_dram[:, :], bass.IndirectOffsetOnAxis(ap=s_cur[b][:, 0:1], axis=0), y_row[b], None,
                                        bounds_check=2 * TOP * T - 1, oob_is_err=False).then_inc(scattered[b], 16)

            gather(0, 0)
            gather(1, 1)

            def two(i):
                for b in range(2):
                    gather(2 * i + 2 + b, b)
                    scatter(2 * i + b, b)

            two(0)
            total = pool.value_load(sched[0:1, S_END + EXPERTS - 1:S_END + EXPERTS], min_val=1, max_val=PASSES)
            with pool.Fori(1, PASSES // 2) as i:
                with pool.If(i * 2 < total):
                    two(i)
            written = (total + 1) // 2 * 16
            landed = written + 16
            for b in range(2):
                pool.wait_ge(scattered[b], written)
                pool.wait_ge(gathered[b], landed)
            pool.sem_inc(moe["done"], 1)

        SQ_BEFORE, STD_BEFORE = 4 * KT, 4
        fgate_r = sem("ffn_gate_ready")
        fhi_r = sem("ffn_hi_ready")
        flo_r = sem("ffn_lo_ready")
        fscaled_r = sem("ffn_gate_scaled")
        fprod_r = sem("ffn_products_scaled")
        s2_r = sem("second_squares_read")
        var_r = sem("second_mean_scaled")
        sums = ar3[:, 24576:25088]
        sums2 = stat_mean[:, :]
        root1 = ar3[:, 25088:25600]
        over_root = stat_std[:, :].unsqueeze(1).to_broadcast([P, 2, T])

        cnt_std = (STD_BEFORE + 1, STD_BEFORE + 5 + 1)

        def sp_ffn(sp, j):
            gate = A[f"w{j + 1}_gate_2"].rearrange("o (k p) n -> p (o k) n", p=P)
            up = A[f"w{j + 1}_up_2"].rearrange("o (k p) n -> p (o k) n", p=P)
            down = A[f"w{j + 1}_down_2"].rearrange("o (k p) n -> p (o k) n", p=P)
            H = CN // 2

            def load_group(g, i=0):
                c = (g + 2 * i) * H
                cols = slice(c, c + H) if isinstance(c, int) else bass.ds(c, H)
                for k in range(4):
                    load_chunk(sp, C_UP[j] + 4 * g + k + 8 * i, (C_UP[j] + k) % RAW, gate[:, 2 * k:2 * k + 2, cols],
                               up[:, 2 * k:2 * k + 2, cols])

            with sp.Fori(0, N_UP // 2) as i:
                for g in range(2):
                    load_group(g, i)
            load_group(N_UP - 1)

            def load_down(kp, i=0):
                r = 2 * kp + 4 * i
                rows = slice(r, r + 2) if isinstance(r, int) else bass.ds(r, 2)
                for half in range(2):
                    load_chunk(sp, C_DN[j] + 2 * kp + half + 4 * i, (C_DN[j] + 2 * kp + half) % RAW,
                               down[:, rows, half * CN:half * CN + CN])

            with sp.Fori(0, N_UP // 2) as i:
                for kp in range(2):
                    load_down(kp, i)
            load_down(N_UP - 1)

        def pe_ffn(pe, j):
            mul_first(pe, C_UP[j], G_UP[j], (4 + 2 * j) * KT)
            group_read(pe, G_UP[j] - 1)
            total_squares(pe, sums, 7)
            if j == 0:
                total_squares(pe, sums2, 6)
                pe.wait_ge(s2_r, 1)
            pe.wait_ge(std_r, cnt_std[j])
            mul_groups(pe, C_UP[j] + 4, G_UP[j] + 1, N_UP - 1, hhi, hlo)
            group_read(pe, G_DN[j] - 2)

            def down(kp, i=0):
                pe.wait_ge(flo_r, N_UP * j + kp + 1 + 2 * i)
                for half in range(2):
                    if kp == 0 and half == 1:
                        group_read(pe, G_DN[j] - 1)
                    c0, g = C_DN[j] + 2 * kp + half, G_DN[j] + half
                    s = c0 % SPLIT
                    pe.wait_ge(w_lo, c0 + 1 + 4 * i)
                    for a in range(CK):
                        kt = 2 * kp + a + 4 * i
                        if isinstance(kt, int):
                            x_h, x_l = ahi[:, kt, :], alo[:, kt, :]
                        else:
                            x_h = ahi[:, bass.ds(kt, 1), :].rearrange("p o n -> p (o n)")
                            x_l = alo[:, bass.ds(kt, 1), :].rearrange("p o n -> p (o n)")
                        for m in range(4):
                            f = slice(m * P, m * P + P)
                            mm = mm3(pe, bank(g, m), whi[:, s, a, f], wlo[:, s, a, f], x_h, x_l,
                                     kp == 0 and a == 0, kp == N_UP - 1 and a == CK - 1)
                    mm.then_inc(w_used, 1)

            down(0)
            with pe.Fori(0, (N_UP - 3) // 2) as i:
                for kp in (1, 2):
                    down(kp, i)
            down(N_UP - 2)
            down(N_UP - 1)

        def act_ffn(act, j, tile_wait):
            def gate(g, i=0):
                act.wait_ge(fscaled_r, N_UP * j + g + 1 + 2 * i)
                act.activation(gated[:, g % 2, :, :], gated[:, g % 2, :, :], ACT.Silu).then_inc(fgate_r, 1)

            def group(g, i=0, step=0, ks=range(4)):
                for k in ks:
                    if k == 3 and g:
                        gate(g - 1, i)
                    split_hi(act, C_UP[j] + 4 * g, k, i, step, up=4 * N_UP * j + 4 * g + k)

            group(0, ks=(0, 1))
            gain = both_gains if j == 0 else gain_of("g_ffn2_2")
            if j == 0:
                act.wait_ge(gain_r, 1)
            gained_high(act, gain, tile_wait)
            squares(act, xT, lambda k: None)
            if j == 0:
                squares(act, xT, lambda k: None, gain=gain_of("norm_final_g"))
            group(0, ks=(2, 3))
            group(1, ks=(0, 1))
            root_of_total(act, root1 if j == 0 else stat_std[:, :], 7)
            if j == 0:
                cnt["root"] += 1
                act.wait_ge(tot_r, cnt["root"])
                act.activation(sq[:, 0, :], psum[:, 6, :], ACT.Copy).then_inc(s2_r, 1)
                act.wait_ge(var_r, 1)
                act.activation(stat_std[:, :], sq[:, 1, :], ACT.Sqrt, bias=eps_col, scale=1.0 / D).then_inc(std_r, 1)
            group(1, ks=(2, 3))
            group(2)
            with act.Fori(1, (N_UP - 1) // 2) as i:
                for g in (1, 2):
                    group(g, i, 8)
            for k in range(2):
                split_hi(act, C_DN[j], k)
            gate(N_UP - 1)
            with act.Fori(0, (N_UP - 1) // 2) as i:
                for k in range(4):
                    split_hi(act, C_DN[j] + 2, k, i, 4)

        def dve_ffn(dve, j):
            def scaled(g, i=0):
                dve.wait_ge(w_used, C_UP[j] + 4 * g + 4 + 8 * i)
                b = 4 * ((G_UP[j] + g) % 2)
                dve.tensor_tensor(gated[:, g % 2, :, :], psum[:, b:b + 2, :], over_root, ALU.mult).then_inc(fscaled_r, 1)

            def products(g, i=0):
                dve.wait_ge(fgate_r, N_UP * j + g + 1 + 2 * i)
                b = 4 * ((G_UP[j] + g) % 2) + 2
                dve.tensor_tensor(gated[:, g % 2, :, :], gated[:, g % 2, :, :], over_root, ALU.mult).then_inc(fprod_r, 1)
                dve.wait_ge(fprod_r, N_UP * j + g + 1 + 2 * i)
                dve.tensor_tensor(gated[:, g % 2, :, :], gated[:, g % 2, :, :], psum[:, b:b + 2, :],
                                  ALU.mult).then_inc(evac[g % 2], 1)

            def pair(g, i):
                kt = 2 * g + 4 * i
                return slice(kt, kt + 2) if isinstance(kt, int) else bass.ds(kt, 2)

            def products_hi(g, i=0):
                dve.wait_ge(evac[g % 2], (G_UP[j] + g) // 2 + 1 + i)
                dve.tensor_scalar(ahi[:, pair(g, i), :], gated[:, g % 2, :, :], 1.0, None, ALU.mult).then_inc(fhi_r, 1)

            def products_lo(g, i=0):
                dve.wait_ge(fhi_r, N_UP * j + g + 1 + 2 * i)
                dve.tensor_tensor(alo[:, pair(g, i), :], gated[:, g % 2, :, :], ahi[:, pair(g, i), :].bitcast(F32),
                                  ALU.subtract).then_inc(flo_r, 1)

            def group(g, i=0, step=0):
                for k in range(4):
                    split_lo(dve, C_UP[j] + 4 * g, k, i, step)
                    if k == 1:
                        if g == 1 and isinstance(i, int):
                            roots()
                        scaled(g - 1, i)
                    if k == 2:
                        products(g - 1, i)
                products_hi(g - 1, i)
                products_lo(g - 1, i)

            def roots():
                if j:
                    inverse(dve)
                    return
                cnt["inverse"] += 1
                dve.wait_ge(std_r, cnt["inverse"])
                dlink(dve, dve.reciprocal(root1, root1))
                dve.wait_ge(s2_r, 1)
                dlink(dve, dve.tensor_tensor(sq[:, 1, :], sq[:, 0, :], root1, ALU.mult))
                dve.tensor_tensor(sq[:, 1, :], sq[:, 1, :], root1, ALU.mult).then_inc(var_r, 1)
                for k in range(KT):
                    dve.scalar_tensor_tensor(out=xT[:, k, :], in0=xT[:, k, :], scalar=col("norm_final_g", k), in1=root1,
                                             op0=ALU.mult, op1=ALU.mult).then_inc(x_r, 1)
                inverse(dve)
                dlink(dve, dve.tensor_tensor(stat_std[:, :], stat_std[:, :], root1, ALU.mult))

            gain = both_gains if j == 0 else gain_of("g_ffn2_2")
            split_lo(dve, C_UP[j], 0)
            gained_low(dve, gain, range(4))
            split_lo(dve, C_UP[j], 1)
            gained_low(dve, gain, range(4, KT))
            for k in (2, 3):
                split_lo(dve, C_UP[j], k)
            for g in (1, 2):
                group(g)
            with dve.Fori(1, (N_UP - 1) // 2) as i:
                for g in (1, 2):
                    group(g, i, 8)
            split_lo(dve, C_DN[j], 0)
            split_lo(dve, C_DN[j], 1)
            scaled(N_UP - 1)
            products(N_UP - 1)
            products_hi(N_UP - 1)
            products_lo(N_UP - 1)
            with dve.Fori(0, (N_UP - 1) // 2) as i:
                for k in range(4):
                    split_lo(dve, C_DN[j] + 2, k, i, 4)
            if j == 0:
                dve.wait_ge(x_r, 4 * KT)
            for half in range(2):
                g = G_DN[j] + half
                dve.wait_ge(w_used, C_DN[j] + 2 * (N_UP - 1) + half + 1)
                for m in range(4):
                    k = 4 * half + m
                    ins = dve.scalar_tensor_tensor(out=xT[:, k, :], in0=bank(g, m), scalar=0.5, in1=xT[:, k, :],
                                                   op0=ALU.mult, op1=ALU.add)
                ins.then_inc(evac[g % 2], 1)

        mx = {n: sem("mix_" + n) for n in (
            "w_uq_in", "w_ukv_in", "k_zero", "rot", "rot_read", "cos", "rope", "kv_t", "kv_tok", "idx", "relu", "acc",
            "lat", "q", "q_raw", "q_rot", "q_rot_read", "q_cos", "q_rope", "k_nope", "k_nope_in", "k_pe", "v", "v_in",
            "best", "marked", "hi", "lo")}
        at_ = {n: sem("att_" + n) for n in ("score", "score_read", "max", "exp", "inverse", "p_pool", "p_act", "p_dve", "p_t", "p_t_in", "out")}
        kv_cols = [sem(f"mix_columns_in{k}") for k in range(4)]

        qa = tiles(ar3[:, 0:2048])
        mixb = tiles(ar3[:, 2048:6144])
        KA, KI, KV, CKV, CQ = 0, 1, 2, 3, 5
        kz = tiles(ar3[:, 6144:8192])
        w_uq = ar3[:, 8192:10496].rearrange("p (k n) -> p k n", k=3)
        w_ukv = ar3[:, 10496:12544].rearrange("p (k n) -> p k n", k=2)
        kB = tiles(ar3[:, 12544:16640])
        vB = tiles(ar3[:, 16640:18688])
        qi = tiles(ar3[:, 18688:22784])
        qB = qi
        sc_at = {1: 22784, 2: 23040, 3: 23424}
        sc = {b: ar3[:, o:o + P * (b + 1)] for b, o in sc_at.items()}
        pr = tiles(ar3[:, 23936:25472])
        p_buf = [pr[:, 0, :], pr[:, 1, :], pr[:, 2, :], mixb[:, KI, :]] + [mixb[:, CQ + k, :] for k in range(3)]
        pT_buf = [sq[:, 0, :], sq[:, 1, :], mixb[:, CKV, :], mixb[:, CKV + 1, :]]
        NP, NT = len(p_buf), len(pT_buf)
        neg_max, p_sum, p_inv = (stat_mean[:, o:o + NP] for o in (32, 48, 64))
        wi_tok = ar3[:, 25472:25536].rearrange("p (t h) -> p t h", h=HI)
        kv_tok = ar3[:, 2048:2560].rearrange("p (t f) -> p t f", f=P)
        best = stat_mean[:, 0:24].rearrange("p (b e) -> p b e", e=8)
        ropes = [(mixb[:, KI, :], "A", (2, 3)), (mixb[:, KA, :], "A", (0, 1)), (mixb[:, KV, :], "B", None)]
        ropes += [(qi[:, k, :], "A", None) for k in range(8)] + [(qa[:, k, :], "A", None) for k in range(4)]
        R_KI, R_KA, R_KV, R_QI, R_QA = 1, 2, 3, 3, 11
        rot_of = {"A": const[:, K_RA:K_RA + P], "B": const[:, K_RB:K_RB + P]}
        cos_of = {"A": const[:, K_CA:K_CA + T], "B": const[:, K_CBT:K_CBT + T]}
        sin_of = {"A": const[:, K_SA:K_SA + T], "B": const[:, K_SB:K_SB + T]}
        HQ = NOPE + ROPE
        pe_rows = slice(NOPE, HQ)
        idx_units = [(h, b) for h in range(HI) for b in (3, 2, 1)]
        units = [("B", 2 * q + j, b) for q in range(HB // 2) for b in range(TT) for j in range(2)]
        units += [("A", h, b) for b in range(TT) for h in range(HA)]
        NB = HB * TT
        ROUNDS = TOPK // 8
        EARLY, MID = 2, 8

        def sp_mix(sp):
            wv = A["w_in_2"].rearrange("o (k p) n -> p (o k) n", p=P)

            def cols(k, dst, src, n, s):
                slot = (C_MIX + k) % RAW
                sp.dma_start(raw[:, slot, :, dst:dst + n], wv[:, 2 * (k % 4):2 * (k % 4) + 2, src:src + n]).then_inc(s, 16)

            for g, c in enumerate((C_QA, C_QI, C_QI + CN)):
                for k in range(4):
                    load_chunk(sp, C_MIX + 4 * g + k, (C_MIX + k) % RAW, wv[:, 2 * k:2 * k + 2, c:c + CN])
            with nc.allow_non_contiguous_dma(reason="narrow columns"):
                for k in range(12, 16):
                    sp.wait_ge(w_lo, C_MIX + k - RAW + 1)
                    cols(k, 0, C_KA, 64, w_raw[(C_MIX + k) % RAW])
                    for dst, src, n in ((64, C_KA, 64), (128, C_KI, 64), (192, C_KI, 64), (256, C_VA, 64),
                                        (320, C_KR, ROPE), (352, C_WI, HI), (368, C_WI, HI), (384, C_CKV, P)):
                        cols(k, dst, src, n, kv_cols[k % 4])
            for k in range(16, 20):
                sp.wait_ge(w_lo, C_MIX + k - RAW + 1)
                cols(k, 0, C_CKV + P, P, w_raw[(C_MIX + k) % RAW])
                cols(k, P, C_CQ, QL, kv_cols[k % 4])
            sp.wait_ge(w_used, C_MIX)
            sp.dma_start(w_uq, A["w_uq_2"].rearrange("o (k p) n -> p (o k) n", p=P)).then_inc(mx["w_uq_in"], 16)
            sp.dma_start(w_ukv, A["w_ukv_2"].rearrange("o (k p) n -> p (o k) n", p=P)).then_inc(mx["w_ukv_in"], 16)
            wo = A["w_out_2"].rearrange("o (k p) n -> p (o k) n", p=P)
            for g in range(2):
                for k in range(4):
                    load_chunk(sp, C_MO + 4 * g + k, (C_MO + k) % RAW, wo[:, 2 * k:2 * k + 2, CN * g:CN * g + CN])

        def scores(pe, u):
            kind, h, b = units[u]
            S = P * (b + 1)
            if u == 0:
                pe.wait_ge(mx["v_in"], TT)
                pe.wait_ge(mx["q_rot_read"], HB)
                pe.wait_ge(mx["k_pe"], HB)
            if kind == "B" and b == 0:
                pe.wait_ge(mx["q_rope"], h + 1)
            if u >= 2:
                pe.wait_ge(at_["score_read"], u - 1)
            if kind == "B":
                lhs, rhs = qB[0:HQ, h, b * P:b * P + P], kB[0:HQ, h, 0:S]
            else:
                lhs, rhs = qa[:, h // 2, b * P:b * P + P], kz[:, h % 2, 0:S]
            pe.matmul(psum[:, u % 2, 0:S], lhs, rhs, start=True, stop=True).then_inc(at_["score"], 1)

        def p_done(u):
            if u % 2 == 0:
                return at_["p_pool"], u // 2 + 1
            return (at_["p_act"], u // 2 + 1) if u < NB else (at_["p_dve"], (u - NB) // 2 + 1)

        def turn_p(pe, u):
            b = units[u][2]
            s, n = p_done(u)
            pe.wait_ge(s, n)
            if u >= 2:
                pe.wait_ge(at_["p_t_in"], u - 1)
            for t in range(b + 1):
                mm = pe.transpose(psum[:, 2 + u % 2, t * P:t * P + P], p_buf[u % NP][:, t * P:t * P + P], ident)
            mm.then_inc(at_["p_t"], 1)

        def weigh(pe, u):
            kind, h, b = units[u]
            if u == NB:
                pe.wait_ge(mx["lo"], 1)
            pe.wait_ge(at_["p_t_in"], u + 2)
            for t in range(b + 1):
                for j in range(2):
                    o = j * 64
                    lhs = vB[:, t, (h + j) * VB:(h + j + 1) * VB] if kind == "B" else kv_tok[:, t, 0:HDA]
                    mm = pe.matmul(psum[o:o + 64, 4 + h // 2, b * P:b * P + P], lhs, pT_buf[(u + j) % NT][:, t * P:t * P + P],
                                   start=(t == 0), stop=(t == b))
            mm.then_inc(at_["out"], 2)

        def pe_mix(pe):
            mul_first(pe, C_MIX, G_MIX, 5 * KT)
            group_read(pe, G_MIX - 1)
            total_squares(pe, sums, 3)
            pe.wait_ge(std_r, STD_BEFORE + 3)
            mul_groups(pe, C_MIX + 4, G_MIX + 1, N_MIX - 1, hhi, hlo)
            for g in range(N_MIX):
                group_read(pe, G_MIX + g)
            for r, (src, kind, _) in enumerate(ropes):
                if r >= 4:
                    pe.wait_ge(mx["rot_read"], r - 3)
                pe.matmul(psum[:, r % 4, :], rot_of[kind], src, start=True, stop=True).then_inc(mx["rot"], 1)
            pe.wait_ge(mx["rope"], R_KV)
            for t in range(TT):
                mm = pe.transpose(psum[:, 4, t * P:t * P + P], mixb[:, KV, t * P:t * P + P], ident)
            mm.then_inc(mx["kv_t"], 1)
            sum_squares(pe, 5, 3)
            sum_squares(pe, 6, 2)
            pe.wait_ge(mx["rot_read"], len(ropes))
            pe.wait_ge(mx["k_zero"], 4)
            for v_, (h, b) in enumerate(idx_units):
                S = P * (b + 1)
                if b == 3 and h % 2 == 0:
                    pe.wait_ge(mx["rope"], R_QI + h // 2 + 1)
                if v_ >= 4:
                    pe.wait_ge(mx["relu"], v_ - 3)
                pe.matmul(psum[:, v_ % 4, 0:S], qi[:, h // 2, b * P:b * P + P], kz[:, 2 + h % 2, 0:S], start=True,
                          stop=True).then_inc(mx["idx"], 1)
            pe.wait_ge(mx["w_uq_in"], 16)
            pe.wait_ge(mx["lat"], 3)
            pe.wait_ge(mx["kv_tok"], 2)

            def rotate(h):
                pe.wait_ge(mx["q_raw"], h + 1)
                if h >= 2:
                    pe.wait_ge(mx["q_rot_read"], h - 1)
                pe.matmul(psum[0:HQ, 6 + h % 2, :], const[0:HQ, K_RB:K_RB + HQ], qB[0:HQ, h, :], start=True,
                          stop=True).then_inc(mx["q_rot"], 1)

            for h in range(HB):
                if h >= 2:
                    pe.wait_ge(mx["q_raw"], h - 1)
                for k in range(3):
                    mm = pe.matmul(psum[0:HQ, 4 + h % 2, :], w_uq[:, k, h * HQ:h * HQ + HQ], mixb[:, CQ + k, :],
                                   start=(k == 0), stop=(k == 2))
                mm.then_inc(mx["q"], 1)
                if h:
                    rotate(h - 1)
            rotate(HB - 1)
            pe.wait_ge(mx["w_ukv_in"], 16)
            pe.wait_ge(mx["lat"], 5)
            pe.wait_ge(mx["relu"], len(idx_units))
            for h in range(HB):
                if h >= 4:
                    pe.wait_ge(mx["k_nope_in"], h - 3)
                for k in range(2):
                    mm = pe.matmul(psum[0:NOPE, h % 4, :], w_ukv[:, k, h * P:h * P + NOPE], mixb[:, CKV + k, :],
                                   start=(k == 0), stop=(k == 1))
                mm.then_inc(mx["k_nope"], 1)
            for t in range(TT):
                pe.wait_ge(mx["k_nope_in"], 5 + t)
                for k in range(2):
                    wv = w_ukv[:, k, :].rearrange("p (h f) -> p h f", f=P)[:, :, NOPE:P]
                    mm = pe.matmul(psum[:, t, :].rearrange("p (h f) -> p h f", f=VB), mixb[:, CKV + k, t * P:t * P + P],
                                   wv, start=(k == 0), stop=(k == 1))
                mm.then_inc(mx["v"], 1)
            for u in range(len(units) + 6):
                if u < len(units):
                    scores(pe, u)
                if 5 <= u < len(units) + 5:
                    turn_p(pe, u - 5)
                if u >= 7 and u % 2 == 1:
                    weigh(pe, u - 7)
            pe.wait_ge(mx["lo"], 2)
            mul_groups(pe, C_MO, G_MO, 2, hhi, hlo)

        def act_mix(act):
            for k in range(SPLIT):
                split_hi(act, C_MIX, k)
            gained_high(act, gain_of("g_mix_2"), lambda k: group_read(act, G_DN[0] + k // 4))
            squares(act, xT, lambda k: None)
            for k in range(SPLIT, 6):
                split_hi(act, C_MIX, k)
            root_of_total(act, stat_std[:, :], 3)
            for k in range(6, 20):
                if k >= 12:
                    act.wait_ge(kv_cols[k % 4], 16 * 8 if k < 16 else 16 * 9)
                split_hi(act, C_MIX, k)
            for k in range(SPLIT):
                split_hi(act, C_MO, k)
            group_read(act, G_MIX + N_MIX - 1)
            squares(act, mixb[:, CQ:CQ + 3, :], lambda k: None, 3)
            root(act, 5, QL)
            act.wait_ge(mx["kv_t"], 1)
            act.wait_ge(mx["rope"], R_KA)
            kv_ps = psum[:, 4, :].rearrange("p (t f) -> p t f", f=P)
            act.activation(kv_tok, kv_ps, ACT.Copy).then_inc(mx["kv_tok"], 1)
            act.activation(wi_tok, kv_ps[:, :, HQ:HQ + HI], ACT.Copy, scale=float(HI * 64) ** -0.5).then_inc(
                mx["kv_tok"], 1)
            squares(act, mixb[:, CKV:CKV + 2, :], lambda k: None, 2)
            act.wait_ge(mx["lat"], 3)
            root(act, 6, KVL)
            act.wait_ge(mx["rope"], len(ropes))
            for v_, (h, b) in enumerate(idx_units):
                act.wait_ge(mx["idx"], v_ + 1)
                if v_ >= 3:
                    act.wait_ge(mx["acc"], v_ - 2)
                S = P * (b + 1)
                act.activation(pr[:, v_ % 3, 0:S], psum[:, v_ % 4, 0:S], ACT.Relu).then_inc(mx["relu"], 1)
            for h in range(HB):
                act.wait_ge(mx["q"], h + 1)
                act.activation(qB[0:HQ, h, :], psum[0:HQ, 4 + h % 2, :], ACT.Copy).then_inc(mx["q_raw"], 1)
            for h in range(HB):
                act.wait_ge(mx["k_nope"], h + 1)
                act.activation(kB[0:NOPE, h, :], psum[0:NOPE, h % 4, :], ACT.Copy).then_inc(mx["k_nope_in"], 1)
            for t in range(TT):
                act.wait_ge(mx["v"], t + 1)
                act.activation(vB[:, t, :], psum[:, t, :], ACT.Copy).then_inc(mx["v_in"], 1)

            def exp(u):
                b = units[u][2]
                act.wait_ge(at_["max"], u + 1)
                act.activation(p_buf[u % NP][:, 0:P * (b + 1)], p_buf[u % NP][:, 0:P * (b + 1)], ACT.Exp,
                               bias=neg_max[:, u % NP:u % NP + 1], accum_out=p_sum[:, u % NP:u % NP + 1]).then_inc(
                    at_["exp"], 1)

            def divide(u):
                act.wait_ge(at_["inverse"], u + 1)
                part = p_buf[u % NP][:, 0:P * (units[u][2] + 1)]
                act.activation(part, part, ACT.Identity, scale=p_inv[:, u % NP:u % NP + 1]).then_inc(at_["p_act"], 1)

            def p_t(u):
                b = units[u][2]
                act.wait_ge(at_["p_t"], u + 1)
                if u >= NT:
                    act.wait_ge(at_["out"], u - NT + 1)
                act.activation(pT_buf[u % NT][:, 0:P * (b + 1)], psum[:, 2 + u % 2, 0:P * (b + 1)], ACT.Copy).then_inc(
                    at_["p_t_in"], 1)

            def high(n, k):
                act.wait_ge(at_["out"], n)
                act.activation(hhi_[:, k * T:(k + 4) * T], psum[:, 4:8, :].rearrange("p b n -> p (b n)"),
                               ACT.Copy).then_inc(mx["hi"], 1)

            for u in range(len(units) + 5):
                if u >= 5:
                    p_t(u - 5)
                if 1 <= u < len(units) + 1:
                    exp(u - 1)
                if u % 2 == 0 and 4 <= u < NB + 4:
                    divide(u - 3)
                if u == NB + 5:
                    high(NB, 4)
            high(len(units), 0)
            for k in range(SPLIT, 8):
                split_hi(act, C_MO, k)

        def dve_mix(dve):
            dsts = [ar3[:, 0:2048], ar3[:, 18688:20736], ar3[:, 20736:22784], ar3[:, 2048:4096], ar3[:, 4096:6144]]

            def read_group(g):
                dve.wait_ge(w_used, C_MIX + 4 * g + 4)
                b = 4 * ((G_MIX + g) % 2)
                dve.tensor_tensor(tiles(dsts[g]), psum[:, b:b + 4, :],
                                  stat_std[:, :].unsqueeze(1).to_broadcast([P, 4, T]), ALU.mult).then_inc(
                    evac[(G_MIX + g) % 2], 1)

            split_lo(dve, C_MIX, 0)
            gained_low(dve, gain_of("g_mix_2"), range(4))
            split_lo(dve, C_MIX, 1)
            gained_low(dve, gain_of("g_mix_2"), range(4, KT))
            for k in range(2, 6):
                split_lo(dve, C_MIX, k)
            inverse(dve)
            for g in range(1, N_MIX):
                read_group(g - 1)
                for k in range(4 * g + 2, min(4 * g + 6, 20)):
                    split_lo(dve, C_MIX, k)
            read_group(N_MIX - 1)
            for g in range(N_MIX):
                group_read(dve, G_MIX + g)

            def sine(r):
                kind = ropes[r][1]
                dve.wait_ge(mx["rot"], r + 1)
                if r >= 3:
                    dve.wait_ge(mx["rope"], r - 2)
                dve.tensor_tensor(pr[:, r % 3, :], psum[:, r % 4, :], sin_of[kind], ALU.mult).then_inc(mx["rot_read"], 1)

            def rotated(r):
                src, kind, halves = ropes[r]
                dve.wait_ge(mx["rot_read"], r + 1)
                dve.wait_ge(mx["cos"], r + 1)
                if halves is None:
                    dve.tensor_tensor(src, src, pr[:, r % 3, :], ALU.add).then_inc(mx["rope"], 1)
                else:
                    dve.tensor_tensor(kz[0:64, halves[0], :], src[0:64], pr[0:64, r % 3, :], ALU.add)
                    dve.tensor_tensor(kz[64:P, halves[1], :], src[64:P], pr[64:P, r % 3, :], ALU.add).then_inc(
                        mx["rope"], 1)

            for r in range(len(ropes) + 1):
                if r < len(ropes):
                    sine(r)
                if r:
                    rotated(r - 1)
            for k in range(SPLIT):
                split_lo(dve, C_MO, k)
            inverse(dve)
            for k in range(3):
                dve.scalar_tensor_tensor(out=mixb[:, CQ + k, :], in0=mixb[:, CQ + k, :], scalar=col("g_q_lat_2", k),
                                         in1=stat_std[:, :], op0=ALU.mult, op1=ALU.mult).then_inc(mx["lat"], 1)
            inverse(dve)
            for k in range(2):
                dve.scalar_tensor_tensor(out=mixb[:, CKV + k, :], in0=mixb[:, CKV + k, :], scalar=col("g_kv_lat_2", k),
                                         in1=stat_std[:, :], op0=ALU.mult, op1=ALU.mult).then_inc(mx["lat"], 1)
            dve.wait_ge(mx["kv_tok"], 2)
            for v_, (h, b) in enumerate(idx_units):
                dve.wait_ge(mx["relu"], v_ + 1)
                part, w = pr[:, v_ % 3, 0:P * (b + 1)], wi_tok[:, b, h:h + 1]
                if h == 0:
                    dve.tensor_scalar(sc[b], part, w, None, ALU.mult).then_inc(mx["acc"], 1)
                else:
                    dve.wait_ge(mx["acc"], v_ - 2)
                    dve.scalar_tensor_tensor(out=sc[b], in0=part, scalar=w, in1=sc[b], op0=ALU.mult,
                                             op1=ALU.add).then_inc(mx["acc"], 1)
            triangle = const[:, K_CB + 384:K_CB + 512]
            dve.wait_ge(mx["acc"], len(idx_units))
            for b in (1, 2, 3):
                dlink(dve, dve.tensor_tensor(sc[b][:, b * P:b * P + P], sc[b][:, b * P:b * P + P], triangle, ALU.add))

            def choose(r):
                for b in (1, 2, 3):
                    dve.max(best[:, b - 1, :], sc[b]).then_inc(mx["best"], 1)
                for b in (1, 2, 3):
                    dve.wait_ge(mx["best"], 3 * r + b)
                    dve.match_replace(sc[b], best[:, b - 1, :], sc[b], MARK).then_inc(mx["marked"], 1)
                dve.wait_ge(mx["marked"], 3 * r + 3)
                if r == ROUNDS - 1:
                    for b in (1, 2, 3):
                        dlink(dve, dve.tensor_scalar(sc[b], sc[b], MARK, NEG, ALU.not_equal, ALU.mult))

            done = 0

            def choose_to(n):
                nonlocal done
                while done < n:
                    choose(done)
                    done += 1

            choose_to(EARLY)
            for h in range(HB):
                dve.wait_ge(mx["q_rot"], h + 1)
                if h >= 3:
                    dve.wait_ge(mx["q_rope"], h - 2)
                dve.tensor_tensor(pr[pe_rows, h % 3, :], psum[pe_rows, 6 + h % 2, :], sin_of["B"][pe_rows],
                                  ALU.mult).then_inc(mx["q_rot_read"], 1)
                dve.wait_ge(mx["q_rot_read"], h + 1)
                dve.wait_ge(mx["q_cos"], h + 1)
                dve.tensor_tensor(qB[pe_rows, h, :], qB[pe_rows, h, :], pr[pe_rows, h % 3, :], ALU.add).then_inc(
                    mx["q_rope"], 1)
                choose_to(EARLY + (h + 1) * MID // HB)
            dve.wait_ge(mx["q_rope"], HB)

            def softmax_in(u):
                kind, h, b = units[u]
                S = P * (b + 1)
                if kind == "B":
                    bias, scale = const[:, K_CB + 384 - P * b:K_CB + 512], float(HQ) ** -0.5
                else:
                    bias, scale = triangle if b == 0 else sc[b], float(HDA) ** -0.5
                dve.wait_ge(at_["score"], u + 1)
                if u >= NP:
                    dve.wait_ge(at_["p_t"], u - NP + 1)
                dve.scalar_tensor_tensor(out=p_buf[u % NP][:, 0:S], in0=psum[:, u % 2, 0:S], scalar=scale, in1=bias,
                                         op0=ALU.mult, op1=ALU.add).then_inc(at_["score_read"], 1)

            def maximum(u):
                S = P * (units[u][2] + 1)
                dve.wait_ge(at_["score_read"], u + 1)
                dve.tensor_reduce(neg_max[:, u % NP:u % NP + 1], p_buf[u % NP][:, 0:S], AX.X, ALU.max,
                                  negate=True).then_inc(at_["max"], 1)

            def low(k, n):
                dve.wait_ge(mx["hi"], n)
                part = slice(k * T, (k + 4) * T)
                dve.tensor_tensor(hlo_[:, part], psum[:, 4:8, :].rearrange("p b n -> p (b n)"), hhi_[:, part].bitcast(F32),
                                  ALU.subtract).then_inc(mx["lo"], 1)

            def invert(u):
                dve.wait_ge(at_["exp"], u + 1)
                dve.reciprocal(p_inv[:, u % NP:u % NP + 1], p_sum[:, u % NP:u % NP + 1]).then_inc(at_["inverse"], 1)

            def divide(u):
                dve.wait_ge(at_["inverse"], u + 1)
                part = p_buf[u % NP][:, 0:P * (units[u][2] + 1)]
                dve.tensor_scalar(part, part, p_inv[:, u % NP:u % NP + 1], None, ALU.mult).then_inc(at_["p_dve"], 1)

            choose_to(ROUNDS)
            for u in range(len(units) + 3):
                if 1 <= u < len(units) + 1:
                    maximum(u - 1)
                if u < len(units):
                    softmax_in(u)
                if 2 <= u < len(units) + 2:
                    invert(u - 2)
                if u % 2 == 0 and u >= NB + 4:
                    divide(u - 3)
                if u == NB + 5:
                    low(4, 1)
            low(0, 2)
            for g in (G_MO, G_MO + 1):
                for k in range(2, 6) if g == G_MO else range(6, 8):
                    split_lo(dve, C_MO, k)
                dve.wait_ge(w_used, C_MO + 4 * (g - G_MO) + 4)
                for m in range(4):
                    k = 4 * (g - G_MO) + m
                    ins = dve.tensor_tensor(xT[:, k, :], bank(g, m), xT[:, k, :], ALU.add)
                ins.then_inc(evac[g % 2], 1)

        def pool_mix(pool):
            pool.wait_ge(tables_in, 16)
            pool.wait_ge(sq_u, SQ_BEFORE + 3 * KT)
            pool.wait_ge(w_used, C_MIX)
            for n in range(4):
                if n:
                    pool.wait_ge(mx["k_zero"], n)
                pool.memset(kz[64:P, n, :] if n % 2 == 0 else kz[0:64, n, :], 0.0).then_inc(mx["k_zero"], 1)
            pool.wait_ge(mx["k_zero"], 4)
            for r, (src, kind, _) in enumerate(ropes):
                pool.wait_ge(mx["rot"], r + 1)
                pool.tensor_tensor(src, src, cos_of[kind], ALU.mult).then_inc(mx["cos"], 1)
            pool.wait_ge(mx["rope"], R_KV)
            pool.wait_ge(mx["cos"], len(ropes))
            for h in range(HB):
                pool.tensor_copy(kB[pe_rows, h, :], mixb[pe_rows, KV, :]).then_inc(mx["k_pe"], 1)
            for h in range(HB):
                pool.wait_ge(mx["q_rot"], h + 1)
                pool.tensor_tensor(qB[pe_rows, h, :], qB[pe_rows, h, :], cos_of["B"][pe_rows], ALU.mult).then_inc(
                    mx["q_cos"], 1)
            pool.wait_ge(mx["q_cos"], HB)
            for u in range(0, len(units), 2):
                b = units[u][2]
                pool.wait_ge(at_["inverse"], u + 1)
                p_u = p_buf[u % NP][:, 0:P * (b + 1)]
                pool.tensor_scalar(p_u, p_u, p_inv[:, u % NP:u % NP + 1], None, ALU.mult).then_inc(at_["p_pool"], 1)

        o_r = sem("out_transposed")
        o_in = sem("out_on_tokens")
        stored = sem("out_stored")
        o_tok = ar3[:, 0:4096].rearrange("p (t d) -> p t d", d=D)

        def sp_last(sp):
            sp_ffn(sp, 1)
            for t in range(TT):
                sp.wait_ge(o_in, t + 1)
                sp.dma_start(out[0, t * P:t * P + P, :], o_tok[:, t, :]).then_inc(stored, 16)
            sp.wait_ge(stored, 16 * TT)

        def pe_last(pe):
            pe_ffn(pe, 1)
            sum_squares(pe, 7)
            for t in range(TT):
                for k in range(KT):
                    pe.wait_ge(h_r, 2 * KT + k + 1)
                    if t == 3:
                        pe.wait_ge(o_in, 1)
                    mm = pe.transpose(psum[:, 2 * (t % 3) + k // 4, (k % 4) * P:(k % 4 + 1) * P],
                                      xT[:, k, t * P:t * P + P], ident)
                mm.then_inc(o_r, 1)

        def act_last(act):
            act_ffn(act, 1, lambda k: group_read(act, G_MO + k // 4))
            squares(act, xT, lambda k: group_read(act, G_DN[1] + k // 4))
            root(act, 7)
            for t in range(TT):
                act.wait_ge(o_r, t + 1)
                act.activation(o_tok[:, t, :], psum[:, 2 * (t % 3):2 * (t % 3) + 2, :].rearrange("p b n -> p (b n)"),
                               ACT.Copy).then_inc(o_in, 1)

        def dve_last(dve):
            dve_ffn(dve, 1)
            inverse(dve)
            scale_rows(dve, xT, xT, "g_final_2", h_r)

        block = ctx.enter_context(nc.Block())

        @block.sync
        def _(sp):
            sp_router(sp)
            sp_block1(sp)
            sp_moe(sp)
            sp_ffn(sp, 0)
            sp_mix(sp)
            sp_last(sp)

        @block.gpsimd
        def _(pool):
            pool_block1(pool)
            pool_moe(pool)
            add_squares(pool, SQ_BEFORE, sums)
            add_squares(pool, SQ_BEFORE + KT, sums2)
            add_squares(pool, SQ_BEFORE + 2 * KT, sums)
            pool_mix(pool)
            add_squares(pool, SQ_BEFORE + 3 * KT + 5, sums)

        @block.tensor
        def _(pe):
            pe_block1(pe)
            pe_moe(pe)
            pe_ffn(pe, 0)
            pe_mix(pe)
            pe_last(pe)

        @block.scalar
        def _(act):
            act_block1(act)
            act_moe(act)
            act_ffn(act, 0, lambda k: act.wait_ge(x_r, 2 * KT + k + 1))
            act_mix(act)
            act_last(act)

        @block.vector
        def _(dve):
            dve_block1(dve)
            dve_moe(dve)
            dve_ffn(dve, 0)
            dve_mix(dve)
            dve_last(dve)


_INS = [
    "x", "norm_mix_g", "w_in", "b_in", "conv_w", "conv_b", "conv_ln_g", "conv_ln_b", "w_conv_out", "b_conv_out",
    "sg_ln_g", "sg_ln_b", "w_sg", "b_sg", "w_sg_out", "b_sg_out", "w_out", "b_out", "norm_ffn_g", "w_router_group",
    "b_router_group", "w_router_expert", "b_router_expert", "w_expert_gate", "w_expert_up", "w_expert_down",
    "norm_final_g", "g_ffn1_2", "w1_gate_2", "w1_up_2", "w1_down_2", "g_mix_2", "w_in_2", "g_q_lat_2",
    "g_kv_lat_2", "w_uq_2", "w_ukv_2", "w_out_2", "g_ffn2_2", "w2_gate_2", "w2_up_2", "w2_down_2", "g_final_2",
]
_OUTS = [((1, T, D), "float32")]


def kernel(**inputs):
    import concourse.bacc as _bacc
    from concourse.bass_utils import run_bass_kernel_spmd as _run

    nc = _bacc.Bacc("TRN2", target_bir_lowering=False, num_devices=1)
    arrays, args = {}, {}
    for name, a in [(n, inputs[n]) for n in _INS] + [("consts", constants())]:
        a = np.ascontiguousarray(a)
        arrays[f"in_{name}_dram"] = a
        args[name] = nc.dram_tensor(f"in_{name}_dram", a.shape, mybir.dt.from_np(a.dtype), kind="ExternalInput").ap()
    (shape, dtype), = _OUTS
    out = nc.dram_tensor("out_0_dram", shape, mybir.dt.from_np(np.dtype(dtype)), kind="ExternalOutput").ap()
    program(nc, args, out)
    r = _run(nc, [arrays], core_ids=[0])
    return r.results[0]["out_0_dram"]
```
